# Optimizing a Trainium2 kernel written in Bass

```python
import jax, jax.numpy as jnp
from jax import lax
import numpy as np
import math

D_MODEL = 1024
BATCH = 1
SEQ = 256
DEPTH = 2

BLOCK = 128
A_HEADS = 8
A_HEAD_DIM = 64
A_WIDTH = A_HEADS * A_HEAD_DIM
DILATED = ((128, 1), (512, 4), (2048, 16))
B_WIDTH = D_MODEL - A_WIDTH
SCONV_WIDTH = 3
IN_SPLITS = (A_WIDTH, A_WIDTH, A_WIDTH, B_WIDTH, B_WIDTH, B_WIDTH)
IN_WIDTH = sum(IN_SPLITS)
RET_HEADS = 4
RET_KDIM = D_MODEL // RET_HEADS
RET_VDIM = 2 * D_MODEL // RET_HEADS
RET_CHUNK = 128
ROPE_BASE = 10000.0
D_FF = 2816
FFN_CONV_WIDTH = 3
EPS = 1e-6
N_EVEN = (DEPTH + 1) // 2
N_ODD = DEPTH // 2


def rms_norm(x, g):
    xf = x.astype(jnp.float32)
    y = xf * lax.rsqrt(jnp.mean(xf * xf, axis=-1, keepdims=True) + EPS)
    return (y * g.astype(jnp.float32)).astype(x.dtype)

def causal_dwconv(x, w):
    K = w.shape[0]
    S = x.shape[1]
    xp = jnp.pad(x, ((0, 0), (K - 1, 0), (0, 0)))
    y = xp[:, 0:S] * w[0]
    for j in range(1, K):
        y = y + xp[:, j:j + S] * w[j]
    return y

def banded_causal_attention(q, k, v, reach):
    L, hd = q.shape[-2], q.shape[-1]
    lead = q.shape[:-2]
    nb = -(-L // BLOCK)
    pad_end = nb * BLOCK - L
    zp = [(0, 0)] * len(lead)
    qb = jnp.pad(q, zp + [(0, pad_end), (0, 0)]).reshape(*lead, nb, BLOCK, hd)
    kp = jnp.pad(k, zp + [(BLOCK, pad_end), (0, 0)]).reshape(*lead, nb + 1, BLOCK, hd)
    vp = jnp.pad(v, zp + [(BLOCK, pad_end), (0, 0)]).reshape(*lead, nb + 1, BLOCK, hd)
    kb = jnp.concatenate([kp[..., :-1, :, :], kp[..., 1:, :, :]], axis=-2)
    vb = jnp.concatenate([vp[..., :-1, :, :], vp[..., 1:, :, :]], axis=-2)
    s = jnp.einsum('...nqd,...nkd->...nqk', qb.astype(jnp.float32), kb.astype(jnp.float32)) * (hd ** -0.5)
    blk = jnp.arange(nb)[:, None, None]
    qi = jnp.arange(BLOCK)[None, :, None]
    kj = jnp.arange(2 * BLOCK)[None, None, :]
    rel = BLOCK + qi - kj
    kpos = blk * BLOCK - BLOCK + kj
    mask = (rel >= 0) & (rel <= reach) & (kpos >= 0)
    s = jnp.where(mask, s, -jnp.inf)
    m = jnp.max(s, axis=-1, keepdims=True)
    p = jnp.exp(s - m)
    den = jnp.sum(p, axis=-1, keepdims=True)
    o = jnp.einsum('...nqk,...nkd->...nqd', p, vb.astype(jnp.float32)) / den
    lse = (m + jnp.log(den))[..., 0]
    o = o.reshape(*lead, nb * BLOCK, hd)[..., :L, :]
    lse = lse.reshape(*lead, nb * BLOCK)[..., :L]
    return o, lse

def dilated_attention(q, k, v):
    Bn, H, S, hd = q.shape
    outs, lses = [], []
    for window, dil in DILATED:
        L = S // dil
        split = lambda t: t.reshape(Bn, H, L, dil, hd).swapaxes(2, 3)
        o, lse = banded_causal_attention(split(q), split(k), split(v), window // dil)
        outs.append(o.swapaxes(2, 3).reshape(Bn, H, S, hd))
        lses.append(lse.swapaxes(2, 3).reshape(Bn, H, S))
    wts = jax.nn.softmax(jnp.stack(lses), axis=0)
    return jnp.sum(wts[..., None] * jnp.stack(outs), axis=0)

def even_mixer(xn, w_in, q_gain, k_gain, sconv_w, w_out):
    Bn, S, _ = xn.shape
    proj = xn @ w_in
    q, k, v, gate_b, gate_c, h = jnp.split(proj, np.cumsum(IN_SPLITS)[:-1].tolist(), axis=-1)
    heads = lambda t: t.reshape(Bn, S, A_HEADS, A_HEAD_DIM)
    q = rms_norm(heads(q), q_gain).transpose(0, 2, 1, 3)
    k = rms_norm(heads(k), k_gain).transpose(0, 2, 1, 3)
    v = heads(v).transpose(0, 2, 1, 3)
    a = dilated_attention(q, k, v).astype(xn.dtype).transpose(0, 2, 1, 3).reshape(Bn, S, A_WIDTH)
    b = gate_b * causal_dwconv(gate_c * h, sconv_w)
    return jnp.concatenate([a, b], axis=-1) @ w_out

def rotary(x, pos):
    half = x.shape[-1] // 2
    inv = ROPE_BASE ** (-jnp.arange(half, dtype=jnp.float32) / half)
    ang = pos[:, None] * inv[None, :]
    cos = jnp.cos(ang)[None, :, None, :]
    sin = jnp.sin(ang)[None, :, None, :]
    x1, x2 = x[..., :half], x[..., half:]
    return jnp.concatenate([x1 * cos - x2 * sin, x1 * sin + x2 * cos], axis=-1)

def chunkwise_retention(q, k, v):
    Bn, S, H, dk = q.shape
    dv = v.shape[-1]
    nc = S // RET_CHUNK
    log_g = jnp.log1p(-(2.0 ** (-5.0 - jnp.arange(H, dtype=jnp.float32))))
    i = jnp.arange(RET_CHUNK, dtype=jnp.float32)
    diff = i[:, None] - i[None, :]
    inner_decay = jnp.where(diff >= 0, jnp.exp(log_g[:, None, None] * jnp.maximum(diff, 0.0)), 0.0)
    q_decay = jnp.exp(log_g[:, None] * (i + 1.0))
    k_decay = jnp.exp(log_g[:, None] * (RET_CHUNK - 1.0 - i))
    chunk_decay = jnp.exp(log_g * RET_CHUNK)
    to_chunks = lambda t: t.reshape(Bn, nc, RET_CHUNK, H, t.shape[-1]).transpose(1, 0, 3, 2, 4)

    def step(state, qkv):
        qc, kc, vc = qkv
        scores = jnp.einsum('bhqd,bhkd->bhqk', qc, kc) * inner_decay
        o = (jnp.einsum('bhqk,bhke->bhqe', scores, vc)
             + jnp.einsum('bhqd,bhde->bhqe', qc, state) * q_decay[..., None])
        state = (state * chunk_decay[:, None, None]
                 + jnp.einsum('bhkd,bhke->bhde', kc * k_decay[..., None], vc))
        return state, o

    state0 = jnp.zeros((Bn, H, dk, dv), jnp.float32)
    _, o = lax.scan(step, state0, (to_chunks(q), to_chunks(k), to_chunks(v)))
    return o.transpose(1, 0, 3, 2, 4).reshape(Bn, S, H, dv)

def retention_mixer(xn, wq, wk, wv, wg, gn_gain, wo):
    Bn, S, _ = xn.shape
    pos = jnp.arange(S, dtype=jnp.float32)
    q = (xn @ wq).reshape(Bn, S, RET_HEADS, RET_KDIM).astype(jnp.float32)
    k = (xn @ wk).reshape(Bn, S, RET_HEADS, RET_KDIM).astype(jnp.float32) * (RET_KDIM ** -0.5)
    v = (xn @ wv).reshape(Bn, S, RET_HEADS, RET_VDIM).astype(jnp.float32)
    o = chunkwise_retention(rotary(q, pos), rotary(k, pos), v)
    mu = jnp.mean(o, axis=-1, keepdims=True)
    var = jnp.mean(jnp.square(o - mu), axis=-1, keepdims=True)
    o = (o - mu) * lax.rsqrt(var + EPS) * gn_gain.astype(jnp.float32)
    o = o.reshape(Bn, S, RET_HEADS * RET_VDIM).astype(xn.dtype)
    return (jax.nn.silu(xn @ wg) * o) @ wo

def conv_glu_ffn(xn, w_up, conv_w, w_down):
    u = causal_dwconv(xn @ w_up, conv_w)
    g, val = jnp.split(u, 2, axis=-1)
    return (jax.nn.silu(g) * val) @ w_down

def first_inputs(seed: int = 0) -> dict:
    key = jax.random.key(seed)
    ks = jax.random.split(key, 24)
    nrm = lambda k, shape, s: jax.random.normal(k, shape, jnp.float32) * s
    gain = lambda k, shape: 1.0 + 0.02 * jax.random.normal(k, shape, jnp.float32)
    D = D_MODEL
    return {
        "x": jax.random.normal(ks[0], (BATCH, SEQ, D), jnp.float32),
        "even_norm": gain(ks[1], (N_EVEN, D)),
        "even_w_in": nrm(ks[2], (N_EVEN, D, IN_WIDTH), D ** -0.5),
        "even_q_gain": gain(ks[3], (N_EVEN, A_HEAD_DIM)),
        "even_k_gain": gain(ks[4], (N_EVEN, A_HEAD_DIM)),
        "even_sconv_w": nrm(ks[5], (N_EVEN, SCONV_WIDTH, B_WIDTH), SCONV_WIDTH ** -0.5),
        "even_w_out": nrm(ks[6], (N_EVEN, A_WIDTH + B_WIDTH, D), (A_WIDTH + B_WIDTH) ** -0.5),
        "odd_norm": gain(ks[7], (N_ODD, D)),
        "ret_wq": nrm(ks[8], (N_ODD, D, RET_HEADS * RET_KDIM), D ** -0.5),
        "ret_wk": nrm(ks[9], (N_ODD, D, RET_HEADS * RET_KDIM), D ** -0.5),
        "ret_wv": nrm(ks[10], (N_ODD, D, RET_HEADS * RET_VDIM), D ** -0.5),
        "ret_wg": nrm(ks[11], (N_ODD, D, RET_HEADS * RET_VDIM), D ** -0.5),
        "ret_gn_gain": gain(ks[12], (N_ODD, RET_HEADS, RET_VDIM)),
        "ret_wo": nrm(ks[13], (N_ODD, RET_HEADS * RET_VDIM, D), (RET_HEADS * RET_VDIM) ** -0.5),
        "ffn_norm": gain(ks[14], (DEPTH, D)),
        "ffn_w_up": nrm(ks[15], (DEPTH, D, 2 * D_FF), D ** -0.5),
        "ffn_conv_w": nrm(ks[16], (DEPTH, FFN_CONV_WIDTH, 2 * D_FF), FFN_CONV_WIDTH ** -0.5),
        "ffn_w_down": nrm(ks[17], (DEPTH, D_FF, D), D_FF ** -0.5),
    }

def first_block(x, even_norm, even_w_in, even_q_gain, even_k_gain, even_sconv_w, even_w_out,
              odd_norm, ret_wq, ret_wk, ret_wv, ret_wg, ret_gn_gain, ret_wo,
              ffn_norm, ffn_w_up, ffn_conv_w, ffn_w_down):
    for l in range(DEPTH):
        if l % 2 == 0:
            e = l // 2
            x = x + even_mixer(rms_norm(x, even_norm[e]), even_w_in[e], even_q_gain[e],
                               even_k_gain[e], even_sconv_w[e], even_w_out[e])
        else:
            o = l // 2
            x = x + retention_mixer(rms_norm(x, odd_norm[o]), ret_wq[o], ret_wk[o], ret_wv[o],
                                    ret_wg[o], ret_gn_gain[o], ret_wo[o])
        x = x + conv_glu_ffn(rms_norm(x, ffn_norm[l]), ffn_w_up[l], ffn_conv_w[l], ffn_w_down[l])
    return x


CHUNK = 64
N_A = DEPTH // 2
N_B = DEPTH - N_A

POOL_WINDOWS = (2, 4, 8, 16)
N_POOL = len(POOL_WINDOWS)
POOL_GD = D_MODEL // N_POOL

N_HEADS = 8
QK_NOPE = 128
QK_ROPE = 64
V_DIM = 128
Q_RANK = 384
KV_RANK = 256
ROPE_THETA = 10000.0
ATTN_SCALE = 1.0 / math.sqrt(QK_NOPE + QK_ROPE)
Q_BLOCK = 128

N_GROUPS = 4
EXPERTS_PER_GROUP = 8
N_EXPERTS = N_GROUPS * EXPERTS_PER_GROUP
TOP_K = 2
D_EXPERT = 512
ROW_BLOCK = 256


def rms_norm_2(x, g):
    xf = x.astype(jnp.float32)
    y = xf * lax.rsqrt(jnp.mean(xf * xf, axis=-1, keepdims=True) + EPS)
    return (y * g.astype(jnp.float32)).astype(x.dtype)

def rope_tables(seq, dtype):
    half = QK_ROPE // 2
    inv = ROPE_THETA ** (-jnp.arange(half, dtype=jnp.float32) / half)
    ang = jnp.arange(seq, dtype=jnp.float32)[:, None] * inv[None, :]
    return jnp.cos(ang).astype(dtype), jnp.sin(ang).astype(dtype)

def apply_rope(x, cos, sin):
    half = QK_ROPE // 2
    x1, x2 = x[..., :half], x[..., half:]
    return jnp.concatenate([x1 * cos - x2 * sin, x2 * cos + x1 * sin], axis=-1)

def pool_mixer(h, w, b, scale):
    B, S, D = h.shape
    hg = h.reshape(B, S, N_POOL, POOL_GD).astype(jnp.float32)
    csum = jnp.pad(jnp.cumsum(hg, axis=1), ((0, 0), (1, 0), (0, 0), (0, 0)))
    t = jnp.arange(S)
    means = []
    for g, win in enumerate(POOL_WINDOWS):
        lo = jnp.maximum(t + 1 - win, 0)
        cnt = (t + 1 - lo).astype(jnp.float32)
        means.append((csum[:, 1:, g] - csum[:, lo, g]) / cnt[:, None])
    pooled = (jnp.stack(means, axis=2) - hg).astype(h.dtype)
    y = jnp.einsum('bsgc,gcd->bsgd', pooled, w) + b
    return y.reshape(B, S, D) * scale

def shared_kv(x, kv_in_norm, w_dkv, kv_norm, w_uk, w_uv, cos, sin):
    B, S, _ = x.shape
    hs = rms_norm_2(x, kv_in_norm)
    ckv = hs @ w_dkv
    c_kv = rms_norm_2(ckv[..., :KV_RANK], kv_norm)
    k_rope = apply_rope(ckv[..., KV_RANK:], cos, sin)
    k_nope = (c_kv @ w_uk).reshape(B, S, N_HEADS, QK_NOPE)
    v = (c_kv @ w_uv).reshape(B, S, N_HEADS, V_DIM)
    return k_nope, k_rope, v

def mla_attention(h, k_nope, k_rope, v, wq_down, q_norm, wq_up, wo, cos, sin):
    B, S, _ = h.shape
    cq = rms_norm_2(h @ wq_down, q_norm)
    q = (cq @ wq_up).reshape(B, S, N_HEADS, QK_NOPE + QK_ROPE)
    q_nope = q[..., :QK_NOPE]
    q_rope = apply_rope(q[..., QK_NOPE:], cos[:, None, :], sin[:, None, :])
    nb = S // Q_BLOCK
    qn_b = q_nope.reshape(B, nb, Q_BLOCK, N_HEADS, QK_NOPE).transpose(1, 0, 2, 3, 4)
    qr_b = q_rope.reshape(B, nb, Q_BLOCK, N_HEADS, QK_ROPE).transpose(1, 0, 2, 3, 4)
    k_chunk = jnp.arange(S) // CHUNK

    def attend(args):
        qn, qr, i = args
        s = (jnp.einsum('bqhd,bkhd->bhqk', qn, k_nope)
             + jnp.einsum('bqhr,bkr->bhqk', qr, k_rope)).astype(jnp.float32) * ATTN_SCALE
        q_chunk = (i * Q_BLOCK + jnp.arange(Q_BLOCK)) // CHUNK
        mask = k_chunk[None, :] <= q_chunk[:, None]
        s = jnp.where(mask[None, None], s, -jnp.inf)
        p = jax.nn.softmax(s, axis=-1).astype(v.dtype)
        return jnp.einsum('bhqk,bkhd->bqhd', p, v)

    o = lax.map(attend, (qn_b, qr_b, jnp.arange(nb)))
    o = o.transpose(1, 0, 2, 3, 4).reshape(B, S, N_HEADS * V_DIM)
    return o @ wo

def hier_moe(h, rg_w, rg_b, re_w, re_b, w_gate, w_up, w_down):
    B, S, D = h.shape
    T = B * S
    ht = h.reshape(T, D)
    gp = jax.nn.softmax((ht @ rg_w + rg_b).astype(jnp.float32), axis=-1)
    g_idx = jnp.argmax(gp, axis=-1)
    g_prob = jnp.take_along_axis(gp, g_idx[:, None], axis=-1)[:, 0]
    el = (ht @ re_w + re_b).astype(jnp.float32).reshape(T, N_GROUPS, EXPERTS_PER_GROUP)
    el = jnp.take_along_axis(el, g_idx[:, None, None], axis=1)[:, 0]
    top_p, top_i = lax.top_k(jax.nn.softmax(el, axis=-1), TOP_K)
    gates = g_prob[:, None] * top_p / jnp.sum(top_p, axis=-1, keepdims=True)
    expert_ids = (g_idx[:, None] * EXPERTS_PER_GROUP + top_i).astype(jnp.int32)

    N = T * TOP_K
    flat_e = expert_ids.reshape(N)
    flat_tok = jnp.arange(N, dtype=jnp.int32) // TOP_K
    flat_g = gates.reshape(N)
    order = jnp.argsort(flat_e, stable=True)
    sorted_e = flat_e[order]
    counts = jnp.bincount(flat_e, length=N_EXPERTS).astype(jnp.int32)
    padded = ((counts + ROW_BLOCK - 1) // ROW_BLOCK) * ROW_BLOCK
    pad_end = jnp.cumsum(padded)
    pad_start = pad_end - padded
    start = jnp.cumsum(counts) - counts
    dest = pad_start[sorted_e] + (jnp.arange(N, dtype=jnp.int32) - start[sorted_e])
    n_blocks = N // ROW_BLOCK + N_EXPERTS
    n_rows = n_blocks * ROW_BLOCK
    row_tok = jnp.zeros((n_rows,), jnp.int32).at[dest].set(flat_tok[order])
    row_w = jnp.zeros((n_rows,), jnp.float32).at[dest].set(flat_g[order])
    block_e = jnp.clip(jnp.searchsorted(pad_end, jnp.arange(n_blocks) * ROW_BLOCK, side='right'),
                       0, N_EXPERTS - 1).astype(jnp.int32)
    xb = ht[row_tok].reshape(n_blocks, ROW_BLOCK, D)

    def expert_block(args):
        xr, e = args
        return (jax.nn.silu(xr @ w_gate[e]) * (xr @ w_up[e])) @ w_down[e]

    y = lax.map(expert_block, (xb, block_e)).reshape(n_rows, D).astype(jnp.float32)
    out = jnp.zeros((T, D), jnp.float32).at[row_tok].add(y * row_w[:, None])
    return out.astype(h.dtype).reshape(B, S, D)

def second_inputs(seed: int = 0) -> dict:
    key = jax.random.key(seed)
    ks = iter(jax.random.split(key, 32))
    f32 = jnp.float32

    def nrm(shape, fan_in):
        return jax.random.normal(next(ks), shape, f32) * (fan_in ** -0.5)

    def gain(shape):
        return 1.0 + 0.02 * jax.random.normal(next(ks), shape, f32)

    def small(shape, s=0.01):
        return s * jax.random.normal(next(ks), shape, f32)

    return {
        "x": jax.random.normal(next(ks), (BATCH, SEQ, D_MODEL), f32),
        "pool_norm": gain((N_A, D_MODEL)),
        "pool_w": nrm((N_A, N_POOL, POOL_GD, POOL_GD), POOL_GD),
        "pool_b": small((N_A, N_POOL, POOL_GD)),
        "pool_scale": gain((N_A, D_MODEL)),
        "kv_in_norm": gain((D_MODEL,)),
        "w_dkv": nrm((D_MODEL, KV_RANK + QK_ROPE), D_MODEL),
        "kv_norm": gain((KV_RANK,)),
        "w_uk": nrm((KV_RANK, N_HEADS * QK_NOPE), KV_RANK),
        "w_uv": nrm((KV_RANK, N_HEADS * V_DIM), KV_RANK),
        "attn_norm": gain((N_B, D_MODEL)),
        "wq_down": nrm((N_B, D_MODEL, Q_RANK), D_MODEL),
        "q_norm": gain((N_B, Q_RANK)),
        "wq_up": nrm((N_B, Q_RANK, N_HEADS * (QK_NOPE + QK_ROPE)), Q_RANK),
        "wo": nrm((N_B, N_HEADS * V_DIM, D_MODEL), N_HEADS * V_DIM),
        "ffn_norm": gain((DEPTH, D_MODEL)),
        "router_group_w": nrm((DEPTH, D_MODEL, N_GROUPS), D_MODEL),
        "router_group_b": small((DEPTH, N_GROUPS)),
        "router_expert_w": nrm((DEPTH, D_MODEL, N_EXPERTS), D_MODEL),
        "router_expert_b": small((DEPTH, N_EXPERTS)),
        "w_gate": nrm((DEPTH, N_EXPERTS, D_MODEL, D_EXPERT), D_MODEL),
        "w_up": nrm((DEPTH, N_EXPERTS, D_MODEL, D_EXPERT), D_MODEL),
        "w_down": nrm((DEPTH, N_EXPERTS, D_EXPERT, D_MODEL), D_EXPERT),
        "final_norm": gain((D_MODEL,)),
    }

def second_block(x, pool_norm, pool_w, pool_b, pool_scale, kv_in_norm, w_dkv, kv_norm, w_uk, w_uv,
              attn_norm, wq_down, q_norm, wq_up, wo, ffn_norm, router_group_w, router_group_b,
              router_expert_w, router_expert_b, w_gate, w_up, w_down, final_norm):
    S = x.shape[1]
    cos, sin = rope_tables(S, x.dtype)
    k_nope = k_rope = v = None
    for l in range(DEPTH):
        if l < N_A:
            x = x + pool_mixer(rms_norm_2(x, pool_norm[l]), pool_w[l], pool_b[l], pool_scale[l])
        else:
            if l == N_A:
                k_nope, k_rope, v = shared_kv(x, kv_in_norm, w_dkv, kv_norm, w_uk, w_uv, cos, sin)
            j = l - N_A
            x = x + mla_attention(rms_norm_2(x, attn_norm[j]), k_nope, k_rope, v,
                                  wq_down[j], q_norm[j], wq_up[j], wo[j], cos, sin)
        x = x + hier_moe(rms_norm_2(x, ffn_norm[l]), router_group_w[l], router_group_b[l],
                         router_expert_w[l], router_expert_b[l], w_gate[l], w_up[l], w_down[l])
    return rms_norm_2(x, final_norm)


def setup_inputs(seed=0):
    out = dict(first_inputs(seed))
    for name, value in second_inputs(seed + 1).items():
        if name != "x":
            out[name + "_2"] = value
    return out


def reference(
    x, even_norm, even_w_in, even_q_gain, even_k_gain, even_sconv_w, even_w_out, odd_norm,
    ret_wq, ret_wk, ret_wv, ret_wg, ret_gn_gain, ret_wo, ffn_norm, ffn_w_up, ffn_conv_w,
    ffn_w_down, pool_norm_2, pool_w_2, pool_b_2, pool_scale_2, kv_in_norm_2, w_dkv_2, kv_norm_2,
    w_uk_2, w_uv_2, attn_norm_2, wq_down_2, q_norm_2, wq_up_2, wo_2, ffn_norm_2,
    router_group_w_2, router_group_b_2, router_expert_w_2, router_expert_b_2, w_gate_2, w_up_2,
    w_down_2, final_norm_2,
):
    x = first_block(
        x, even_norm, even_w_in, even_q_gain, even_k_gain, even_sconv_w, even_w_out, odd_norm,
        ret_wq, ret_wk, ret_wv, ret_wg, ret_gn_gain, ret_wo, ffn_norm, ffn_w_up, ffn_conv_w,
        ffn_w_down,
    )
    return second_block(
        x, pool_norm_2, pool_w_2, pool_b_2, pool_scale_2, kv_in_norm_2, w_dkv_2, kv_norm_2,
        w_uk_2, w_uv_2, attn_norm_2, wq_down_2, q_norm_2, wq_up_2, wo_2, ffn_norm_2,
        router_group_w_2, router_group_b_2, router_expert_w_2, router_expert_b_2, w_gate_2,
        w_up_2, w_down_2, final_norm_2,
    )


_drawn_inputs = setup_inputs


def setup_inputs(seed=0):
    import zlib

    import numpy as np

    out = dict(_drawn_inputs(seed))
    spreads = {}
    factors = {'even_q_gain': 4.707,
     'even_k_gain': 4.775,
     'pool_norm_2': 3.025,
     'pool_b_2': 3.457,
     'pool_scale_2': 2.744,
     'kv_in_norm_2': 8.0,
     'kv_norm_2': 8.0,
     'attn_norm_2': 8.0,
     'q_norm_2': 8.0,
     'router_group_b_2': 21.436,
     'router_expert_b_2': 3.86,
     'final_norm_2': 8.104}
    for name, (base, spread) in spreads.items():
        noise = np.random.default_rng([zlib.crc32(name.encode()), seed]).standard_normal(out[name].shape)
        drawn = base * np.exp(spread * noise) if base else spread * noise
        out[name] = __import__('jax').numpy.asarray(drawn.astype(out[name].dtype))
    for name, factor in factors.items():
        out[name] = (out[name] * factor).astype(out[name].dtype)
    return out
```

```python
from contextlib import ExitStack

import numpy as np

import concourse.bass as bass
from concourse import mybir

F32 = mybir.dt.float32
F32R = mybir.dt.float32r
I32 = mybir.dt.int32
ALU = mybir.AluOpType
ACT = mybir.ActivationFunctionType
AX_X = mybir.AxisListType.X

P = 128
S = 256
NT = S // P
D = 1024
DC = D // P
BANK = 512
EPS = 1e-6
NEG = -1.0e30
FAR = -2.0e30

A_HEADS, A_DIM = 8, 64
DILATED = ((128, 1), (512, 4), (2048, 16))
RET_HEADS, RET_K, RET_V = 4, 256, 512
RET_CHUNK = 128
ROPE_BASE = 10000.0
D_FF = 2816
SLAB = 256
N_SLABS = D_FF // SLAB
POOL_WINDOWS = (2, 4, 8, 16)
M_HEADS, M_NOPE, M_ROPE, M_V = 8, 128, 64, 128
Q_RANK, KV_RANK = 384, 256
M_CHUNK = 64
M_SCALE = 1.0 / float(np.sqrt(M_NOPE + M_ROPE))
N_GROUPS, GROUP = 4, 8
N_EXP = N_GROUPS * GROUP
N_ROUTE = N_GROUPS + N_EXP
D_EXP = 512
CAP = 64
N_PAIRS = N_EXP // 2
ROUNDS = S // CAP
SLOTS = 6
UNIT = 4096
SC = P + S


def shape_constants():
    f = np.float32
    q = np.arange(S)[:, None]
    k = np.arange(S)[None, :]
    diff = q - k
    times = np.zeros((S, S))
    for window, dil in DILATED:
        times += (diff >= 0) & (diff % dil == 0) & (diff // dil <= window // dil)
    dil_mask = np.where(times > 0, np.log(np.maximum(times, 1)), NEG)
    mla_mask = np.where(k // M_CHUNK <= q // M_CHUNK, 0.0, NEG)

    def by_tile(m):
        return np.concatenate([m[0:P, 0:P], m[P:S, 0:S]], axis=1)

    log_g = np.log1p(-(2.0 ** (-5.0 - np.arange(RET_HEADS))))
    decay = []
    for h in range(RET_HEADS):
        m = np.where(diff >= 0, np.exp(log_g[h] * np.maximum(diff, 0)), 0.0).T * RET_K ** -0.5
        decay.append(np.concatenate([m[0:P, 0:S], m[P:S, P:S]], axis=1))
    half = RET_K // 2
    inv = f(ROPE_BASE) ** (-np.arange(half, dtype=f) / f(half))
    ang = (np.arange(S, dtype=f)[:, None] * inv[None, :]).astype(f).T
    half = M_ROPE // 2
    inv = f(ROPE_BASE) ** (-np.arange(half, dtype=f) / f(half))
    ang2 = (np.arange(S, dtype=f)[:, None] * inv[None, :]).astype(f).reshape(NT, P, half).transpose(1, 0, 2)
    count = [1.0 / np.minimum(np.arange(S) + 1, w) for w in POOL_WINDOWS]
    row = np.arange(P)
    parts = {
        "ident": np.eye(P),
        "dil_mask": by_tile(dil_mask),
        "mla_mask": by_tile(mla_mask),
        "r_cos": np.cos(ang), "r_sin": np.sin(ang),
        "m_cos": np.cos(ang2).reshape(P, -1), "m_sin": np.sin(ang2).reshape(P, -1),
        "inv_count": np.tile(np.concatenate(count)[None, :], (P, 1)),
        "before": (row[:, None] < row[None, :]) * 1.0,
        "ones": np.ones((P, P)),
        "column": np.tile(row[None, :], (P, 1)),
        "first4": np.tile(N_GROUPS - np.arange(N_GROUPS)[None, :], (P, 1)),
        "first32": np.tile(N_EXP - np.arange(N_EXP)[None, :], (P, 1)),
        "row_of": np.tile(CAP * np.arange(N_EXP)[None, :], (P, 1)),
        "minus_half": np.full((P, NT * 2 * A_HEADS), -0.5),
    }
    where, at = {}, 0
    for name, a in parts.items():
        where[name] = (at, at + a.shape[1])
        at += a.shape[1]
    table = np.concatenate([a.astype(f) for a in parts.values()], axis=1)
    return table, where, np.concatenate(decay, axis=1).astype(f)


PARAMS = [
    ("g_even", DC), ("g_ffn0", DC), ("g_odd", DC), ("g_ffn1", DC), ("g_pool", DC),
    ("g_moe0", DC), ("g_kvin", DC), ("g_attn", DC), ("g_moe1", DC),
    ("q_gain", 1), ("k_gain", 1), ("sconv", 12), ("gn", 16), ("conv0", 132), ("conv1", 132),
    ("kv_norm", 2), ("q_norm", 3), ("route0", DC * N_ROUTE), ("route1", DC * N_ROUTE),
    ("route_b0", N_ROUTE), ("route_b1", N_ROUTE),
]
ROWS = [("pool_b", D), ("pool_scale", D), ("final", D)]


def places(table):
    where, at = {}, 0
    for name, n in table:
        where[name] = (at, at + n)
        at += n
    return where, at


class Chain:

    def __init__(self, eng, sem):
        self.eng, self.sem, self.n, self.turn, self.per, self.base = eng, sem, 0, None, 0, 0

    def __call__(self, ins):
        self.n += 1
        ins.then_inc(self.sem, 1)
        self.eng.wait_ge(self.sem, self.n if self.turn is None else self.turn * self.per + self.n)

    def loop(self, turn, per):
        self.turn, self.per, self.base = turn, per, self.n

    def done(self, turns):
        assert self.n - self.base == self.per, (self.n - self.base, self.per)
        self.turn, self.n = None, self.base + self.per * turns


def build(nc, const, decay_in, params, rows, x_in, w_in, w_out, wq, wk, wv, wg, wo_r, w_up, w_down, pool_w, w_dkv, w_uk, w_uv,
          wq_down, wq_up, wo_m, e_gate, e_up, e_down, out):
    const_at = shape_constants()[1]
    param_at, n_params = places(PARAMS)
    row_at, n_rows = places(ROWS)
    n_const = const.shape[1]
    ctx = ExitStack()
    with ctx:
        def sb(name, shape, dt=F32):
            return ctx.enter_context(nc.sbuf_tensor(name, shape, dt))

        def sem(name):
            return ctx.enter_context(nc.semaphore(name))

        ring = sb("ring", [P, SLOTS, UNIT])
        cst = sb("cst", [P, n_const])
        par = sb("par", [P, n_params])
        x = sb("x_res", [P, NT, D])
        hs = sb("hs", [P, NT, D])
        small = sb("small", [P, 512])
        flag = sb("flag", [P, 2], I32)
        WORK = 14720
        late_at = -(-nc.sbuf_base // 32) * 32
        xnT_at = late_at + 4 * n_rows
        work_at = xnT_at + 4 * DC * S

        def placed(name, shape, at, dt=F32):
            return nc.alloc_sbuf_tensor_at(name, shape, dt, offset=at)

        late = placed("late", [P, n_rows], late_at)
        xnT = placed("xnT", [P, DC, S], xnT_at)[:, :, :]
        work = placed("work", [P, WORK], work_at)
        PS = ctx.enter_context(nc.psum_tensor("PS", [P, 8, BANK], F32))

        def C(name):
            a, b = const_at[name]
            return cst[:, a:b]

        def G(name):
            a, b = param_at[name]
            return par[:, a:b]

        def R(name):
            a, b = row_at[name]
            return late[:, a:b]

        def view(v, *shape):
            if len(shape) == 2:
                return v.rearrange("p (a b) -> p a b", b=shape[1])
            if len(shape) == 3:
                return v.rearrange("p (a b c) -> p a b c", b=shape[1], c=shape[2])
            return v

        def area(at, *shape):
            n = int(np.prod(shape))
            assert at + n <= WORK
            return view(work[:, at:at + n], *shape)

        def scratch(at, *shape):
            return view(small[:, at:at + int(np.prod(shape))], *shape)

        def bank(b, *shape):
            return view(PS[:, b, 0:int(np.prod(shape))], *shape) if shape else PS[:, b, :]

        def spread(col, *shape):
            return col.unsqueeze(len(col.shape)).to_broadcast([P, *shape])

        ident = C("ident")
        decay = view(late[:, 0:RET_HEADS * SC], RET_HEADS, SC)

        ss, ms, rstd = scratch(0, NT), scratch(2, NT), scratch(4, NT)
        hss, hms, hrstd = scratch(8, NT, 16), scratch(40, NT, 16), scratch(72, NT, 16)
        nmx, den, rden = scratch(104, 2, 2), scratch(108, 2, 2), scratch(112, 2, 2)
        gqk = scratch(116, 1)
        stats, mv, gvar, grstd = scratch(120, NT, 6), scratch(132, NT, 2), scratch(136, NT), scratch(138, NT)
        gmax, gprob, cmax, m1, m2 = (scratch(144 + 2 * i, NT) for i in range(5))
        r2, rd2, count_max = scratch(154, NT), scratch(156, NT), scratch(158, 1)
        pos, gate = scratch(160, NT, 2), scratch(164, NT, 2)
        rank1, rank2, over = scratch(168, NT), scratch(170, NT), scratch(172, NT)
        gsh, goh, gcand, pen = (scratch(176 + 8 * i, NT, N_GROUPS) for i in range(4))
        lg = scratch(208, NT, N_ROUTE)

        qk_t = area(0, NT, 2 * BANK)
        v_t = area(2048, NT, BANK)
        qT, kT = area(3072, 4, S), area(4096, 4, S)
        gbT, gcT, zT = area(5120, 4, S), area(6144, 4, S), area(7168, 4, S)
        mixT = area(8192, 8, S)
        scor, prob, probT = area(10240, 2, SC), area(11008, 2, SC), area(11776, 2, SC)
        sq = area(12544, D)
        convt = area(13568, 4, S)
        f_u = area(0, 4, S)
        f_cw = area(1024, 12)
        f_at = work_at + 4 * 1040
        HALF = UNIT // 2
        f_w = [[placed(f"f_w_{kind}_{part}", [P, HALF], f_at + 4 * HALF * (2 * i + j), F32R)
                for j, part in enumerate(("hi", "lo"))] for i, kind in enumerate(("gate", "value", "down"))]
        f_h = [placed(f"f_h_{part}", [P, 2, S], f_at + 4 * (6 * HALF + j * 2 * S), F32R) for j, part in enumerate(("hi", "lo"))]
        f_x = [placed("f_x_hi", [P, DC, S], xnT_at, F32R), placed("f_x_lo", [P, DC, S], late_at, F32R)]
        assert 1040 + 6 * HALF + 4 * S <= WORK and DC * S <= n_rows
        rqT, rkT = area(0, DC, S), area(2048, DC, S)
        rv = area(4096, NT, RET_HEADS * RET_V)
        ryT = area(8192, 16, S)
        rope_c, rope_s = area(12288, 2, S), area(12800, 2, S)
        r_sg = area(12288, NT, RET_V)
        r_sT = area(13312, SC)
        r_y = area(13696, NT, RET_V)
        pl_a, pl_b, pl_o = area(0, DC, S), area(2048, DC, S), area(4096, DC, S)
        pl_y = area(6144, NT, D)
        xkvT = area(0, DC, S)
        qnT = area(0, M_HEADS, S)
        ckv, cq, kr2 = area(2048, NT, 320), area(2688, NT, Q_RANK), area(3456, NT, P)
        m_aT = area(2048, M_HEADS, S)
        ckvT, cqT = area(4096, 2, S), area(4608, 3, S)
        knT = area(5376, M_HEADS, S)
        m_v = area(7424, NT, M_HEADS * M_V)
        qr, qrT = area(9472, NT, BANK), area(10496, 4, S)
        m_scor, m_prob, m_probT = area(11520, 2, SC), area(12288, 2, SC), area(13056, 2, SC)
        m_sq, krT = area(13824, Q_RANK), area(14208, S)
        sel, wsel, wtmp = area(0, 2, NT, P), area(512, 2, NT, P), area(1024, P)
        wT, xg = area(1152, 2, S), area(1664, 2, DC * P)
        sg, e_h, e_hT, e_y = area(3712, BANK), area(4224, BANK), area(4736, 4, P), area(5248, D)
        oh1, oh2, ohs, em, er, ea = (area(6400 + 64 * i, NT, N_EXP) for i in range(6))

        named = {}

        def E(name):
            if name not in named:
                named[name] = sem(name)
            return named[name]

        loaded = [sem(f"loaded{i}") for i in range(SLOTS)]
        used = sem("used")

        class Units:

            def __init__(self, eng):
                self.eng, self.n, self.turn, self.per, self.base = eng, 0, None, 0, 0

            def slot(self, k=0):
                return ring[:, (self.n + k) % SLOTS, :]

            def wait(self, k=0):
                u = self.n + k
                there = 16 * (u // SLOTS + 1)
                if self.turn is not None:
                    there = self.turn * (16 * self.per // SLOTS) + there
                self.eng.wait_ge(loaded[u % SLOTS], there)

            def load(self, dst, src):
                u = self.n
                if u >= SLOTS:
                    done = u - SLOTS + 1
                    self.eng.wait_ge(used, done if self.turn is None else self.turn * self.per + done)
                self.eng.dma_start(dst, src).then_inc(loaded[u % SLOTS], 16)
                self.n += 1

            def loop(self, turn, per):
                self.turn, self.per, self.base = turn, per, self.n

            def done(self, turns):
                assert self.n - self.base == self.per
                self.turn, self.n = None, self.base + self.per * turns

        NORMS = ["g_even", "g_ffn0", "g_odd", "g_ffn1", "g_pool", "g_moe0", "g_attn", "g_moe1"]
        X_DONE = [("x_in", 16 * NT), ("even_add", 4), ("ffn_add", 4), ("ret_add", 4), ("ffn_add", 8),
                  ("pool_add", NT), ("moe_add", 4 * N_PAIRS + 1), ("mla_add", 4), ("moe_add", 8 * N_PAIRS + 2)]
        SPLIT = (1, 3)
        A_BANKS = [sum(4 if i in SPLIT or i == 6 else 2 for i in range(k)) for k in range(9)]
        D_BANKS = A_BANKS

        def chunk(t, k, c):
            if NORMS[k] == "g_pool":
                return t[:, c * P:(c + 1) * P]
            return t[:, c:D:DC]

        def norm_act(act, link, k):
            name, value = X_DONE[k]
            act.wait_ge(E(name), value)
            for t in range(NT):
                link(nc.scalar.activation(hs[:, t, :], x[:, t, :], ACT.Square,
                                          accum_out=ss[:, t:t + 1]))
            nc.scalar.activation(ms, ss, ACT.Copy, bias=EPS, scale=1.0 / D).then_inc(E("n_ms"), 1)
            if k == 8:
                return
            g = G(NORMS[k])
            for b in (range(4) if k == 6 or k in SPLIT else [1, 3]):
                act.wait_ge(E("n_tr"), 4 * k + b + 1)
                if k == 6:
                    act.wait_ge(E("n_xd"), D_BANKS[k] + b + 1)
                for j in range(2):
                    c = 2 * b + j
                    last = nc.scalar.activation((f_x[0] if k in SPLIT else xnT)[:, c, :], bank(b)[:, j * S:(j + 1) * S], ACT.Copy,
                                                scale=g[:, c:c + 1])
                last.then_inc(E("n_xa"), 1)

        def norm_pool(pool, k):
            pool.wait_ge(E("n_ms"), k + 1)
            nc.gpsimd.tensor_tensor(rstd, ms, C("minus_half")[:, 0:NT], ALU.pow).then_inc(E("n_rstd"), 1)

        def norm_dve(dve, link, k):
            dve.wait_ge(E("n_rstd"), k + 1)
            for t in range(NT):
                nc.vector.tensor_scalar(hs[:, t, :], x[:, t, :], rstd[:, t:t + 1], None,
                                        ALU.mult).then_inc(E("n_hs"), 1)
            g = G("g_kvin" if k == 6 else NORMS[k])
            if k in SPLIT:
                for b in range(4):
                    dve.wait_ge(E("n_xa"), A_BANKS[k] + b + 1)
                    for c in (2 * b, 2 * b + 1):
                        last = nc.vector.scalar_tensor_tensor(
                            f_x[1][:, c, :], bank(b)[:, (c % 2) * S:(c % 2 + 1) * S], g[:, c:c + 1],
                            f_x[0][:, c, :].bitcast(F32), ALU.mult, ALU.subtract)
                    last.then_inc(E("n_xd"), 1)
                return
            dst = xkvT if k == 6 else xnT
            for b in ([0, 2] if k != 6 else range(4)):
                dve.wait_ge(E("n_tr"), 4 * k + b + 1)
                nc.vector.tensor_tensor(dst[:, 2 * b:2 * b + 2, :], bank(b, 2, S),
                                        spread(g[:, 2 * b:2 * b + 2], 2, S), ALU.mult).then_inc(E("n_xd"), 1)

        def norm_pe(pe, k):
            pe.wait_ge(E("n_hs"), NT * (k + 1))
            for b in range(4):
                for j in range(2):
                    for t in range(NT):
                        last = nc.tensor.transpose(bank(b)[:, j * S + t * P:j * S + (t + 1) * P],
                                                   chunk(hs[:, t, :], k, 2 * b + j), ident)
                last.then_inc(E("n_tr"), 1)

        def norm_done(eng, k):
            eng.wait_ge(E("n_xa"), A_BANKS[k + 1])
            eng.wait_ge(E("n_xd"), D_BANKS[k + 1])

        def rows_of(dst, lhs, w, n):
            for c in range(n):
                last = nc.tensor.matmul(dst, lhs(c), w(c), start=(c == 0), stop=(c == n - 1))
            return last

        def tile_of(src, t):
            return lambda c: src[:, c, t * P:(t + 1) * P]

        def first_head(kind):
            return 8 if kind == "ml" else 0

        def heads_pe(pe, kind, score, value, out_of, per_evac):
            for i in range(8 + 2):
                if i < 8:
                    h = i
                    if h >= 2:
                        pe.wait_ge(E("at_sc"), first_head(kind) + h - 1)
                    last = score(h, bank(h % 2))
                    last.then_inc(E("at_s_ps"), 1)
                if 1 <= i <= 8:
                    h = i - 1
                    pe.wait_ge(E("at_p"), first_head(kind) + h + 1)
                    if h >= 2:
                        pe.wait_ge(E("at_pT"), first_head(kind) + h - 1)
                    p = (prob if kind == "ev" else m_prob)[:, h % 2, :]
                    for j in range(3):
                        last = nc.tensor.transpose(bank(2 + h % 2)[:, j * P:(j + 1) * P], p[:, j * P:(j + 1) * P], ident)
                    last.then_inc(E("at_t_ps"), 1)
                if i >= 2:
                    h = i - 2
                    pe.wait_ge(E("at_pT"), first_head(kind) + h + 1)
                    n = h // per_evac
                    if h % per_evac == 0 and n >= 2:
                        pe.wait_ge(E("at_o"), (4 if kind == "ml" else 0) + n - 1)
                    pT = (probT if kind == "ev" else m_probT)[:, h % 2, :]
                    dst = out_of(h)
                    nc.tensor.matmul(dst, value(h, 0), pT[:, 0:S], start=True, stop=False)
                    nc.tensor.matmul(dst[:, P:S], value(h, 1), pT[:, S:SC], start=False,
                                     stop=True).then_inc(E("at_o_ps"), 1)

        def heads_dve(dve, link, kind, mask, scale):
            sc, pr = (scor, prob) if kind == "ev" else (m_scor, m_prob)
            for i in range(8 + 1):
                if i < 8:
                    h = i
                    dve.wait_ge(E("at_s_ps"), first_head(kind) + h + 1)
                    if h >= 2:
                        dve.wait_ge(E("at_e"), first_head(kind) + h - 1)
                    nc.vector.scalar_tensor_tensor(sc[:, h % 2, :], bank(h % 2)[:, 0:SC], scale, mask, ALU.mult,
                                                   ALU.add).then_inc(E("at_sc"), 1)
                    dve.wait_ge(E("at_sc"), first_head(kind) + h + 1)
                    nc.vector.tensor_reduce(nmx[:, h % 2, 0:1], sc[:, h % 2, 0:P], AX_X, ALU.max, negate=True)
                    nc.vector.tensor_reduce(nmx[:, h % 2, 1:2], sc[:, h % 2, P:SC], AX_X, ALU.max,
                                            negate=True).then_inc(E("at_m"), 1)
                if i >= 1:
                    h = i - 1
                    dve.wait_ge(E("at_e"), first_head(kind) + h + 1)
                    link(nc.vector.reciprocal(rden[:, h % 2, :], den[:, h % 2, :]))
                    p = pr[:, h % 2, :]
                    nc.vector.tensor_scalar(p[:, 0:P], p[:, 0:P], rden[:, h % 2, 0:1], None, ALU.mult)
                    nc.vector.tensor_scalar(p[:, P:SC], p[:, P:SC], rden[:, h % 2, 1:2], None,
                                            ALU.mult).then_inc(E("at_p"), 1)

        def heads_act(act, link, kind, dst_of, src_of, per_evac):
            sc, pr, prT = (scor, prob, probT) if kind == "ev" else (m_scor, m_prob, m_probT)
            for i in range(8 + 2):
                if i < 8:
                    h = i
                    act.wait_ge(E("at_m"), first_head(kind) + h + 1)
                    if h >= 2:
                        act.wait_ge(E("at_t_ps"), first_head(kind) + h - 1)
                    nc.scalar.activation(pr[:, h % 2, 0:P], sc[:, h % 2, 0:P], ACT.Exp, bias=nmx[:, h % 2, 0:1],
                                         accum_out=den[:, h % 2, 0:1])
                    nc.scalar.activation(pr[:, h % 2, P:SC], sc[:, h % 2, P:SC], ACT.Exp, bias=nmx[:, h % 2, 1:2],
                                         accum_out=den[:, h % 2, 1:2]).then_inc(E("at_e"), 1)
                if 1 <= i <= 8:
                    h = i - 1
                    act.wait_ge(E("at_t_ps"), first_head(kind) + h + 1)
                    if h >= 2:
                        act.wait_ge(E("at_o_ps"), first_head(kind) + h - 1)
                    nc.scalar.activation(prT[:, h % 2, :], bank(2 + h % 2)[:, 0:SC],
                                         ACT.Copy).then_inc(E("at_pT"), 1)
                if i >= 2 and (i - 2) % per_evac == per_evac - 1:
                    h = i - 2
                    act.wait_ge(E("at_o_ps"), first_head(kind) + h + 1)
                    nc.scalar.activation(dst_of(h // per_evac), src_of(h // per_evac),
                                         ACT.Copy).then_inc(E("at_o"), 1)

        def residual_dve(dve, name, before=0):
            for n in range(2):
                for t in range(NT):
                    dve.wait_ge(E(name + "_ps"), before + n * NT + t + 1)
                    v = x[:, t, n * BANK:(n + 1) * BANK]
                    nc.vector.tensor_tensor(v, v, bank(n * NT + t), ALU.add).then_inc(E(name + "_add"), 1)

        def even_load(units):
            for n in range(6):
                units.load(view(units.slot(), DC, BANK),
                           w_in[0].rearrange("(p c) n -> p c n", c=DC)[:, :, n * BANK:(n + 1) * BANK])
            for n in range(2):
                units.load(view(units.slot(), DC, BANK),
                           w_out[0].rearrange("(c p) n -> p c n", p=P)[:, :, n * BANK:(n + 1) * BANK])

        def even_pe(pe, units):
            norm_done(pe, 0)
            for n in range(3):
                units.wait()
                w = view(units.slot(), DC, BANK)
                for t in range(NT):
                    i = n * NT + t
                    if i >= 4:
                        pe.wait_ge(E("ev_qkv"), i - 3)
                    last = rows_of(bank(4 + i % 4), tile_of(xnT, t), lambda c: w[:, c, :], DC)
                    last.then_inc(E("ev_qkv_ps"), 1)
                units.n += 1
                pe.wait_ge(E("ev_qkv_ps"), NT * (n + 1))
                pe.sem_inc(used, 1)
            for n in range(3):
                units.wait()
                w = view(units.slot(), DC, BANK)
                if n == 2:
                    pe.wait_ge(E("ev_gb"), 2)
                for m in range(4):
                    dst = bank(2 * (n % 2) + m // 2)[:, (m % 2) * S:(m % 2 + 1) * S]
                    last = rows_of(dst, lambda c: w[:, c, m * P:(m + 1) * P], lambda c: xnT[:, c, :], DC)
                    if m == 1:
                        last.then_inc(E("ev_cv_ps"), 1)
                last.then_inc(E("ev_cv_ps"), 1)
                units.n += 1
                pe.wait_ge(E("ev_cv_ps"), 2 * (n + 1))
                pe.sem_inc(used, 1)
            pe.wait_ge(E("ev_qkv"), 6)
            pe.wait_ge(E("ev_qkn"), NT)
            for half in range(2):
                for j in range(4):
                    for t in range(NT):
                        last = nc.tensor.transpose(
                            bank(4 + 2 * half + j // 2)[:, (j % 2) * S + t * P:(j % 2) * S + (t + 1) * P],
                            qk_t[:, t, half * BANK + j * P:half * BANK + (j + 1) * P], ident)
                last.then_inc(E("ev_qkT_ps"), 1)
            pe.wait_ge(E("ev_qT"), 2)
            pe.wait_ge(E("ev_kT"), 2)
            pe.wait_ge(E("ev_z"), 2)
            pe.wait_ge(E("ev_gb"), 4)

            def score(h, dst):
                a = A_DIM * (h % 2)
                q, k = qT[a:a + A_DIM, h // 2, :], kT[a:a + A_DIM, h // 2, :]
                nc.tensor.matmul(dst[:, 0:P], q[:, 0:P], k[:, 0:P], start=True, stop=True)
                return nc.tensor.matmul(dst[:, P:SC], q[:, P:S], k, start=True, stop=True)

            heads_pe(pe, "ev", score, lambda h, t: v_t[:, t, h * A_DIM:(h + 1) * A_DIM],
                     lambda h: PS[A_DIM * (h % 2):A_DIM * (h % 2) + A_DIM, 4 + (h // 2) % 2, 0:S], 2)
            pe.wait_ge(E("at_o"), 4)
            pe.wait_ge(E("ev_conv"), 1)
            for n in range(2):
                units.wait()
                w = view(units.slot(), DC, BANK)
                for t in range(NT):
                    last = rows_of(bank(n * NT + t), tile_of(mixT, t), lambda c: w[:, c, :], DC)
                    last.then_inc(E("even_ps"), 1)
                units.n += 1
                pe.wait_ge(E("even_ps"), NT * (n + 1))
                pe.sem_inc(used, 1)

        def even_act(act, link):
            for i in range(6):
                n, t = i // NT, i % NT
                act.wait_ge(E("ev_qkv_ps"), i + 1)
                dst = v_t[:, t, :] if n == 2 else qk_t[:, t, n * BANK:(n + 1) * BANK]
                nc.scalar.activation(dst, bank(4 + i % 4), ACT.Copy).then_inc(E("ev_qkv"), 1)
            for n, dst in enumerate([gbT, gcT]):
                for b in range(2):
                    act.wait_ge(E("ev_cv_ps"), 2 * n + b + 1)
                    nc.scalar.activation(dst[:, 2 * b:2 * b + 2, :], bank(2 * n + b, 2, S),
                                         ACT.Copy).then_inc(E("ev_gb"), 1)
            act.wait_ge(E("ev_gqk"), 1)
            act.wait_ge(E("ev_qkT_ps"), 1)
            for b in range(2):
                nc.scalar.activation(qT[:, 2 * b:2 * b + 2, :], bank(4 + b, 2, S), ACT.Copy,
                                     scale=gqk).then_inc(E("ev_qT"), 1)
            heads_act(act, link, "ev", lambda j: mixT[:, j, :], lambda j: bank(4 + j % 2)[:, 0:S], 2)

        def even_pool(pool):
            pool.wait_ge(E("ev_hms"), 1)
            nc.gpsimd.tensor_tensor(hrstd, hms, view(C("minus_half"), NT, 2 * A_HEADS), ALU.pow).then_inc(E("ev_hr"), 1)

        def conv3(link, dst, src, taps):
            for j in range(dst.shape[1]):
                link(nc.vector.tensor_scalar(dst[:, j, :], src[:, j, :], taps[:, 3 * j + 2:3 * j + 3], None, ALU.mult))
                for back in (1, 2):
                    link(nc.vector.scalar_tensor_tensor(dst[:, j, back:S], src[:, j, 0:S - back],
                                                        taps[:, 3 * j + 2 - back:3 * j + 3 - back],
                                                        dst[:, j, back:S], ALU.mult, ALU.add))

        def even_dve(dve, link):
            nc.vector.tensor_tensor(gqk, G("q_gain"), G("k_gain"), ALU.mult).then_inc(E("ev_gqk"), 1)
            dve.wait_ge(E("ev_qkv"), 4)
            for t in range(NT):
                link(nc.vector.tensor_tensor(sq, qk_t[:, t, :], qk_t[:, t, :], ALU.mult))
                link(nc.vector.tensor_reduce(hss[:, t, :], view(sq, 16, A_DIM), AX_X, ALU.add))
            nc.vector.tensor_scalar(hms, hss, 1.0 / A_DIM, EPS, ALU.mult, ALU.add).then_inc(E("ev_hms"), 1)
            dve.wait_ge(E("ev_hr"), 1)
            for t in range(NT):
                v = view(qk_t[:, t, :], 16, A_DIM)
                nc.vector.tensor_tensor(v, v, spread(hrstd[:, t, :], 16, A_DIM), ALU.mult).then_inc(E("ev_qkn"), 1)
            dve.wait_ge(E("ev_qkT_ps"), 2)
            for b in range(2):
                nc.vector.tensor_copy(kT[:, 2 * b:2 * b + 2, :], bank(6 + b, 2, S)).then_inc(E("ev_kT"), 1)
            dve.wait_ge(E("ev_gb"), 4)
            for b in range(2):
                dve.wait_ge(E("ev_cv_ps"), 4 + b + 1)
                nc.vector.tensor_tensor(zT[:, 2 * b:2 * b + 2, :], gcT[:, 2 * b:2 * b + 2, :], bank(b, 2, S),
                                        ALU.mult).then_inc(E("ev_z"), 1)
            dve.wait_ge(E("ev_z"), 2)
            conv3(link, convt, zT, G("sconv"))
            nc.vector.tensor_tensor(mixT[:, 4:8, :], convt, gbT, ALU.mult).then_inc(E("ev_conv"), 1)
            heads_dve(dve, link, "ev", C("dil_mask"), A_DIM ** -0.5)
            residual_dve(dve, "even")

        IN_LOOP = 3
        LOOP_TURNS = (N_SLABS - 2) // IN_LOOP
        assert 2 + IN_LOOP * LOOP_TURNS == N_SLABS
        GATE, VALUE, DOWN = range(3)

        def ffn_load(sp, units, l):
            up = w_up[l].rearrange("(p c) (g n) -> p c g n", c=DC, g=2)
            down = w_down[l].rearrange("(c p) n -> p c n", p=P)

            def load_up(at):
                units.load(view(units.slot(), DC, 2, SLAB), up[:, :, :, bass.ds(at, SLAB)])

            def load_down(at):
                units.load(view(units.slot()[:, 0:2 * D], 2, D), down[:, bass.ds(at, 2), :])

            load_up(0)
            load_up(SLAB)
            load_down(0)
            with sp.Fori(0, LOOP_TURNS) as turn:
                units.loop(turn, SLOTS)
                for j in range(IN_LOOP):
                    load_up(turn * (IN_LOOP * SLAB) + (2 + j) * SLAB)
                    load_down(turn * (IN_LOOP * 2) + (1 + j) * 2)
                units.done(LOOP_TURNS)
            load_down(2 * (N_SLABS - 1))

        SPLITS = 3 * N_SLABS

        def split_count(l, kind, s):
            if isinstance(s, int) and s == 0 and kind != DOWN:
                return l * SPLITS + 1 + kind
            if kind == DOWN:
                last = isinstance(s, int) and s == N_SLABS - 1
                return l * SPLITS + (SPLITS if last else 3 * s + 5)
            return l * SPLITS + 3 * s + kind

        def three_products(dst, lhs, rhs, start, stop):
            nc.tensor.matmul(dst, lhs[0], rhs[0], start=start, stop=False, skip_group_check=True)
            nc.tensor.matmul(dst, lhs[0], rhs[1], start=False, stop=False, skip_group_check=True)
            return nc.tensor.matmul(dst, lhs[1], rhs[0], start=False, stop=stop, skip_group_check=True)

        def ffn_pe(pe, units, l):
            s0 = l * N_SLABS

            def up(s):
                for kind in (GATE, VALUE):
                    pe.wait_ge(E("ffn_split"), split_count(l, kind, s))
                    w = [view(f_w[kind][i][:, :], DC, SLAB) for i in range(2)]
                    for j in range(2):
                        m = 2 * kind + j
                        if l > 0 or not isinstance(s, int) or s > 0:
                            pe.wait_ge(E("ffn_u"), 4 * (s0 + s))
                        for c in range(DC):
                            last = three_products(bank(4 + m)[:, 0:S], [v[:, c, j * P:(j + 1) * P] for v in w],
                                                  [v[:, c, :] for v in f_x], c == 0, c == DC - 1)
                        last.then_inc(E("ffn_u_ps"), 1)

            def down(s, start=False, stop=False):
                pe.wait_ge(E("ffn_split"), split_count(l, DOWN, s))
                pe.wait_ge(E("ffn_h"), 1 + s0 + s + 1)
                w = [view(f_w[DOWN][i][:, :], 2, D) for i in range(2)]
                for n in range(2):
                    for t in range(NT):
                        for c in range(2):
                            last = three_products(bank(n * NT + t), [v[:, c, t * P:(t + 1) * P] for v in f_h],
                                                  [v[:, c, n * BANK:(n + 1) * BANK] for v in w],
                                                  start and c == 0, stop and c == 1)
                        if stop:
                            last.then_inc(E("ffn_ps"), 1)
                if not stop:
                    last.then_inc(E("ffn_d"), 1)

            if l == 0:
                pe.sem_inc(E("ffn_d"), 1)
            norm_done(pe, 1 + 2 * l)
            up(0)
            up(1)
            down(0, start=True)
            with pe.Fori(2, N_SLABS) as s:
                up(s)
                down(s - 1)
            down(N_SLABS - 1, stop=True)
            units.n += 2 * N_SLABS

        def raw_half(kind, slot):
            if kind == DOWN:
                return view(slot[:, 0:HALF], DC, SLAB)
            return view(slot, DC, 2, SLAB)[:, :, kind, :]

        def ffn_slabs(eng, units, slab, link=None, links=0):
            slab(0)
            with eng.Fori(0, LOOP_TURNS) as turn:
                units.loop(turn, SLOTS)
                if link:
                    link.loop(turn, IN_LOOP * links)
                for j in range(IN_LOOP):
                    slab(turn * IN_LOOP + (1 + j))
                units.done(LOOP_TURNS)
                if link:
                    link.done(LOOP_TURNS)
            slab(N_SLABS - 1)

        def ffn_act(act, units, l):
            s0 = l * N_SLABS

            def newest(s, m):
                act.wait_ge(E("ffn_cw"), s0 + s + 1)
                act.wait_ge(E("ffn_u_ps"), 4 * (s0 + s) + m + 1)
                act.wait_ge(E("ffn_h"), 1 + s0 + s)
                nc.scalar.activation(f_u[:, m, :], bank(4 + m)[:, 0:S], ACT.Copy,
                                     scale=f_cw[:, 3 * m + 2:3 * m + 3]).then_inc(E("ffn_t"), 1)

            def round_half(kind, slot):
                nc.scalar.activation(view(f_w[kind][0][:, :], DC, SLAB), raw_half(kind, slot),
                                     ACT.Copy).then_inc(E("ffn_round"), 1)

            def slab(s):
                last = isinstance(s, int) and s == N_SLABS - 1
                for kind in (GATE, VALUE):
                    for j in range(2):
                        newest(s, 2 * kind + j)
                    if not last:
                        if kind == GATE:
                            units.wait()
                        round_half(kind, units.slot())
                act.wait_ge(E("ffn_u"), 4 * (s0 + s) + 2)
                nc.scalar.activation(f_u[:, 0:2, :], f_u[:, 0:2, :], ACT.Silu).then_inc(E("ffn_g"), 1)
                if not last:
                    units.n += 1
                units.wait()
                act.wait_ge(E("ffn_d"), 1 + s0 - l + s)
                round_half(DOWN, units.slot())
                units.n += 1

            units.wait()
            for kind in (GATE, VALUE):
                if l > 0:
                    act.wait_ge(E("ffn_u_ps"), 4 * s0)
                    act.wait_ge(E("ffn_ps"), 2 * NT * l)
                round_half(kind, units.slot())
            units.n += 1
            ffn_slabs(act, units, slab)

        FFN_LINKS = 7

        def ffn_dve(dve, units, link, l):
            s0 = l * N_SLABS
            taps = G(f"conv{l}")

            def conv(s, m):
                dve.wait_ge(E("ffn_t"), 4 * (s0 + s) + m + 1)
                u = bank(4 + m)
                link(nc.vector.scalar_tensor_tensor(f_u[:, m, 1:S], u[:, 0:S - 1], f_cw[:, 3 * m + 1:3 * m + 2],
                                                    f_u[:, m, 1:S], ALU.mult, ALU.add))
                nc.vector.scalar_tensor_tensor(f_u[:, m, 2:S], u[:, 0:S - 2], f_cw[:, 3 * m:3 * m + 1],
                                               f_u[:, m, 2:S], ALU.mult, ALU.add).then_inc(E("ffn_u"), 1)

            def rest_half(kind, s, slot):
                dve.wait_ge(E("ffn_round"), split_count(l, kind, s))
                nc.vector.tensor_tensor(view(f_w[kind][1][:, :], DC, SLAB), raw_half(kind, slot),
                                        view(f_w[kind][0][:, :], DC, SLAB).bitcast(F32), ALU.subtract).then_inc(E("ffn_split"), 1)

            def give_back(kind, s):
                dve.wait_ge(E("ffn_split"), split_count(l, kind, s))
                dve.sem_inc(used, 1)
                units.n += 1

            def slab(s):
                last = isinstance(s, int) and s == N_SLABS - 1
                link(nc.vector.tensor_copy(f_cw, taps[:, bass.ds(s * 12, 12)]))
                dve.sem_inc(E("ffn_cw"), 1)
                for kind in (GATE, VALUE):
                    for j in range(2):
                        conv(s, 2 * kind + j)
                    if not last:
                        rest_half(kind, s + 1, units.slot())
                if not last:
                    give_back(VALUE, s + 1)
                dve.wait_ge(E("ffn_u"), 4 * (s0 + s) + 4)
                dve.wait_ge(E("ffn_g"), s0 + s + 1)
                link(nc.vector.tensor_tensor(f_u[:, 0:2, :], f_u[:, 0:2, :], f_u[:, 2:4, :], ALU.mult))
                dve.wait_ge(E("ffn_d"), 1 + s0 - l + s)
                link(nc.vector.tensor_copy(f_h[0][:, :, :], f_u[:, 0:2, :]))
                nc.vector.tensor_tensor(f_h[1][:, :, :], f_u[:, 0:2, :], f_h[0][:, :, :].bitcast(F32),
                                        ALU.subtract).then_inc(E("ffn_h"), 1)
                rest_half(DOWN, s, units.slot())
                give_back(DOWN, s)

            if l == 0:
                dve.sem_inc(E("ffn_h"), 1)
            for kind in (GATE, VALUE):
                rest_half(kind, 0, units.slot())
            give_back(VALUE, 0)
            ffn_slabs(dve, units, slab, link, FFN_LINKS)
            residual_dve(dve, "ffn", 4 * l)

        def ret_load(units):
            for w, n_slabs in ((wq, 2), (wk, 2), (wv, 4), (wg, 4)):
                for n in range(n_slabs):
                    units.load(view(units.slot(), DC, BANK),
                               w[0].rearrange("(p c) n -> p c n", c=DC)[:, :, n * BANK:(n + 1) * BANK])
            for n in range(4):
                units.load(view(units.slot(), 4, D), wo_r[0].rearrange("(c p) n -> p c n", p=P)[:, 4 * n:4 * n + 4, :])

        def ret_pe(pe, units):
            norm_done(pe, 2)
            for n in range(4):
                units.wait()
                w = view(units.slot(), DC, BANK)
                if n >= 2:
                    pe.wait_ge(E("rt_ro"), 2 * (n - 1))
                for m in range(4):
                    dst = bank(4 + 2 * (n % 2) + m // 2)[:, (m % 2) * S:(m % 2 + 1) * S]
                    last = rows_of(dst, lambda c: w[:, c, m * P:(m + 1) * P], lambda c: xnT[:, c, :], DC)
                    if m % 2:
                        last.then_inc(E("rt_qk_ps"), 1)
                units.n += 1
                pe.wait_ge(E("rt_qk_ps"), 2 * (n + 1))
                pe.sem_inc(used, 1)
            for h in range(RET_HEADS):
                units.wait()
                w = view(units.slot(), DC, BANK)
                if h >= 2:
                    pe.wait_ge(E("rt_v"), NT * (h - 1))
                for t in range(NT):
                    last = rows_of(bank(2 * (h % 2) + t), tile_of(xnT, t), lambda c: w[:, c, :], DC)
                    last.then_inc(E("rt_v_ps"), 1)
                units.n += 1
                pe.wait_ge(E("rt_v_ps"), NT * (h + 1))
                pe.sem_inc(used, 1)
            pe.wait_ge(E("rt_ro"), 8)
            pe.wait_ge(E("rt_v"), 8)

            def turn_back(h):
                pe.wait_ge(E("rt_y"), NT * (h + 1))
                for t in range(NT):
                    for c in range(4):
                        last = nc.tensor.transpose(bank(6 + c // 2)[:, (c % 2) * S + t * P:(c % 2) * S + (t + 1) * P],
                                                   r_y[:, t, c * P:(c + 1) * P], ident)
                last.then_inc(E("rt_yT_ps"), 1)

            for h in range(RET_HEADS):
                if h >= 1:
                    pe.wait_ge(E("rt_dec"), h)
                    pe.wait_ge(E("rt_on"), NT * h)
                for cc in range(2):
                    nc.tensor.matmul(bank(2)[:, 0:S], rkT[:, 2 * h + cc, 0:P], rqT[:, 2 * h + cc, :],
                                     start=(cc == 0), stop=(cc == 1))
                for cc in range(2):
                    last = nc.tensor.matmul(bank(2)[:, S:SC], rkT[:, 2 * h + cc, P:S], rqT[:, 2 * h + cc, P:S],
                                            start=(cc == 0), stop=(cc == 1))
                last.then_inc(E("rt_s_ps"), 1)
                units.wait()
                w = view(units.slot(), DC, BANK)
                if h >= 1:
                    pe.wait_ge(E("rt_sg"), NT * h)
                for t in range(NT):
                    last = rows_of(bank(t), tile_of(xnT, t), lambda c: w[:, c, :], DC)
                    last.then_inc(E("rt_g_ps"), 1)
                units.n += 1
                pe.wait_ge(E("rt_g_ps"), NT * (h + 1))
                pe.sem_inc(used, 1)
                pe.wait_ge(E("rt_dec"), h + 1)
                v = [rv[:, t, h * RET_V:(h + 1) * RET_V] for t in range(NT)]
                nc.tensor.matmul(bank(4), r_sT[:, 0:P], v[0], start=True, stop=True).then_inc(E("rt_o_ps"), 1)
                nc.tensor.matmul(bank(5), r_sT[:, P:S], v[0], start=True, stop=False)
                nc.tensor.matmul(bank(5), r_sT[:, S:SC], v[1], start=False, stop=True).then_inc(E("rt_o_ps"), 1)
                if h >= 1:
                    pe.wait_ge(E("rt_yT"), 2 * h - 2) if h >= 2 else None
                    turn_back(h - 1)
            pe.wait_ge(E("rt_yT"), 2 * RET_HEADS - 2)
            turn_back(RET_HEADS - 1)
            pe.wait_ge(E("rt_sg"), NT * RET_HEADS)
            pe.wait_ge(E("rt_yT"), 2 * RET_HEADS)
            for n in range(4):
                units.wait()
                w = view(units.slot(), 4, D)
                for m in range(2):
                    for t in range(NT):
                        for c in range(4):
                            last = nc.tensor.matmul(bank(m * NT + t), ryT[:, 4 * n + c, t * P:(t + 1) * P],
                                                    w[:, c, m * BANK:(m + 1) * BANK], start=(n == 0 and c == 0),
                                                    stop=(n == 3 and c == 3), skip_group_check=True)
                        if n == 3:
                            last.then_inc(E("ret_ps"), 1)
                if n < 3:
                    last.then_inc(E("rt_wo"), 1)
                    pe.wait_ge(E("rt_wo"), n + 1)
                else:
                    pe.wait_ge(E("ret_ps"), 4)
                units.n += 1
                pe.sem_inc(used, 1)

        def ret_act(act, link):
            for h in range(RET_HEADS):
                for t in range(NT):
                    act.wait_ge(E("rt_v_ps"), NT * h + t + 1)
                    nc.scalar.activation(rv[:, t, h * RET_V:(h + 1) * RET_V], bank(2 * (h % 2) + t),
                                         ACT.Copy).then_inc(E("rt_v"), 1)
            act.wait_ge(E("rt_ro"), 8)
            for h in range(RET_HEADS):
                for t in range(NT):
                    act.wait_ge(E("rt_g_ps"), NT * h + t + 1)
                    if h >= 1:
                        act.wait_ge(E("rt_y"), NT * (h - 1) + t + 1)
                    nc.scalar.activation(r_sg[:, t, :], bank(t), ACT.Silu).then_inc(E("rt_sg"), 1)

        def ret_pool(pool):
            for h in range(RET_HEADS):
                pool.wait_ge(E("rt_var"), h + 1)
                nc.gpsimd.tensor_tensor(grstd, gvar, C("minus_half")[:, 0:NT], ALU.pow).then_inc(E("rt_rstd"), 1)

        def ret_dve(dve, link):
            for i in range(8):
                dve.wait_ge(E("rt_qk_ps"), i + 1)
                dst = (rqT if i < 4 else rkT)[:, 2 * (i % 4):2 * (i % 4) + 2, :]
                src = bank(4 + i % 4, 2, S)
                cos = C("r_cos").unsqueeze(1).to_broadcast([P, 2, S])
                sin = C("r_sin").unsqueeze(1).to_broadcast([P, 2, S])
                link(nc.vector.tensor_tensor(rope_c, src, cos, ALU.mult))
                link(nc.vector.tensor_tensor(rope_s, src, sin, ALU.mult))
                link(nc.vector.tensor_tensor(dst[:, 0, :], rope_c[:, 0, :], rope_s[:, 1, :], ALU.subtract))
                nc.vector.tensor_tensor(dst[:, 1, :], rope_s[:, 0, :], rope_c[:, 1, :], ALU.add).then_inc(E("rt_ro"), 1)
                dve.wait_ge(E("rt_ro"), i + 1)

            def turned_back(h):
                dve.wait_ge(E("rt_yT_ps"), h + 1)
                for b in range(2):
                    c = 4 * h + 2 * b
                    nc.vector.tensor_tensor(ryT[:, c:c + 2, :], bank(6 + b, 2, S),
                                            spread(G("gn")[:, c:c + 2], 2, S), ALU.mult).then_inc(E("rt_yT"), 1)

            dve.wait_ge(E("decay_in"), 16)
            for h in range(RET_HEADS):
                dve.wait_ge(E("rt_s_ps"), h + 1)
                if h >= 1:
                    dve.wait_ge(E("rt_o_ps"), NT * h)
                nc.vector.tensor_tensor(r_sT, bank(2)[:, 0:SC], decay[:, h, :], ALU.mult).then_inc(E("rt_dec"), 1)
                if h >= 1:
                    turned_back(h - 1)
                for t in range(NT):
                    dve.wait_ge(E("rt_o_ps"), NT * h + t + 1)
                    link(nc.vector.bn_stats(stats[:, t, :], bank(4 + t)))
                    link(nc.vector.bn_aggr(mv[:, t, :], stats[:, t, :]))
                nc.vector.tensor_scalar(gvar, mv[:, :, 1], EPS, None, ALU.add).then_inc(E("rt_var"), 1)
                dve.wait_ge(E("rt_rstd"), h + 1)
                if h >= 1:
                    dve.wait_ge(E("rt_yT_ps"), h)
                for t in range(NT):
                    nc.vector.tensor_scalar(r_y[:, t, :], bank(4 + t), mv[:, t, 0:1], grstd[:, t:t + 1], ALU.subtract,
                                            ALU.mult).then_inc(E("rt_on"), 1)
                for t in range(NT):
                    dve.wait_ge(E("rt_on"), NT * h + t + 1)
                    dve.wait_ge(E("rt_sg"), NT * h + t + 1)
                    nc.vector.tensor_tensor(r_y[:, t, :], r_y[:, t, :], r_sg[:, t, :], ALU.mult).then_inc(E("rt_y"), 1)
            turned_back(RET_HEADS - 1)
            residual_dve(dve, "ret")

        def pool_load(units):
            units.load(view(units.slot()[:, 0:2 * D], 8, 256), pool_w[0].rearrange("g (c p) n -> p (g c) n", p=P))

        def pool_dve(dve, link):
            norm_done(dve, 4)
            link(nc.vector.tensor_copy(pl_a, xnT))
            src, dst = pl_a, pl_b
            for i, back in enumerate((1, 2, 4, 8)):
                c = 2 * i
                link(nc.vector.tensor_tensor(dst[:, c:DC, back:S], src[:, c:DC, back:S], src[:, c:DC, 0:S - back], ALU.add))
                link(nc.vector.tensor_copy(dst[:, c:DC, 0:back], src[:, c:DC, 0:back]))
                count = C("inv_count")[:, i * S:(i + 1) * S].unsqueeze(1).to_broadcast([P, 2, S])
                link(nc.vector.tensor_tensor(pl_o[:, c:c + 2, :], dst[:, c:c + 2, :], count, ALU.mult))
                src, dst = dst, src
            nc.vector.tensor_tensor(pl_o, pl_o, xnT, ALU.subtract).then_inc(E("pl_pooled"), 1)
            dve.wait_ge(E("rows_in"), 16)
            for t in range(NT):
                dve.wait_ge(E("pl_ps"), t + 1)
                y = pl_y[:, t, :]
                link(nc.vector.tensor_tensor(view(y, 2, BANK), PS[:, 4 + 2 * t:6 + 2 * t, :], view(R("pool_b"), 2, BANK), ALU.add))
                link(nc.vector.tensor_tensor(y, y, R("pool_scale"), ALU.mult))
                nc.vector.tensor_tensor(x[:, t, :], x[:, t, :], y, ALU.add).then_inc(E("pool_add"), 1)

        def pool_pe(pe, units):
            units.wait()
            w = view(units.slot()[:, 0:2 * D], 8, 256)
            pe.wait_ge(E("pl_pooled"), 1)
            for t in range(NT):
                for g in range(4):
                    dst = bank(4 + 2 * t + g // 2)[:, (g % 2) * 256:(g % 2 + 1) * 256]
                    for c in range(2):
                        last = nc.tensor.matmul(dst, pl_o[:, 2 * g + c, t * P:(t + 1) * P], w[:, 2 * g + c, :],
                                                start=(c == 0), stop=(c == 1))
                last.then_inc(E("pl_ps"), 1)
            units.n += 1
            pe.wait_ge(E("pl_ps"), NT)
            pe.sem_inc(used, 1)

        def mla_load(units):
            units.load(view(units.slot()[:, 0:DC * 320], DC, 320), w_dkv.rearrange("(p c) n -> p c n", c=DC))
            units.load(view(units.slot()[:, 0:DC * Q_RANK], DC, Q_RANK), wq_down[0].rearrange("(p c) n -> p c n", c=DC))
            units.load(view(units.slot()[:, 0:2 * D], 2, D), w_uk.rearrange("(c p) n -> p c n", p=P))
            units.load(view(units.slot()[:, 0:2 * D], 2, D), w_uv.rearrange("(c p) n -> p c n", p=P))
            for n in range(2):
                units.load(view(units.slot()[:, 0:3 * 768], 3, 768),
                           wq_up[0].rearrange("(c p) n -> p c n", p=P)[:, :, n * 768:(n + 1) * 768])
            for n in range(2):
                units.load(view(units.slot(), DC, BANK),
                           wo_m[0].rearrange("(c p) n -> p c n", p=P)[:, :, n * BANK:(n + 1) * BANK])

        def mla_pe(pe, units):
            norm_done(pe, 6)
            units.wait()
            w = view(units.slot()[:, 0:DC * 320], DC, 320)
            for t in range(NT):
                last = rows_of(bank(4 + t)[:, 0:320], tile_of(xkvT, t), lambda c: w[:, c, :], DC)
                last.then_inc(E("ml_kv_ps"), 1)
            units.n += 1
            pe.wait_ge(E("ml_kv_ps"), NT)
            pe.sem_inc(used, 1)
            units.wait()
            w = view(units.slot()[:, 0:DC * Q_RANK], DC, Q_RANK)
            for t in range(NT):
                last = rows_of(bank(6 + t)[:, 0:Q_RANK], tile_of(xnT, t), lambda c: w[:, c, :], DC)
                last.then_inc(E("ml_q_ps"), 1)
            units.n += 1
            pe.wait_ge(E("ml_q_ps"), NT)
            pe.sem_inc(used, 1)
            pe.wait_ge(E("ml_lat"), 2 * NT)
            pe.wait_ge(E("ml_kr"), 1)
            for t in range(NT):
                for c in range(2):
                    nc.tensor.transpose(bank(0)[:, c * S + t * P:c * S + (t + 1) * P], ckv[:, t, c * P:(c + 1) * P], ident)
                for c in range(2):
                    nc.tensor.transpose(bank(1)[:, c * S + t * P:c * S + (t + 1) * P], cq[:, t, c * P:(c + 1) * P], ident)
                nc.tensor.transpose(bank(2)[:, t * P:(t + 1) * P], cq[:, t, 2 * P:3 * P], ident)
                last = nc.tensor.transpose(bank(2)[:, S + t * P:S + (t + 1) * P], kr2[:, t, :], ident)
            last.then_inc(E("ml_t_ps"), 1)
            pe.wait_ge(E("ml_t"), 4)
            units.wait()
            w = view(units.slot()[:, 0:2 * D], 2, D)
            for h in range(M_HEADS):
                if h >= 2 and h % 2 == 0:
                    pe.wait_ge(E("ml_kn"), h // 2 - 1) if h >= 4 else None
                last = rows_of(bank((h // 2) % 2)[:, (h % 2) * S:(h % 2 + 1) * S],
                               lambda c: w[:, c, h * P:(h + 1) * P], lambda c: ckvT[:, c, :], 2)
                if h % 2:
                    last.then_inc(E("ml_kn_ps"), 1)
            units.n += 1
            pe.wait_ge(E("ml_kn_ps"), 4)
            pe.sem_inc(used, 1)
            units.wait()
            w = view(units.slot()[:, 0:2 * D], 2, D)
            for t in range(NT):
                for n in range(2):
                    last = rows_of(bank(4 + 2 * t + n), tile_of(ckvT, t), lambda c: w[:, c, n * BANK:(n + 1) * BANK], 2)
                    last.then_inc(E("ml_v_ps"), 1)
            units.n += 1
            pe.wait_ge(E("ml_v_ps"), 4)
            pe.sem_inc(used, 1)
            pe.wait_ge(E("ml_v"), 2)
            for n in range(2):
                units.wait()
                w = view(units.slot()[:, 0:3 * 768], 3, 768)
                wh = w.rearrange("p c (h d) -> p c h d", h=4)
                for t in range(NT):
                    last = rows_of(view(bank(4 + t)[:, n * S:(n + 1) * S], 4, M_ROPE), tile_of(cqT, t),
                                   lambda c: wh[:, c, :, M_NOPE:], 3)
                    if n == 1:
                        last.then_inc(E("ml_qr_ps"), 1)
                for j in range(4):
                    h = 4 * n + j
                    if j % 2 == 0:
                        if h >= 4:
                            pe.wait_ge(E("ml_qn"), h // 2 - 1)
                        else:
                            pe.wait_ge(E("ml_kn"), 3 + h // 2)
                    last = rows_of(bank((h // 2) % 2)[:, (h % 2) * S:(h % 2 + 1) * S],
                                   lambda c: wh[:, c, j, 0:M_NOPE], lambda c: cqT[:, c, :], 3)
                    if j % 2:
                        last.then_inc(E("ml_qn_ps"), 1)
                units.n += 1
                pe.wait_ge(E("ml_qn_ps"), 2 * (n + 1))
                pe.sem_inc(used, 1)
            pe.wait_ge(E("ml_qr"), NT)
            for j in range(4):
                for t in range(NT):
                    last = nc.tensor.transpose(bank(2 + j // 2)[:, (j % 2) * S + t * P:(j % 2) * S + (t + 1) * P],
                                               qr[:, t, j * P:(j + 1) * P], ident)
            last.then_inc(E("ml_qrT_ps"), 1)
            pe.wait_ge(E("ml_qrT"), 2)
            pe.wait_ge(E("ml_qn"), 4)
            pe.wait_ge(E("ml_v"), 4)

            def score(h, dst):
                a = M_ROPE * (h % 2)
                q2, k2 = qrT[a:a + M_ROPE, h // 2, :], krT[a:a + M_ROPE, :]
                nc.tensor.matmul(dst[:, 0:P], qnT[:, h, 0:P], knT[:, h, 0:P], start=True, stop=False)
                nc.tensor.matmul(dst[:, 0:P], q2[:, 0:P], k2[:, 0:P], start=False, stop=True)
                nc.tensor.matmul(dst[:, P:SC], qnT[:, h, P:S], knT[:, h, :], start=True, stop=False)
                return nc.tensor.matmul(dst[:, P:SC], q2[:, P:S], k2, start=False, stop=True)

            heads_pe(pe, "ml", score, lambda h, t: m_v[:, t, h * M_V:(h + 1) * M_V], lambda h: bank(4 + h % 2)[:, 0:S], 1)
            pe.wait_ge(E("at_o"), 4 + 8)
            for n in range(2):
                units.wait()
                w = view(units.slot(), DC, BANK)
                for t in range(NT):
                    last = rows_of(bank(n * NT + t), tile_of(m_aT, t), lambda c: w[:, c, :], DC)
                    last.then_inc(E("mla_ps"), 1)
                units.n += 1
                pe.wait_ge(E("mla_ps"), NT * (n + 1))
                pe.sem_inc(used, 1)

        def mla_act(act, link):
            for t in range(NT):
                act.wait_ge(E("ml_kv_ps"), t + 1)
                nc.scalar.activation(ckv[:, t, :], bank(4 + t)[:, 0:320], ACT.Copy).then_inc(E("ml_c"), 1)
            for t in range(NT):
                act.wait_ge(E("ml_q_ps"), t + 1)
                nc.scalar.activation(cq[:, t, :], bank(6 + t)[:, 0:Q_RANK], ACT.Copy).then_inc(E("ml_c"), 1)
            act.wait_ge(E("ml_t_ps"), 1)
            for c in range(2):
                last = nc.scalar.activation(ckvT[:, c, :], bank(0)[:, c * S:(c + 1) * S], ACT.Copy, scale=G("kv_norm")[:, c:c + 1])
            last.then_inc(E("ml_t"), 1)
            for c in range(3):
                last = nc.scalar.activation(cqT[:, c, :], bank(1 + c // 2)[:, (c % 2) * S:(c % 2 + 1) * S], ACT.Copy,
                                            scale=G("q_norm")[:, c:c + 1])
            last.then_inc(E("ml_t"), 2)
            nc.scalar.activation(krT, bank(2)[:, S:2 * S], ACT.Copy).then_inc(E("ml_t"), 1)
            for j in range(4):
                act.wait_ge(E("ml_kn_ps"), j + 1)
                nc.scalar.activation(knT[:, 2 * j:2 * j + 2, :], bank(j % 2, 2, S), ACT.Copy).then_inc(E("ml_kn"), 1)
            for j in range(4):
                act.wait_ge(E("ml_qn_ps"), j + 1)
                nc.scalar.activation(qnT[:, 2 * j:2 * j + 2, :], bank(j % 2, 2, S), ACT.Copy).then_inc(E("ml_qn"), 1)
            heads_act(act, link, "ml", lambda h: m_aT[:, h, :], lambda h: bank(4 + h % 2)[:, 0:S], 1)

        def mla_pool(pool):
            pool.wait_ge(E("ml_ms"), 1)
            nc.gpsimd.tensor_tensor(hrstd[:, :, 0:2], hms[:, :, 0:2],
                                    view(C("minus_half")[:, 0:4], NT, 2), ALU.pow).then_inc(E("ml_rstd"), 1)

        def turn_rows(link, dst, src, t, n):
            half = M_ROPE // 2
            cos = view(C("m_cos"), NT, half)[:, t, :].unsqueeze(1).to_broadcast([P, n, half])
            sin = view(C("m_sin"), NT, half)[:, t, :].unsqueeze(1).to_broadcast([P, n, half])
            a, b = src[:, :, 0:half], src[:, :, half:]
            u = view(m_scor.rearrange("p a b -> p (a b)")[:, 0:n * half], n, half)
            link(nc.vector.tensor_tensor(dst[:, :, 0:half], a, cos, ALU.mult))
            link(nc.vector.tensor_tensor(u, b, sin, ALU.mult))
            link(nc.vector.tensor_tensor(dst[:, :, 0:half], dst[:, :, 0:half], u, ALU.subtract))
            link(nc.vector.tensor_tensor(dst[:, :, half:], b, cos, ALU.mult))
            link(nc.vector.tensor_tensor(u, a, sin, ALU.mult))
            return nc.vector.tensor_tensor(dst[:, :, half:], dst[:, :, half:], u, ALU.add)

        def mla_dve(dve, link):
            dve.wait_ge(E("ml_c"), 2 * NT)
            for t in range(NT):
                link(nc.vector.tensor_tensor(m_sq[:, 0:KV_RANK], ckv[:, t, 0:KV_RANK], ckv[:, t, 0:KV_RANK], ALU.mult))
                link(nc.vector.tensor_reduce(hss[:, t, 0:1], m_sq[:, 0:KV_RANK], AX_X, ALU.add))
                link(nc.vector.tensor_tensor(m_sq, cq[:, t, :], cq[:, t, :], ALU.mult))
                link(nc.vector.tensor_reduce(hss[:, t, 1:2], m_sq, AX_X, ALU.add))
            link(nc.vector.tensor_scalar(hms[:, :, 0:1], hss[:, :, 0:1], 1.0 / KV_RANK, EPS, ALU.mult, ALU.add))
            nc.vector.tensor_scalar(hms[:, :, 1:2], hss[:, :, 1:2], 1.0 / Q_RANK, EPS, ALU.mult, ALU.add).then_inc(E("ml_ms"), 1)
            for t in range(NT):
                link(turn_rows(link, view(kr2[:, t, 0:M_ROPE], 1, M_ROPE), view(ckv[:, t, KV_RANK:], 1, M_ROPE), t, 1))
                last = nc.vector.tensor_copy(kr2[:, t, M_ROPE:], kr2[:, t, 0:M_ROPE])
                if t == 0:
                    link(last)
            last.then_inc(E("ml_kr"), 1)
            dve.wait_ge(E("ml_rstd"), 1)
            for t in range(NT):
                nc.vector.tensor_scalar(ckv[:, t, 0:KV_RANK], ckv[:, t, 0:KV_RANK], hrstd[:, t, 0:1], None,
                                        ALU.mult).then_inc(E("ml_lat"), 1)
                nc.vector.tensor_scalar(cq[:, t, :], cq[:, t, :], hrstd[:, t, 1:2], None, ALU.mult).then_inc(E("ml_lat"), 1)
            for t in range(NT):
                for n in range(2):
                    dve.wait_ge(E("ml_v_ps"), 2 * t + n + 1)
                    nc.vector.tensor_copy(m_v[:, t, n * BANK:(n + 1) * BANK], bank(4 + 2 * t + n)).then_inc(E("ml_v"), 1)
            for t in range(NT):
                dve.wait_ge(E("ml_qr_ps"), t + 1)
                turn_rows(link, view(qr[:, t, :], M_HEADS, M_ROPE), bank(4 + t, M_HEADS, M_ROPE), t,
                          M_HEADS).then_inc(E("ml_qr"), 1)
                dve.wait_ge(E("ml_qr"), t + 1)
            dve.wait_ge(E("ml_qrT_ps"), 1)
            for b in range(2):
                nc.vector.tensor_copy(qrT[:, 2 * b:2 * b + 2, :], bank(2 + b, 2, S)).then_inc(E("ml_qrT"), 1)
            heads_dve(dve, link, "ml", C("mla_mask"), M_SCALE)
            residual_dve(dve, "mla")

        def route_pe(pe, l):
            norm_done(pe, 5 + 2 * l)
            w = view(G(f"route{l}"), DC, N_ROUTE)
            for t in range(NT):
                last = rows_of(bank(4)[:, t * N_ROUTE:(t + 1) * N_ROUTE], tile_of(xnT, t), lambda c: w[:, c, :], DC)
            last.then_inc(E("ro_ps"), 1)
            pe.wait_ge(E("ro_oh"), l + 1)
            r = bank(5)
            nc.tensor.matmul(r[:, 0:N_EXP], C("before"), ohs[:, 0, :], start=True, stop=True)
            nc.tensor.matmul(r[:, N_EXP:2 * N_EXP], C("ones"), ohs[:, 0, :], start=True, stop=False)
            nc.tensor.matmul(r[:, N_EXP:2 * N_EXP], C("before"), ohs[:, 1, :], start=False, stop=True)
            nc.tensor.matmul(r[:, 2 * N_EXP:3 * N_EXP], C("ones"), ohs[:, 0, :], start=True, stop=False)
            nc.tensor.matmul(r[:, 2 * N_EXP:3 * N_EXP], C("ones"), ohs[:, 1, :], start=False,
                             stop=True).then_inc(E("ro_rank_ps"), 1)

        def route_act(act, link, l):
            act.wait_ge(E("ro_gsh"), l + 1)
            nc.scalar.activation(gcand, gsh, ACT.Exp).then_inc(E("ro_gexp"), 1)
            act.wait_ge(E("ro_m2"), l + 1)
            nc.scalar.activation(r2, m2, ACT.Exp).then_inc(E("ro_r2"), 1)

        def route_dve(dve, link, l):
            v = nc.vector

            def first(dst, values, top, order, n, cand):
                link(v.tensor_tensor(dst, values, spread(top, NT, n), ALU.is_equal))
                link(v.tensor_tensor(cand, dst, order.unsqueeze(1).to_broadcast([P, NT, n]), ALU.mult))
                link(v.tensor_reduce(cmax, cand, AX_X, ALU.max))
                link(v.tensor_tensor(dst, cand, spread(cmax, NT, n), ALU.is_equal))

            dve.wait_ge(E("ro_ps"), l + 1)
            link(v.tensor_tensor(lg, bank(4, NT, N_ROUTE), G(f"route_b{l}").unsqueeze(1).to_broadcast([P, NT, N_ROUTE]), ALU.add))
            lg_g, lg_e = lg[:, :, 0:N_GROUPS], lg[:, :, N_GROUPS:]
            link(v.tensor_reduce(gmax, lg_g, AX_X, ALU.max))
            v.tensor_tensor(gsh, lg_g, spread(gmax, NT, N_GROUPS), ALU.subtract).then_inc(E("ro_gsh"), 1)
            dve.wait_ge(E("ro_gexp"), l + 1)
            link(v.tensor_reduce(gprob, gcand, AX_X, ALU.add))
            link(v.reciprocal(gprob, gprob))
            first(goh, lg_g, gmax, C("first4"), N_GROUPS, gcand)
            link(v.tensor_scalar(pen, goh, -NEG, NEG, ALU.mult, ALU.add))
            for t in range(NT):
                link(v.tensor_tensor(view(em[:, t, :], N_GROUPS, GROUP), view(lg_e[:, t, :], N_GROUPS, GROUP),
                                     spread(pen[:, t, :], N_GROUPS, GROUP), ALU.add))
            link(v.tensor_reduce(m1, em, AX_X, ALU.max))
            first(oh1, em, m1, C("first32"), N_EXP, er)
            link(v.scalar_tensor_tensor(em, oh1, FAR, em, ALU.mult, ALU.add))
            link(v.tensor_reduce(m2, em, AX_X, ALU.max))
            first(oh2, em, m2, C("first32"), N_EXP, er)
            v.tensor_tensor(ohs, oh1, oh2, ALU.add).then_inc(E("ro_oh"), 1)
            v.tensor_tensor(m2, m2, m1, ALU.subtract).then_inc(E("ro_m2"), 1)
            dve.wait_ge(E("ro_r2"), l + 1)
            link(v.tensor_scalar(rd2, r2, 1.0, None, ALU.add))
            link(v.reciprocal(rd2, rd2))
            link(v.tensor_tensor(gate[:, :, 0], gprob, rd2, ALU.mult))
            link(v.tensor_tensor(gate[:, :, 1], gate[:, :, 0], r2, ALU.mult))
            dve.wait_ge(E("ro_rank_ps"), l + 1)
            ranks = bank(5)[:, 0:NT * N_EXP].rearrange("p (t e) -> p t e", t=NT)
            link(v.tensor_reduce(count_max, bank(5)[:, 2 * N_EXP:3 * N_EXP], AX_X, ALU.max))
            v.tensor_copy(flag[:, l:l + 1], count_max).then_inc(E("ro_flag"), 1)
            link(v.tensor_tensor(ea, ranks, C("row_of").unsqueeze(1).to_broadcast([P, NT, N_EXP]), ALU.add))
            for k, oh in enumerate((oh1, oh2)):
                link(v.tensor_tensor(er, oh, ranks, ALU.mult))
                link(v.tensor_reduce(rank1, er, AX_X, ALU.add))
                link(v.tensor_tensor(er, oh, ea, ALU.mult))
                link(v.tensor_reduce(pos[:, :, k], er, AX_X, ALU.add))
                for r in range(1, ROUNDS):
                    link(v.tensor_scalar(over, rank1, float(r * CAP), float(CAP * (N_EXP - 1)), ALU.is_ge, ALU.mult))
                    link(v.tensor_tensor(pos[:, :, k], pos[:, :, k], over, ALU.add))

        PER_STEP = {"xg_ps": 2, "xg": 2, "wT_ps": 1, "wT": 1, "sel": 1, "gu_ps": 2, "sg": 1, "h": 1, "hT_ps": 1, "hT": 1,
                    "y_ps": 2, "y": 2, "c_ps": 4, "add": 4}
        AHEAD = ("xg_ps", "xg", "wT_ps", "wT", "sel")
        PRIMED = ("xg", "h", "c_ps", "add", "y_ps")

        class Pairs:

            def __init__(self, name, ahead, runs=0):
                self.name, self.ahead, self.runs = name, ahead, runs

            def __getitem__(self, what):
                return E(self.name + "_" + what)

            def wait(self, eng, what, value):
                before = self.runs * (PER_STEP[what] * (N_PAIRS + (what in AHEAD)) + (what in PRIMED))
                eng.wait_ge(self[what], before + (what in PRIMED) + value)

        def select(dve, link, q, b):
            v, col = nc.vector, C("column")
            for t in range(NT):
                link(v.tensor_scalar(wtmp, col, pos[:, t, 0:1], gate[:, t, 0:1], ALU.is_equal, ALU.mult))
                link(v.tensor_scalar(wsel[:, b, t, :], col, pos[:, t, 1:2], gate[:, t, 1:2], ALU.is_equal, ALU.mult))
                link(v.tensor_tensor(wsel[:, b, t, :], wsel[:, b, t, :], wtmp, ALU.add))
                link(v.tensor_scalar(wtmp, col, pos[:, t, 0:1], None, ALU.is_equal))
                link(v.scalar_tensor_tensor(sel[:, b, t, :], col, pos[:, t, 1:2], wtmp, ALU.is_equal, ALU.add))
            link(v.tensor_scalar(pos, pos, float(P), None, ALU.subtract))

        LINKS = 5 * NT + 1

        def gather_dve(dve, q, b, l, n, half):
            q.wait(dve, "xg_ps", 2 * n + half + 1)
            g = G(f"g_moe{l}")[:, 4 * half:4 * half + 4]
            nc.vector.tensor_tensor(view(xg[:, b, half * 4 * P:(half + 1) * 4 * P], 4, P), bank(4 + half, 4, P),
                                    spread(g, 4, P), ALU.mult).then_inc(q["xg"], 1)

        def gather_pe(b, q, half):
            for c in range(4 * half, 4 * half + 4):
                for t in range(NT):
                    last = nc.tensor.matmul(bank(4 + half)[:, (c % 4) * P:(c % 4 + 1) * P], hs[:, t, c:D:DC],
                                            sel[:, b, t, :], start=(t == 0), stop=(t == NT - 1))
            last.then_inc(q["xg_ps"], 1)

        def weights_pe(b, q):
            for t in range(NT):
                last = nc.tensor.transpose(bank(7)[:, t * P:(t + 1) * P], wsel[:, b, t, :], ident)
            last.then_inc(q["wT_ps"], 1)

        def pair_pe(pe, q, s, b, six, release):
            q.wait(pe, "xg", 2 * s + 2 * q.ahead)
            q.wait(pe, "add", 4 * s)
            for what in range(2):
                w = [view(six(2 * what + e), DC, BANK) for e in range(2)]
                for c in range(DC):
                    for e in range(2):
                        last = nc.tensor.matmul(PS[CAP * e:CAP * (e + 1), what, :],
                                                xg[:, b, c * P + CAP * e:c * P + CAP * (e + 1)], w[e][:, c, :],
                                                start=(c == 0), stop=(c == DC - 1))
                last.then_inc(q["gu_ps"], 1)
                release("gu_ps", 2 * s + what + 1)
            q.wait(pe, "sel", s + 1 + q.ahead)
            gather_pe(1 - b, q, 0)
            q.wait(pe, "h", s + 1)
            for c in range(4):
                last = nc.tensor.transpose(bank(6)[:, c * P:(c + 1) * P], e_h[:, c:D_EXP:4], ident)
            last.then_inc(q["hT_ps"], 1)
            weights_pe(1 - b, q)
            gather_pe(1 - b, q, 1)
            w = [view(six(4 + e), 4, D) for e in range(2)]
            q.wait(pe, "hT", s + 1)
            for n in range(2):
                for c in range(4):
                    for e in range(2):
                        last = nc.tensor.matmul(PS[CAP * e:CAP * (e + 1), 2 + n, :], e_hT[:, c, CAP * e:CAP * (e + 1)],
                                                w[e][:, c, n * BANK:(n + 1) * BANK], start=(c == 0), stop=(c == 3))
                last.then_inc(q["y_ps"], 1)
            release("y_ps", 2 * s + 2)
            q.wait(pe, "wT", s + 1 + q.ahead)
            q.wait(pe, "xg", 2 * s + 2 * q.ahead + 1)
            for n in range(2):
                q.wait(pe, "y", 2 * s + n + 1)
                for t in range(NT):
                    nc.tensor.matmul(bank(COMBINE[n][t]), wT[:, b, t * P:(t + 1) * P], e_y[:, n * BANK:(n + 1) * BANK],
                                     start=True, stop=True).then_inc(q["c_ps"], 1)

        COMBINE = ((2, 7), (3, 4))

        def pair_act(act, q, s, b):
            q.wait(act, "gu_ps", 2 * s + 1)
            q.wait(act, "h", s)
            nc.scalar.activation(sg, bank(0), ACT.Silu).then_inc(q["sg"], 1)
            q.wait(act, "wT_ps", s + q.ahead + 1)
            q.wait(act, "c_ps", 4 * s)
            nc.scalar.activation(wT[:, 1 - b, :], bank(7)[:, 0:S], ACT.Copy).then_inc(q["wT"], 1)
            for n in range(2):
                q.wait(act, "y_ps", 2 * s + n + 1)
                nc.scalar.activation(e_y[:, n * BANK:(n + 1) * BANK], bank(2 + n), ACT.Copy).then_inc(q["y"], 1)

        def pair_dve(dve, link, q, s, b, l):
            select(dve, link, q, 1 - b)
            dve.sem_inc(q["sel"], 1)
            q.wait(dve, "gu_ps", 2 * s + 2)
            q.wait(dve, "sg", s + 1)
            nc.vector.tensor_tensor(e_h, sg, bank(1), ALU.mult).then_inc(q["h"], 1)
            gather_dve(dve, q, 1 - b, l, s + q.ahead, 0)
            q.wait(dve, "hT_ps", s + 1)
            nc.vector.tensor_copy(e_hT, bank(6, 4, P)).then_inc(q["hT"], 1)
            gather_dve(dve, q, 1 - b, l, s + q.ahead, 1)
            for n in range(2):
                for t in range(NT):
                    q.wait(dve, "c_ps", 4 * s + 2 * n + t + 1)
                    v = x[:, t, n * BANK:(n + 1) * BANK]
                    nc.vector.tensor_tensor(v, v, bank(COMBINE[n][t]), ALU.add).then_inc(q["add"], 1)

        def expert_source(l, e, k):
            src = (e_gate, e_up, e_down)[k // 2]
            rows = src[l].rearrange("e (p c) n -> e p (c n)", p=P)
            return rows[bass.ds(e + k % 2, 1)].rearrange("e p n -> p (e n)")

        TURNS = N_PAIRS // 2

        def moe_load(sp, units, l):
            with sp.Fori(0, TURNS) as turn:
                units.loop(turn, 2 * SLOTS)
                for j in range(2):
                    for k in range(6):
                        units.load(units.slot(), expert_source(l, turn * 4 + 2 * j, k))
                units.done(TURNS)
            more = Pairs(f"more{l}", 0)
            sp.wait_ge(E("ro_flag"), l + 1)
            count = sp.value_load(flag[0:1, l:l + 1])
            with sp.If(count > CAP):
                sp.wait_ge(used, units.n)
                with sp.Fori(0, ROUNDS - 1) as r:
                    with sp.Fori(0, N_PAIRS) as e:
                        sp.wait_ge(more["y_ps"], (r * N_PAIRS + e) * 2 + 1)
                        for k in range(6):
                            sp.dma_start(ring[:, k, :], expert_source(l, e * 2, k)).then_inc(more["loaded"], 16)
                sp.wait_ge(more["loaded"], 96 * (ROUNDS - 1) * N_PAIRS)
                sp.wait_ge(more["y_ps"], (ROUNDS - 1) * N_PAIRS * 2 + 1)

        def moe_pe(pe, units, l):
            q = Pairs("moe", 1, l)
            for what in ("c_ps", "y_ps"):
                pe.sem_inc(q[what], 1)
            route_pe(pe, l)
            q.wait(pe, "sel", 1)
            gather_pe(0, q, 0)
            weights_pe(0, q)
            gather_pe(0, q, 1)
            q.wait(pe, "wT", 1)
            with pe.Fori(0, TURNS) as turn:
                units.loop(turn, 2 * SLOTS)
                for j in range(2):
                    def six(k):
                        units.wait()
                        got = units.slot()
                        units.n += 1
                        return got

                    def release(done, value):
                        q.wait(pe, done, value)
                        pe.sem_inc(used, 2)

                    pair_pe(pe, q, turn * 2 + j, j, six, release)
                units.done(TURNS)
            more = Pairs(f"more{l}", 0)
            pe.wait_ge(E("ro_flag"), l + 1)
            count = pe.value_load(flag[0:1, l:l + 1])
            with pe.If(count > CAP):
                q.wait(pe, "xg", 2 * N_PAIRS + 2)
                q.wait(pe, "wT", N_PAIRS + 1)
                q.wait(pe, "add", 4 * N_PAIRS)
                for what in ("c_ps", "y_ps"):
                    pe.sem_inc(more[what], 1)
                with pe.Fori(0, (ROUNDS - 1) * N_PAIRS // 2) as turn:
                    for j in range(2):
                        s = turn * 2 + j
                        pe.wait_ge(more["loaded"], 96 * s + 96)
                        pair_pe(pe, more, s, j, lambda k: ring[:, k, :], lambda done, value: None)

        def moe_act(act, link, l):
            q = Pairs("moe", 1, l)
            route_act(act, link, l)
            q.wait(act, "wT_ps", 1)
            nc.scalar.activation(wT[:, 0, :], bank(7)[:, 0:S], ACT.Copy).then_inc(q["wT"], 1)
            with act.Fori(0, TURNS) as turn:
                for j in range(2):
                    pair_act(act, q, turn * 2 + j, j)
            more = Pairs(f"more{l}", 0)
            act.wait_ge(E("ro_flag"), l + 1)
            count = act.value_load(flag[0:1, l:l + 1])
            with act.If(count > CAP):
                q.wait(act, "c_ps", 4 * N_PAIRS)
                q.wait(act, "h", N_PAIRS)
                with act.Fori(0, (ROUNDS - 1) * N_PAIRS // 2) as turn:
                    for j in range(2):
                        pair_act(act, more, turn * 2 + j, j)
                more.wait(act, "add", 4 * (ROUNDS - 1) * N_PAIRS)

        def moe_dve(dve, link, l, links):
            q = Pairs("moe", 1, l)
            for what in ("xg", "h", "add"):
                dve.sem_inc(q[what], 1)
            route_dve(dve, link, l)
            select(dve, link, q, 0)
            dve.sem_inc(q["sel"], 1)
            gather_dve(dve, q, 0, l, 0, 0)
            gather_dve(dve, q, 0, l, 0, 1)
            with dve.Fori(0, TURNS) as turn:
                link.loop(turn, 2 * LINKS)
                for j in range(2):
                    pair_dve(dve, link, q, turn * 2 + j, j, l)
                link.done(TURNS)
            more = Pairs(f"more{l}", 0)
            dve.wait_ge(E("ro_flag"), l + 1)
            count = dve.value_load(flag[0:1, l:l + 1])
            with dve.If(count > CAP):
                link2 = Chain(dve, more["links"])
                for what in ("xg", "h", "add"):
                    dve.sem_inc(more[what], 1)
                with dve.Fori(0, (ROUNDS - 1) * N_PAIRS // 2) as turn:
                    link2.loop(turn, 2 * LINKS)
                    for j in range(2):
                        pair_dve(dve, link2, more, turn * 2 + j, j, l)
                    link2.done((ROUNDS - 1) * N_PAIRS // 2)

        EVEN_UNITS, RET_UNITS = 8, 16

        block = ctx.enter_context(nc.Block())

        @block.sync
        def _(sp):
            units = Units(sp)
            sp.dma_start(x[:, 0, :], x_in[0, 0:P, :]).then_inc(E("x_in"), 16)
            sp.dma_start(x[:, 1, :], x_in[0, P:S, :]).then_inc(E("x_in"), 16)
            even_load(units)
            ffn_load(sp, units, 0)
            ret_load(units)
            ffn_load(sp, units, 1)
            pool_load(units)
            moe_load(sp, units, 0)
            mla_load(units)
            moe_load(sp, units, 1)
            for t in range(NT):
                sp.wait_ge(E("out_rdy"), t + 1)
                sp.dma_start(out[0, t * P:(t + 1) * P, :], hs[:, t, :]).then_inc(E("out_sent"), 16)
            sp.wait_ge(E("out_sent"), 16 * NT)

        @block.tensor
        def _(pe):
            units = Units(pe)
            pe.wait_ge(E("const_in"), 16)
            pe.wait_ge(E("param_in"), 16)
            norm_pe(pe, 0)
            even_pe(pe, units)
            norm_pe(pe, 1)
            ffn_pe(pe, units, 0)
            norm_pe(pe, 2)
            ret_pe(pe, units)
            norm_pe(pe, 3)
            ffn_pe(pe, units, 1)
            norm_pe(pe, 4)
            pool_pe(pe, units)
            norm_pe(pe, 5)
            moe_pe(pe, units, 0)
            norm_pe(pe, 6)
            mla_pe(pe, units)
            norm_pe(pe, 7)
            moe_pe(pe, units, 1)

        @block.scalar
        def _(act):
            act.dma_start(cst[:, :], const).then_inc(E("const_in"), 16)
            act.dma_start(par[:, :], params).then_inc(E("param_in"), 16)
            link = Chain(act, E("act_link"))
            units = Units(act)
            units.n = EVEN_UNITS
            act.wait_ge(E("const_in"), 16)
            act.wait_ge(E("param_in"), 16)
            norm_act(act, link, 0)
            even_act(act, link)
            norm_act(act, link, 1)
            ffn_act(act, units, 0)
            act.wait_ge(E("ffn_ps"), 2 * NT)
            act.dma_start(late[:, 0:RET_HEADS * SC], decay_in).then_inc(E("decay_in"), 16)
            norm_act(act, link, 2)
            ret_act(act, link)
            norm_act(act, link, 3)
            units.n += RET_UNITS
            ffn_act(act, units, 1)
            act.wait_ge(E("ffn_ps"), 4 * NT)
            act.dma_start(late[:, :], rows).then_inc(E("rows_in"), 16)
            norm_act(act, link, 4)
            norm_act(act, link, 5)
            moe_act(act, link, 0)
            norm_act(act, link, 6)
            mla_act(act, link)
            norm_act(act, link, 7)
            moe_act(act, link, 1)
            norm_act(act, link, 8)

        @block.gpsimd
        def _(pool):
            pool.wait_ge(E("const_in"), 16)
            norm_pool(pool, 0)
            even_pool(pool)
            norm_pool(pool, 1)
            norm_pool(pool, 2)
            ret_pool(pool)
            for k in range(3, 7):
                norm_pool(pool, k)
            mla_pool(pool)
            norm_pool(pool, 7)
            norm_pool(pool, 8)

        @block.vector
        def _(dve):
            link = Chain(dve, E("dve_link"))
            units = Units(dve)
            units.n = EVEN_UNITS
            dve.wait_ge(E("const_in"), 16)
            dve.wait_ge(E("param_in"), 16)
            norm_dve(dve, link, 0)
            even_dve(dve, link)
            norm_dve(dve, link, 1)
            ffn_dve(dve, units, link, 0)
            norm_dve(dve, link, 2)
            ret_dve(dve, link)
            norm_dve(dve, link, 3)
            units.n += RET_UNITS
            ffn_dve(dve, units, link, 1)
            norm_dve(dve, link, 4)
            pool_dve(dve, link)
            norm_dve(dve, link, 5)
            moe_dve(dve, link, 0, None)
            norm_dve(dve, link, 6)
            mla_dve(dve, link)
            norm_dve(dve, link, 7)
            moe_dve(dve, link, 1, None)
            dve.wait_ge(E("n_rstd"), 9)
            dve.wait_ge(E("rows_in"), 16)
            for t in range(NT):
                nc.vector.scalar_tensor_tensor(hs[:, t, :], x[:, t, :], rstd[:, t:t + 1], R("final"), ALU.mult,
                                               ALU.mult).then_inc(E("out_rdy"), 1)


def kernel(**inputs):
    import concourse.bacc as bacc
    from concourse.bass_utils import run_bass_kernel_spmd

    a = {k: np.ascontiguousarray(v) for k, v in inputs.items()}
    table, _, decay = shape_constants()

    def striped(v):
        return v.reshape(P, -1)

    def stacked(v):
        return v.reshape(-1, P).T

    def router(l):
        w = np.concatenate([a["router_group_w_2"][l], a["router_expert_w_2"][l]], axis=1)
        return w.reshape(P, DC * N_ROUTE)

    def router_bias(l):
        b = np.concatenate([a["router_group_b_2"][l], a["router_expert_b_2"][l]])
        return np.broadcast_to(b[None, :], (P, N_ROUTE))

    def ffn_taps(l):
        w = a["ffn_conv_w"][l].reshape(3, 2, N_SLABS, 2, P)
        return w.transpose(4, 2, 1, 3, 0).reshape(P, -1)

    by_name = {
        "g_even": striped(a["even_norm"][0]), "g_ffn0": striped(a["ffn_norm"][0]), "g_odd": striped(a["odd_norm"][0]),
        "g_ffn1": striped(a["ffn_norm"][1]), "g_pool": stacked(a["pool_norm_2"][0]), "g_moe0": striped(a["ffn_norm_2"][0]),
        "g_kvin": striped(a["kv_in_norm_2"]), "g_attn": striped(a["attn_norm_2"][0]), "g_moe1": striped(a["ffn_norm_2"][1]),
        "q_gain": np.concatenate([a["even_q_gain"][0]] * 2)[:, None],
        "k_gain": np.concatenate([a["even_k_gain"][0]] * 2)[:, None],
        "sconv": a["even_sconv_w"][0].reshape(3, 4, P).transpose(2, 1, 0).reshape(P, -1),
        "gn": stacked(a["ret_gn_gain"][0].reshape(-1)), "conv0": ffn_taps(0), "conv1": ffn_taps(1),
        "kv_norm": stacked(a["kv_norm_2"]), "q_norm": stacked(a["q_norm_2"][0]),
        "route0": router(0), "route1": router(1), "route_b0": router_bias(0), "route_b1": router_bias(1),
    }
    params = np.ascontiguousarray(np.concatenate([by_name[n] for n, _ in PARAMS], axis=1))
    row_values = {"pool_b": a["pool_b_2"][0].reshape(-1), "pool_scale": a["pool_scale_2"][0], "final": a["final_norm_2"]}
    rows = np.ascontiguousarray(np.broadcast_to(np.concatenate([row_values[n] for n, _ in ROWS])[None, :], (P, 3 * D)))
    arrays = {"const": np.ascontiguousarray(table), "decay": decay, "params": params, "rows": rows}
    for name in ("x", "even_w_in", "even_w_out", "ret_wq", "ret_wk", "ret_wv", "ret_wg", "ret_wo", "ffn_w_up", "ffn_w_down",
                 "pool_w_2", "w_dkv_2", "w_uk_2", "w_uv_2", "wq_down_2", "wq_up_2", "wo_2", "w_gate_2", "w_up_2", "w_down_2"):
        arrays[name] = a[name]
    nc = bacc.Bacc("TRN2", target_bir_lowering=False, num_devices=1)
    args = [nc.dram_tensor(k, v.shape, F32, kind="ExternalInput").ap() for k, v in arrays.items()]
    args.append(nc.dram_tensor("out", (1, S, D), F32, kind="ExternalOutput").ap())
    build(nc, *args)
    r = run_bass_kernel_spmd(nc, [arrays], core_ids=[0])
    return r.results[0]["out"]
```

```python
from contextlib import ExitStack

import numpy as np

import concourse.bass as bass
from concourse import mybir

F32 = mybir.dt.float32
F32R = mybir.dt.float32r
I32 = mybir.dt.int32
ALU = mybir.AluOpType
ACT = mybir.ActivationFunctionType
AX_X = mybir.AxisListType.X

P = 128
S = 256
NT = S // P
D = 1024
DC = D // P
BANK = 512
EPS = 1e-6
NEG = -1.0e30
FAR = -2.0e30

A_HEADS, A_DIM = 8, 64
DILATED = ((128, 1), (512, 4), (2048, 16))
RET_HEADS, RET_K, RET_V = 4, 256, 512
RET_CHUNK = 128
ROPE_BASE = 10000.0
D_FF = 2816
SLAB = 256
N_SLABS = D_FF // SLAB
POOL_WINDOWS = (2, 4, 8, 16)
M_HEADS, M_NOPE, M_ROPE, M_V = 8, 128, 64, 128
Q_RANK, KV_RANK = 384, 256
M_CHUNK = 64
M_SCALE = 1.0 / float(np.sqrt(M_NOPE + M_ROPE))
N_GROUPS, GROUP = 4, 8
N_EXP = N_GROUPS * GROUP
N_ROUTE = N_GROUPS + N_EXP
D_EXP = 512
CAP = 64
N_PAIRS = N_EXP // 2
ROUNDS = S // CAP
SLOTS = 6
UNIT = 4096
SC = P + S


def shape_constants():
    f = np.float32
    q = np.arange(S)[:, None]
    k = np.arange(S)[None, :]
    diff = q - k
    times = np.zeros((S, S))
    for window, dil in DILATED:
        times += (diff >= 0) & (diff % dil == 0) & (diff // dil <= window // dil)
    dil_mask = np.where(times > 0, np.log(np.maximum(times, 1)), NEG)
    mla_mask = np.where(k // M_CHUNK <= q // M_CHUNK, 0.0, NEG)

    def by_tile(m):
        return np.concatenate([m[0:P, 0:P], m[P:S, 0:S]], axis=1)

    log_g = np.log1p(-(2.0 ** (-5.0 - np.arange(RET_HEADS))))
    decay = []
    for h in range(RET_HEADS):
        m = np.where(diff >= 0, np.exp(log_g[h] * np.maximum(diff, 0)), 0.0).T * RET_K ** -0.5
        decay.append(np.concatenate([m[0:P, 0:S], m[P:S, P:S]], axis=1))
    half = RET_K // 2
    inv = f(ROPE_BASE) ** (-np.arange(half, dtype=f) / f(half))
    ang = (np.arange(S, dtype=f)[:, None] * inv[None, :]).astype(f).T
    half = M_ROPE // 2
    inv = f(ROPE_BASE) ** (-np.arange(half, dtype=f) / f(half))
    ang2 = (np.arange(S, dtype=f)[:, None] * inv[None, :]).astype(f).reshape(NT, P, half).transpose(1, 0, 2)
    band = []
    for window in POOL_WINDOWS:
        m = ((diff >= 0) & (diff < window)) / np.minimum(q + 1, window) - np.eye(S)
        band.append(np.concatenate([m.T[0:P, 0:S], m.T[P:S, P:S]], axis=1))
    row = np.arange(P)
    parts = {
        "ident": np.eye(P),
        "minus_half": np.full((P, NT * 2 * A_HEADS), -0.5),
        "dil_mask": by_tile(dil_mask),
        "mla_mask": by_tile(mla_mask),
        "r_cos": np.cos(ang), "r_sin": np.sin(ang),
        "m_cos": np.cos(ang2).reshape(P, -1), "m_sin": np.sin(ang2).reshape(P, -1),
        "before": (row[:, None] < row[None, :]) * 1.0,
        "ones": np.ones((P, P)),
        "column": np.tile(row[None, :], (P, 1)),
        "first4": np.tile(N_GROUPS - np.arange(N_GROUPS)[None, :], (P, 1)),
        "first32": np.tile(N_EXP - np.arange(N_EXP)[None, :], (P, 1)),
        "row_of": np.tile(CAP * np.arange(N_EXP)[None, :], (P, 1)),
    }
    where, at = {}, 0
    for name, a in parts.items():
        where[name] = (at, at + a.shape[1])
        at += a.shape[1]
    table = np.concatenate([a.astype(f) for a in parts.values()], axis=1)
    return table, where, np.concatenate(decay, axis=1).astype(f), np.concatenate(band, axis=1).astype(f)


PARAMS = [
    ("g_even", DC), ("g_ffn0", DC), ("g_odd", DC), ("g_ffn1", DC), ("g_pool", DC),
    ("g_moe0", DC), ("g_kvin", DC), ("g_attn", DC), ("g_moe1", DC),
    ("q_gain", 1), ("k_gain", 1), ("sconv", 12), ("gn", 16), ("conv0", 132), ("conv1", 132),
    ("kv_norm", 2), ("q_norm", 3), ("route0", DC * N_ROUTE), ("route1", DC * N_ROUTE),
    ("route_b0", N_ROUTE), ("route_b1", N_ROUTE),
]
ROWS = [("pool_b", D), ("pool_scale", D), ("final", D)]


def places(table):
    where, at = {}, 0
    for name, n in table:
        where[name] = (at, at + n)
        at += n
    return where, at


class Chain:

    def __init__(self, eng, sem):
        self.eng, self.sem, self.n, self.turn, self.per, self.base = eng, sem, 0, None, 0, 0

    def __call__(self, ins):
        self.n += 1
        ins.then_inc(self.sem, 1)
        self.eng.wait_ge(self.sem, self.n if self.turn is None else self.turn * self.per + self.n)

    def loop(self, turn, per):
        self.turn, self.per, self.base = turn, per, self.n

    def done(self, turns):
        assert self.n - self.base == self.per, (self.n - self.base, self.per)
        self.turn, self.n = None, self.base + self.per * turns


def build(nc, const, decay_in, band_in, params, rows, x_in, w_in, w_out, wq, wk, wv, wg, wo_r, w_up, w_down, pool_w, w_dkv, w_uk, w_uv,
          wq_down, wq_up, wo_m, e_gate, e_up, e_down, out):
    const_at = shape_constants()[1]
    param_at, n_params = places(PARAMS)
    row_at, n_rows = places(ROWS)
    n_const = const.shape[1]
    ctx = ExitStack()
    with ctx:
        def sb(name, shape, dt=F32):
            return ctx.enter_context(nc.sbuf_tensor(name, shape, dt))

        def sem(name):
            return ctx.enter_context(nc.semaphore(name))

        ring = sb("ring", [P, SLOTS, UNIT])
        cst = sb("cst", [P, n_const])
        par = sb("par", [P, n_params])
        x = sb("x_res", [P, NT, D])
        hs = sb("hs", [P, NT, D])
        small = sb("small", [P, 512])
        flag = sb("flag", [P, 2], I32)
        WORK = 14720
        late_at = -(-nc.sbuf_base // 32) * 32
        xnT_at = late_at + 4 * n_rows
        work_at = xnT_at + 4 * DC * S

        def placed(name, shape, at, dt=F32):
            return nc.alloc_sbuf_tensor_at(name, shape, dt, offset=at)

        late = placed("late", [P, n_rows], late_at)
        xnT = placed("xnT", [P, DC, S], xnT_at)[:, :, :]
        work = placed("work", [P, WORK], work_at)
        PS = ctx.enter_context(nc.psum_tensor("PS", [P, 8, BANK], F32))

        def C(name):
            a, b = const_at[name]
            return cst[:, a:b]

        def G(name):
            a, b = param_at[name]
            return par[:, a:b]

        def R(name):
            a, b = row_at[name]
            return late[:, a:b]

        def view(v, *shape):
            if len(shape) == 2:
                return v.rearrange("p (a b) -> p a b", b=shape[1])
            if len(shape) == 3:
                return v.rearrange("p (a b c) -> p a b c", b=shape[1], c=shape[2])
            return v

        def area(at, *shape):
            n = int(np.prod(shape))
            assert at + n <= WORK
            return view(work[:, at:at + n], *shape)

        def scratch(at, *shape):
            return view(small[:, at:at + int(np.prod(shape))], *shape)

        def bank(b, *shape):
            return view(PS[:, b, 0:int(np.prod(shape))], *shape) if shape else PS[:, b, :]

        def spread(col, *shape):
            return col.unsqueeze(len(col.shape)).to_broadcast([P, *shape])

        ident = C("ident")
        decay = view(late[:, 0:RET_HEADS * SC], RET_HEADS, SC)

        ss, ms, rstd = scratch(0, NT), scratch(2, NT), scratch(4, NT)
        hss, hms, hrstd = scratch(8, NT, 16), scratch(40, NT, 16), scratch(72, NT, 16)
        nmx, den, rden = scratch(104, 2, 2), scratch(108, 2, 2), scratch(112, 2, 2)
        gqk = scratch(116, 1)
        stats, mv, gvar, grstd = scratch(120, NT, 6), scratch(132, NT, 2), scratch(136, NT), scratch(138, NT)
        gmax, gprob, cmax, m1, m2 = (scratch(144 + 2 * i, NT) for i in range(5))
        r2, rd2, count_max = scratch(154, NT), scratch(156, NT), scratch(158, 1)
        pos, gate = scratch(160, NT, 2), scratch(164, NT, 2)
        rank1, rank2, over = scratch(168, NT), scratch(170, NT), scratch(172, NT)
        gsh, goh, gcand, pen = (scratch(176 + 8 * i, NT, N_GROUPS) for i in range(4))
        lg = scratch(208, NT, N_ROUTE)

        qk_t = area(0, NT, 2 * BANK)
        v_t = area(2048, NT, BANK)
        qT, kT = area(3072, 4, S), area(4096, 4, S)
        gbT, gcT, zT = area(5120, 4, S), area(6144, 4, S), area(7168, 4, S)
        mixT = area(8192, 8, S)
        scor, prob, probT = area(10240, 2, SC), area(11008, 2, SC), area(11776, 2, SC)
        sq = area(12544, D)
        convt = area(13568, 4, S)
        f_u = area(0, 4, S)
        f_cw = area(1024, 12)
        f_at = work_at + 4 * 1040
        HALF = UNIT // 2
        f_w = [[placed(f"f_w_{kind}_{part}", [P, HALF], f_at + 4 * HALF * (2 * i + j), F32R)
                for j, part in enumerate(("hi", "lo"))] for i, kind in enumerate(("gate", "value", "down"))]
        f_h = [placed(f"f_h_{part}", [P, 2, S], f_at + 4 * (6 * HALF + j * 2 * S), F32R) for j, part in enumerate(("hi", "lo"))]
        f_x = [placed("f_x_hi", [P, DC, S], xnT_at, F32R), placed("f_x_lo", [P, DC, S], late_at, F32R)]
        assert 1040 + 6 * HALF + 4 * S <= WORK and DC * S <= n_rows
        rqT, rkT = area(0, DC, S), area(2048, DC, S)
        rv = area(4096, NT, RET_HEADS * RET_V)
        ryT = area(8192, 16, S)
        rope_c, rope_s = area(12288, 2, S), area(12800, 2, S)
        r_sg = area(12288, NT, RET_V)
        r_sT = area(13312, SC)
        r_y = area(13696, NT, RET_V)
        pl_band = area(0, 4, SC)
        pl_y = area(1536, NT, D)
        pl_bs = area(3584, D)
        xkvT = area(0, DC, S)
        qnT = area(0, M_HEADS, S)
        ckv, cq, kr2 = area(2048, NT, 320), area(2688, NT, Q_RANK), area(3456, NT, P)
        m_aT = area(2048, M_HEADS, S)
        ckvT, cqT = area(4096, 2, S), area(4608, 3, S)
        knT = area(5376, M_HEADS, S)
        m_v = area(7424, NT, M_HEADS * M_V)
        qr, qrT = area(9472, NT, BANK), area(10496, 4, S)
        m_scor, m_prob, m_probT = area(11520, 2, SC), area(12288, 2, SC), area(13056, 2, SC)
        m_sq, krT = area(13824, Q_RANK), area(14208, S)
        sel, wsel, wtmp = area(0, 2, NT, P), area(512, 2, NT, P), area(1024, P)
        wT, xg = area(1152, 2, S), area(1664, 2, DC * P)
        sg, e_h, e_hT, e_y = area(3712, BANK), area(4224, BANK), area(4736, 4, P), area(5248, D)
        oh1, oh2, ohs, em, er, ea = (area(6400 + 64 * i, NT, N_EXP) for i in range(6))

        named = {}

        def E(name):
            if name not in named:
                named[name] = sem(name)
            return named[name]

        loaded = [sem(f"loaded{i}") for i in range(SLOTS)]
        used = sem("used")

        class Units:

            def __init__(self, eng):
                self.eng, self.n, self.turn, self.per, self.base = eng, 0, None, 0, 0

            def slot(self, k=0):
                return ring[:, (self.n + k) % SLOTS, :]

            def wait(self, k=0):
                u = self.n + k
                there = 16 * (u // SLOTS + 1)
                if self.turn is not None:
                    there = self.turn * (16 * self.per // SLOTS) + there
                self.eng.wait_ge(loaded[u % SLOTS], there)

            def load(self, dst, src):
                u = self.n
                if u >= SLOTS:
                    done = u - SLOTS + 1
                    self.eng.wait_ge(used, done if self.turn is None else self.turn * self.per + done)
                self.eng.dma_start(dst, src).then_inc(loaded[u % SLOTS], 16)
                self.n += 1

            def loop(self, turn, per):
                self.turn, self.per, self.base = turn, per, self.n

            def done(self, turns):
                assert self.n - self.base == self.per
                self.turn, self.n = None, self.base + self.per * turns

        NORMS = ["g_even", "g_ffn0", "g_odd", "g_ffn1", "g_pool", "g_moe0", "g_attn", "g_moe1"]
        X_DONE = [("x_in", (16 * NT, 16 * NT)), ("even_add", (3, 4)), ("ffn_add", (3, 4)), ("ret_add", (3, 4)),
                  ("ffn_add", (7, 8)), ("pool_add", (1, 2)), ("moe_add", (4 * N_PAIRS, 4 * N_PAIRS + 1)),
                  ("mla_add", (3, 4)), ("moe_add", (8 * N_PAIRS + 1, 8 * N_PAIRS + 2))]
        SPLIT = (1, 3)
        A_BANKS = [sum(4 if i in SPLIT or i == 6 else 2 for i in range(k)) for k in range(9)]
        D_BANKS = A_BANKS

        def chunk(t, k, c):
            if NORMS[k] == "g_pool":
                return t[:, c * P:(c + 1) * P]
            return t[:, c:D:DC]

        def norm_act(act, link, k):
            name, values = X_DONE[k]
            for t in range(NT):
                act.wait_ge(E(name), values[t])
                link(nc.scalar.activation(hs[:, t, :], x[:, t, :], ACT.Square, accum_out=ss[:, t:t + 1]))
                nc.scalar.activation(ms[:, t:t + 1], ss[:, t:t + 1], ACT.Copy, bias=EPS,
                                     scale=1.0 / D).then_inc(E("n_ms"), 1)
            if k == 8:
                return
            g = G(NORMS[k])
            for b in (range(4) if k == 6 or k in SPLIT else [1, 3]):
                act.wait_ge(E("n_tr"), 4 * k + b + 1)
                if k == 6:
                    act.wait_ge(E("n_xd"), D_BANKS[k] + b + 1)
                for j in range(2):
                    c = 2 * b + j
                    last = nc.scalar.activation((f_x[0] if k in SPLIT else xnT)[:, c, :], bank(b)[:, j * S:(j + 1) * S], ACT.Copy,
                                                scale=g[:, c:c + 1])
                last.then_inc(E("n_xa"), 1)

        def norm_pool(pool, k):
            for t in range(NT):
                pool.wait_ge(E("n_ms"), NT * k + t + 1)
                nc.gpsimd.tensor_tensor(rstd[:, t:t + 1], ms[:, t:t + 1], C("minus_half")[:, 0:1],
                                        ALU.pow).then_inc(E("n_rstd"), 1)

        def norm_dve(dve, link, k):
            for t in range(NT):
                dve.wait_ge(E("n_rstd"), NT * k + t + 1)
                nc.vector.tensor_scalar(hs[:, t, :], x[:, t, :], rstd[:, t:t + 1], None,
                                        ALU.mult).then_inc(E("n_hs"), 1)
            g = G("g_kvin" if k == 6 else NORMS[k])
            if k in SPLIT:
                for b in range(4):
                    dve.wait_ge(E("n_xa"), A_BANKS[k] + b + 1)
                    for c in (2 * b, 2 * b + 1):
                        last = nc.vector.scalar_tensor_tensor(
                            f_x[1][:, c, :], bank(b)[:, (c % 2) * S:(c % 2 + 1) * S], g[:, c:c + 1],
                            f_x[0][:, c, :].bitcast(F32), ALU.mult, ALU.subtract)
                    last.then_inc(E("n_xd"), 1)
                return
            dst = xkvT if k == 6 else xnT
            for b in ([0, 2] if k != 6 else range(4)):
                dve.wait_ge(E("n_tr"), 4 * k + b + 1)
                nc.vector.tensor_tensor(dst[:, 2 * b:2 * b + 2, :], bank(b, 2, S),
                                        spread(g[:, 2 * b:2 * b + 2], 2, S), ALU.mult).then_inc(E("n_xd"), 1)

        def norm_pe(pe, k):
            if NORMS[k] == "g_pool":
                pe.wait_ge(E("n_hs"), NT * (k + 1))
                pe.wait_ge(E("band_in"), 16)
                for c in range(DC):
                    dst = bank(c // 2)[:, (c % 2) * S:(c % 2 + 1) * S]
                    nc.tensor.matmul(dst, chunk(hs[:, 0, :], k, c), pl_band[:, c // 2, 0:S], start=True, stop=False)
                    last = nc.tensor.matmul(dst[:, P:S], chunk(hs[:, 1, :], k, c), pl_band[:, c // 2, S:SC],
                                            start=False, stop=True)
                    if c % 2:
                        last.then_inc(E("n_tr"), 1)
                return
            for t in range(NT):
                pe.wait_ge(E("n_hs"), NT * k + t + 1)
                for c in range(DC):
                    last = nc.tensor.transpose(bank(c // 2)[:, (c % 2) * S + t * P:(c % 2) * S + (t + 1) * P],
                                               chunk(hs[:, t, :], k, c), ident)
                    if t == NT - 1 and c % 2:
                        last.then_inc(E("n_tr"), 1)

        def norm_done(eng, k):
            eng.wait_ge(E("n_xa"), A_BANKS[k + 1])
            eng.wait_ge(E("n_xd"), D_BANKS[k + 1])

        def rows_of(dst, lhs, w, n):
            for c in range(n):
                last = nc.tensor.matmul(dst, lhs(c), w(c), start=(c == 0), stop=(c == n - 1))
            return last

        def tile_of(src, t):
            return lambda c: src[:, c, t * P:(t + 1) * P]

        def first_head(kind):
            return 8 if kind == "ml" else 0

        HEAD_BANKS = {"ev": (4, 6), "ml": (0, 2)}

        def heads_pe(pe, kind, score, value, out_of, per_evac, between=None):
            s_bank, t_bank = HEAD_BANKS[kind]
            for i in range(8 + 2):
                if i < 8:
                    h = i
                    if h >= 2:
                        pe.wait_ge(E("at_sc"), first_head(kind) + h - 1)
                    last = score(h, bank(s_bank + h % 2))
                    last.then_inc(E("at_s_ps"), 1)
                if between:
                    between(i)
                if 1 <= i <= 8:
                    h = i - 1
                    pe.wait_ge(E("at_p"), first_head(kind) + h + 1)
                    if h >= 2:
                        pe.wait_ge(E("at_pT"), first_head(kind) + h - 1)
                    p = (prob if kind == "ev" else m_prob)[:, h % 2, :]
                    for j in range(3):
                        last = nc.tensor.transpose(bank(t_bank + h % 2)[:, j * P:(j + 1) * P], p[:, j * P:(j + 1) * P], ident)
                    last.then_inc(E("at_t_ps"), 1)
                if i >= 2:
                    h = i - 2
                    pe.wait_ge(E("at_pT"), first_head(kind) + h + 1)
                    n = h // per_evac
                    if h % per_evac == 0 and n >= 2:
                        pe.wait_ge(E("at_o"), (4 if kind == "ml" else 0) + n - 1)
                    pT = (probT if kind == "ev" else m_probT)[:, h % 2, :]
                    dst = out_of(h)
                    nc.tensor.matmul(dst, value(h, 0), pT[:, 0:S], start=True, stop=False)
                    nc.tensor.matmul(dst[:, P:S], value(h, 1), pT[:, S:SC], start=False,
                                     stop=True).then_inc(E("at_o_ps"), 1)

        def heads_dve(dve, link, kind, mask, scale, between=None):
            s_bank, t_bank = HEAD_BANKS[kind]
            sc, pr = (scor, prob) if kind == "ev" else (m_scor, m_prob)
            for i in range(8 + 1):
                if i < 8:
                    h = i
                    dve.wait_ge(E("at_s_ps"), first_head(kind) + h + 1)
                    if h >= 2:
                        dve.wait_ge(E("at_e"), first_head(kind) + h - 1)
                    nc.vector.scalar_tensor_tensor(sc[:, h % 2, :], bank(s_bank + h % 2)[:, 0:SC], scale, mask, ALU.mult,
                                                   ALU.add).then_inc(E("at_sc"), 1)
                    dve.wait_ge(E("at_sc"), first_head(kind) + h + 1)
                    nc.vector.tensor_reduce(nmx[:, h % 2, 0:1], sc[:, h % 2, 0:P], AX_X, ALU.max, negate=True)
                    nc.vector.tensor_reduce(nmx[:, h % 2, 1:2], sc[:, h % 2, P:SC], AX_X, ALU.max,
                                            negate=True).then_inc(E("at_m"), 1)
                if i >= 1:
                    h = i - 1
                    dve.wait_ge(E("at_e"), first_head(kind) + h + 1)
                    link(nc.vector.reciprocal(rden[:, h % 2, :], den[:, h % 2, :]))
                    p = pr[:, h % 2, :]
                    nc.vector.tensor_scalar(p[:, 0:P], p[:, 0:P], rden[:, h % 2, 0:1], None, ALU.mult)
                    nc.vector.tensor_scalar(p[:, P:SC], p[:, P:SC], rden[:, h % 2, 1:2], None,
                                            ALU.mult).then_inc(E("at_p"), 1)
                if between:
                    between(i)

        def heads_act(act, link, kind, dst_of, src_of, per_evac, between=None):
            s_bank, t_bank = HEAD_BANKS[kind]
            sc, pr, prT = (scor, prob, probT) if kind == "ev" else (m_scor, m_prob, m_probT)
            for i in range(8 + 2):
                if i < 8:
                    h = i
                    act.wait_ge(E("at_m"), first_head(kind) + h + 1)
                    if h >= 2:
                        act.wait_ge(E("at_t_ps"), first_head(kind) + h - 1)
                    nc.scalar.activation(pr[:, h % 2, 0:P], sc[:, h % 2, 0:P], ACT.Exp, bias=nmx[:, h % 2, 0:1],
                                         accum_out=den[:, h % 2, 0:1])
                    nc.scalar.activation(pr[:, h % 2, P:SC], sc[:, h % 2, P:SC], ACT.Exp, bias=nmx[:, h % 2, 1:2],
                                         accum_out=den[:, h % 2, 1:2]).then_inc(E("at_e"), 1)
                if 1 <= i <= 8:
                    h = i - 1
                    act.wait_ge(E("at_t_ps"), first_head(kind) + h + 1)
                    if h >= 2:
                        act.wait_ge(E("at_o_ps"), first_head(kind) + h - 1)
                    nc.scalar.activation(prT[:, h % 2, :], bank(t_bank + h % 2)[:, 0:SC],
                                         ACT.Copy).then_inc(E("at_pT"), 1)
                if i >= 2 and (i - 2) % per_evac == per_evac - 1:
                    h = i - 2
                    act.wait_ge(E("at_o_ps"), first_head(kind) + h + 1)
                    nc.scalar.activation(dst_of(h // per_evac), src_of(h // per_evac),
                                         ACT.Copy).then_inc(E("at_o"), 1)
                if between:
                    between(i)

        def residual_dve(dve, name, before=0, units=0):
            for n in range(2):
                for t in range(NT):
                    dve.wait_ge(E(name + "_ps"), before + n * NT + t + 1)
                    if t == NT - 1 and n >= 2 - units:
                        dve.sem_inc(used, 1)
                    v = x[:, t, n * BANK:(n + 1) * BANK]
                    nc.vector.tensor_tensor(v, v, bank(n * NT + t), ALU.add).then_inc(E(name + "_add"), 1)

        W_IN_ORDER = (0, 1, 2, 4, 5, 3)
        CONV_FIRST, CONV_PAIRS = 2, 6

        def even_load(units):
            for n in W_IN_ORDER:
                units.load(view(units.slot(), DC, BANK),
                           w_in[0].rearrange("(p c) n -> p c n", c=DC)[:, :, n * BANK:(n + 1) * BANK])
            for n in range(2):
                units.load(view(units.slot(), DC, BANK),
                           w_out[0].rearrange("(c p) n -> p c n", p=P)[:, :, n * BANK:(n + 1) * BANK])

        def even_pe(pe, units):
            norm_done(pe, 0)
            for n in range(3):
                units.wait()
                w = view(units.slot(), DC, BANK)
                for t in range(NT):
                    i = n * NT + t
                    if i >= 4:
                        pe.wait_ge(E("ev_qkv"), i - 3)
                    last = rows_of(bank(4 + i % 4), tile_of(xnT, t), lambda c: w[:, c, :], DC)
                    last.then_inc(E("ev_qkv_ps"), 1)
                units.n += 1

            def conv_chunk(i):
                pair, m = i // 2, i % 4
                if i % 4 == 0:
                    units.wait()
                if i % 2 == 0 and pair >= 2:
                    pe.wait_ge(*((E("ev_gc"), pair - 1) if pair < 4 else (E("ev_z"), pair - 3)))
                w = view(units.slot(), DC, BANK)
                last = rows_of(bank(pair % 2)[:, (i % 2) * S:(i % 2 + 1) * S], lambda c: w[:, c, m * P:(m + 1) * P],
                               lambda c: xnT[:, c, :], DC)
                if i % 2:
                    last.then_inc(E("ev_cv_ps"), 1)
                if i % 4 == 3:
                    units.n += 1

            for i in range(2 * CONV_FIRST):
                conv_chunk(i)
            pe.wait_ge(E("ev_qkv"), 6)
            pe.wait_ge(E("ev_qkn"), NT)
            for half in range(2):
                for j in range(4):
                    for t in range(NT):
                        last = nc.tensor.transpose(
                            bank(4 + 2 * half + j // 2)[:, (j % 2) * S + t * P:(j % 2) * S + (t + 1) * P],
                            qk_t[:, t, half * BANK + j * P:half * BANK + (j + 1) * P], ident)
                last.then_inc(E("ev_qkT_ps"), 1)
            conv_chunk(2 * CONV_FIRST)
            pe.wait_ge(E("ev_qT"), 2)
            pe.wait_ge(E("ev_kT"), 2)

            def score(h, dst):
                a = A_DIM * (h % 2)
                q, k = qT[a:a + A_DIM, h // 2, :], kT[a:a + A_DIM, h // 2, :]
                nc.tensor.matmul(dst[:, 0:P], q[:, 0:P], k[:, 0:P], start=True, stop=True)
                return nc.tensor.matmul(dst[:, P:SC], q[:, P:S], k, start=True, stop=True)

            def between(i):
                if 2 * CONV_FIRST + 1 + i < 2 * CONV_PAIRS:
                    conv_chunk(2 * CONV_FIRST + 1 + i)

            heads_pe(pe, "ev", score, lambda h, t: v_t[:, t, h * A_DIM:(h + 1) * A_DIM],
                     lambda h: PS[A_DIM * (h % 2):A_DIM * (h % 2) + A_DIM, 2 + (h // 2) % 2, 0:S], 2, between)
            pe.wait_ge(E("at_o"), 4)
            pe.wait_ge(E("ev_conv"), 1)
            for n in range(2):
                units.wait()
                w = view(units.slot(), DC, BANK)
                for t in range(NT):
                    last = rows_of(bank(n * NT + t), tile_of(mixT, t), lambda c: w[:, c, :], DC)
                    last.then_inc(E("even_ps"), 1)
                units.n += 1

        def even_act(act, link):
            for i in range(6):
                n, t = i // NT, i % NT
                act.wait_ge(E("ev_qkv_ps"), i + 1)
                if t == NT - 1:
                    act.sem_inc(used, 1)
                dst = v_t[:, t, :] if n == 2 else qk_t[:, t, n * BANK:(n + 1) * BANK]
                nc.scalar.activation(dst, bank(4 + i % 4), ACT.Copy).then_inc(E("ev_qkv"), 1)
            for b in range(2):
                act.wait_ge(E("ev_cv_ps"), b + 1)
                if b == 1:
                    act.sem_inc(used, 1)
                nc.scalar.activation(gcT[:, 2 * b:2 * b + 2, :], bank(b, 2, S), ACT.Copy).then_inc(E("ev_gc"), 1)
            act.wait_ge(E("ev_gqk"), 1)
            act.wait_ge(E("ev_qkT_ps"), 1)
            for b in range(2):
                nc.scalar.activation(qT[:, 2 * b:2 * b + 2, :], bank(4 + b, 2, S), ACT.Copy,
                                     scale=gqk).then_inc(E("ev_qT"), 1)

            def between(i):
                if i == 4:
                    act.wait_ge(E("ev_cv_ps"), 4)
                    act.sem_inc(used, 1)
                if i in (6, 8):
                    b = (i - 6) // 2
                    act.wait_ge(E("ev_cv_ps"), 5 + b)
                    if b == 1:
                        act.sem_inc(used, 1)
                    nc.scalar.activation(gbT[:, 2 * b:2 * b + 2, :], bank(b, 2, S), ACT.Copy).then_inc(E("ev_gb"), 1)

            heads_act(act, link, "ev", lambda j: mixT[:, j, :], lambda j: bank(2 + j % 2)[:, 0:S], 2, between)

        def even_pool(pool):
            pool.wait_ge(E("ev_hms"), 1)
            nc.gpsimd.tensor_tensor(hrstd, hms, view(C("minus_half"), NT, 2 * A_HEADS), ALU.pow).then_inc(E("ev_hr"), 1)

        def conv3(link, dst, src, taps, chunks):
            for j in chunks:
                link(nc.vector.tensor_scalar(dst[:, j, :], src[:, j, :], taps[:, 3 * j + 2:3 * j + 3], None, ALU.mult))
                for back in (1, 2):
                    link(nc.vector.scalar_tensor_tensor(dst[:, j, back:S], src[:, j, 0:S - back],
                                                        taps[:, 3 * j + 2 - back:3 * j + 3 - back],
                                                        dst[:, j, back:S], ALU.mult, ALU.add))

        def even_dve(dve, units, link):
            nc.vector.tensor_tensor(gqk, G("q_gain"), G("k_gain"), ALU.mult).then_inc(E("ev_gqk"), 1)
            dve.wait_ge(E("ev_qkv"), 4)
            for t in range(NT):
                link(nc.vector.tensor_tensor(sq, qk_t[:, t, :], qk_t[:, t, :], ALU.mult))
                link(nc.vector.tensor_reduce(hss[:, t, :], view(sq, 16, A_DIM), AX_X, ALU.add))
            nc.vector.tensor_scalar(hms, hss, 1.0 / A_DIM, EPS, ALU.mult, ALU.add).then_inc(E("ev_hms"), 1)
            dve.wait_ge(E("ev_hr"), 1)
            for t in range(NT):
                v = view(qk_t[:, t, :], 16, A_DIM)
                nc.vector.tensor_tensor(v, v, spread(hrstd[:, t, :], 16, A_DIM), ALU.mult).then_inc(E("ev_qkn"), 1)
            dve.wait_ge(E("ev_qkT_ps"), 2)
            for b in range(2):
                nc.vector.tensor_copy(kT[:, 2 * b:2 * b + 2, :], bank(6 + b, 2, S)).then_inc(E("ev_kT"), 1)

            def between(i):
                if i in (2, 4):
                    b = (i - 2) // 2
                    dve.wait_ge(E("ev_gc"), b + 1)
                    dve.wait_ge(E("ev_cv_ps"), 2 + b + 1)
                    nc.vector.tensor_tensor(zT[:, 2 * b:2 * b + 2, :], gcT[:, 2 * b:2 * b + 2, :], bank(b, 2, S),
                                            ALU.mult).then_inc(E("ev_z"), 1)
                    dve.wait_ge(E("ev_z"), b + 1)
                if 2 <= i < 6:
                    conv3(link, convt, zT, G("sconv"), [i - 2])

            heads_dve(dve, link, "ev", C("dil_mask"), A_DIM ** -0.5, between)
            dve.wait_ge(E("ev_gb"), 2)
            nc.vector.tensor_tensor(mixT[:, 4:8, :], convt, gbT, ALU.mult).then_inc(E("ev_conv"), 1)
            dve.wait_ge(E("ev_conv"), 1)
            ffn_first_dve(dve, units, 0, GATE)
            residual_dve(dve, "even", units=2)

        IN_LOOP = 3
        LOOP_TURNS = (N_SLABS - 2) // IN_LOOP
        assert 2 + IN_LOOP * LOOP_TURNS == N_SLABS
        GATE, VALUE, DOWN = range(3)

        def ffn_load(sp, units, l):
            up = w_up[l].rearrange("(p c) (g n) -> p c g n", c=DC, g=2)
            down = w_down[l].rearrange("(c p) n -> p c n", p=P)

            def load_up(at):
                units.load(view(units.slot(), DC, 2, SLAB), up[:, :, :, bass.ds(at, SLAB)])

            def load_down(at):
                units.load(view(units.slot()[:, 0:2 * D], 2, D), down[:, bass.ds(at, 2), :])

            load_up(0)
            load_up(SLAB)
            load_down(0)
            with sp.Fori(0, LOOP_TURNS) as turn:
                units.loop(turn, SLOTS)
                for j in range(IN_LOOP):
                    load_up(turn * (IN_LOOP * SLAB) + (2 + j) * SLAB)
                    load_down(turn * (IN_LOOP * 2) + (1 + j) * 2)
                units.done(LOOP_TURNS)
            load_down(2 * (N_SLABS - 1))

        SPLITS = 3 * N_SLABS

        def split_count(l, kind, s):
            if isinstance(s, int) and s == 0 and kind != DOWN:
                return l * SPLITS + 1 + kind
            if kind == DOWN:
                last = isinstance(s, int) and s == N_SLABS - 1
                return l * SPLITS + (SPLITS if last else 3 * s + 5)
            return l * SPLITS + 3 * s + kind

        def three_products(dst, lhs, rhs, start, stop):
            nc.tensor.matmul(dst, lhs[0], rhs[0], start=start, stop=False, skip_group_check=True)
            nc.tensor.matmul(dst, lhs[0], rhs[1], start=False, stop=False, skip_group_check=True)
            return nc.tensor.matmul(dst, lhs[1], rhs[0], start=False, stop=stop, skip_group_check=True)

        def ffn_pe(pe, units, l):
            s0 = l * N_SLABS

            def up(s):
                for kind in (GATE, VALUE):
                    pe.wait_ge(E("ffn_split"), split_count(l, kind, s))
                    w = [view(f_w[kind][i][:, :], DC, SLAB) for i in range(2)]
                    for j in range(2):
                        m = 2 * kind + j
                        if l > 0 or not isinstance(s, int) or s > 0:
                            pe.wait_ge(E("ffn_u"), 4 * (s0 + s))
                        for c in range(DC):
                            last = three_products(bank(4 + m)[:, 0:S], [v[:, c, j * P:(j + 1) * P] for v in w],
                                                  [v[:, c, :] for v in f_x], c == 0, c == DC - 1)
                        last.then_inc(E("ffn_u_ps"), 1)

            def down(s, start=False, stop=False):
                pe.wait_ge(E("ffn_split"), split_count(l, DOWN, s))
                pe.wait_ge(E("ffn_h"), 1 + s0 + s + 1)
                w = [view(f_w[GATE if stop else DOWN][i][:, :], 2, D) for i in range(2)]
                for n in range(2):
                    for t in range(NT):
                        for c in range(2):
                            last = three_products(bank(n * NT + t), [v[:, c, t * P:(t + 1) * P] for v in f_h],
                                                  [v[:, c, n * BANK:(n + 1) * BANK] for v in w],
                                                  start and c == 0, stop and c == 1)
                        if stop:
                            last.then_inc(E("ffn_ps"), 1)
                if not stop:
                    last.then_inc(E("ffn_d"), 1)

            if l == 0:
                pe.sem_inc(E("ffn_d"), 1)
            norm_done(pe, 1 + 2 * l)
            up(0)
            up(1)
            down(0, start=True)
            with pe.Fori(2, N_SLABS) as s:
                up(s)
                down(s - 1)
            down(N_SLABS - 1, stop=True)
            units.n += 2 * N_SLABS

        def raw_half(kind, slot):
            if kind == DOWN:
                return view(slot[:, 0:HALF], DC, SLAB)
            return view(slot, DC, 2, SLAB)[:, :, kind, :]

        def ffn_slabs(eng, units, slab, link=None, links=0):
            slab(0)
            with eng.Fori(0, LOOP_TURNS) as turn:
                units.loop(turn, SLOTS)
                if link:
                    link.loop(turn, IN_LOOP * links)
                for j in range(IN_LOOP):
                    slab(turn * IN_LOOP + (1 + j))
                units.done(LOOP_TURNS)
                if link:
                    link.done(LOOP_TURNS)
            slab(N_SLABS - 1)

        def round_half(kind, slot, into=None):
            nc.scalar.activation(view(f_w[kind if into is None else into][0][:, :], DC, SLAB), raw_half(kind, slot),
                                 ACT.Copy).then_inc(E("ffn_round"), 1)

        def ffn_first_act(act, units, l, kind):
            if kind == GATE:
                act.wait_ge(*((E("at_o_ps"), 8) if l == 0 else (E("rt_o_ps"), NT * RET_HEADS)))
                units.wait()
            else:
                act.wait_ge(E("even_ps" if l == 0 else "ret_ps"), 2 * NT)
            round_half(kind, units.slot())
            if kind == VALUE:
                units.n += 1

        def ffn_act(act, units, l):
            s0 = l * N_SLABS

            def newest(s, m):
                act.wait_ge(E("ffn_cw"), s0 + s + 1)
                act.wait_ge(E("ffn_u_ps"), 4 * (s0 + s) + m + 1)
                act.wait_ge(E("ffn_h"), 1 + s0 + s)
                nc.scalar.activation(f_u[:, m, :], bank(4 + m)[:, 0:S], ACT.Copy,
                                     scale=f_cw[:, 3 * m + 2:3 * m + 3]).then_inc(E("ffn_t"), 1)


            def slab(s):
                last = isinstance(s, int) and s == N_SLABS - 1
                for kind in (GATE, VALUE):
                    for j in range(2):
                        newest(s, 2 * kind + j)
                    if kind == GATE:
                        units.wait()
                    if not last:
                        round_half(kind, units.slot())
                    elif kind == GATE:
                        round_half(DOWN, units.slot(), into=GATE)
                        units.n += 1
                act.wait_ge(E("ffn_u"), 4 * (s0 + s) + 2)
                nc.scalar.activation(f_u[:, 0:2, :], f_u[:, 0:2, :], ACT.Silu).then_inc(E("ffn_g"), 1)
                if not last:
                    units.n += 1
                    units.wait()
                    act.wait_ge(E("ffn_d"), 1 + s0 - l + s)
                    round_half(DOWN, units.slot())
                    units.n += 1

            ffn_slabs(act, units, slab)

        def rest_half(dve, l, kind, s, slot, into=None):
            hi, lo = f_w[kind if into is None else into]
            dve.wait_ge(E("ffn_round"), split_count(l, kind, s))
            nc.vector.tensor_tensor(view(lo[:, :], DC, SLAB), raw_half(kind, slot), view(hi[:, :], DC, SLAB).bitcast(F32),
                                    ALU.subtract).then_inc(E("ffn_split"), 1)

        def give_back(dve, units, l, kind, s):
            dve.wait_ge(E("ffn_split"), split_count(l, kind, s))
            dve.sem_inc(used, 1)
            units.n += 1

        def ffn_first_dve(dve, units, l, kind):
            rest_half(dve, l, kind, 0, units.slot())
            if kind == VALUE:
                give_back(dve, units, l, VALUE, 0)

        FFN_LINKS = 7

        def ffn_dve(dve, units, link, l):
            s0 = l * N_SLABS
            taps = G(f"conv{l}")

            def conv(s, m):
                dve.wait_ge(E("ffn_t"), 4 * (s0 + s) + m + 1)
                u = bank(4 + m)
                link(nc.vector.scalar_tensor_tensor(f_u[:, m, 1:S], u[:, 0:S - 1], f_cw[:, 3 * m + 1:3 * m + 2],
                                                    f_u[:, m, 1:S], ALU.mult, ALU.add))
                nc.vector.scalar_tensor_tensor(f_u[:, m, 2:S], u[:, 0:S - 2], f_cw[:, 3 * m:3 * m + 1],
                                               f_u[:, m, 2:S], ALU.mult, ALU.add).then_inc(E("ffn_u"), 1)

            def slab(s):
                last = isinstance(s, int) and s == N_SLABS - 1
                link(nc.vector.tensor_copy(f_cw, taps[:, bass.ds(s * 12, 12)]))
                dve.sem_inc(E("ffn_cw"), 1)
                for kind in (GATE, VALUE):
                    for j in range(2):
                        conv(s, 2 * kind + j)
                    if not last:
                        rest_half(dve, l, kind, s + 1, units.slot())
                    elif kind == GATE:
                        rest_half(dve, l, DOWN, s, units.slot(), into=GATE)
                        give_back(dve, units, l, DOWN, s)
                if not last:
                    give_back(dve, units, l, VALUE, s + 1)
                dve.wait_ge(E("ffn_u"), 4 * (s0 + s) + 4)
                dve.wait_ge(E("ffn_g"), s0 + s + 1)
                link(nc.vector.tensor_tensor(f_u[:, 0:2, :], f_u[:, 0:2, :], f_u[:, 2:4, :], ALU.mult))
                dve.wait_ge(E("ffn_d"), 1 + s0 - l + s)
                link(nc.vector.tensor_copy(f_h[0][:, :, :], f_u[:, 0:2, :]))
                nc.vector.tensor_tensor(f_h[1][:, :, :], f_u[:, 0:2, :], f_h[0][:, :, :].bitcast(F32),
                                        ALU.subtract).then_inc(E("ffn_h"), 1)
                if not last:
                    rest_half(dve, l, DOWN, s, units.slot())
                    give_back(dve, units, l, DOWN, s)

            if l == 0:
                dve.sem_inc(E("ffn_h"), 1)
            ffn_slabs(dve, units, slab, link, FFN_LINKS)
            residual_dve(dve, "ffn", 4 * l)

        def ret_load(units):
            for w, n_slabs in ((wq, 2), (wk, 2), (wv, 4), (wg, 4)):
                for n in range(n_slabs):
                    units.load(view(units.slot(), DC, BANK),
                               w[0].rearrange("(p c) n -> p c n", c=DC)[:, :, n * BANK:(n + 1) * BANK])
            for n in range(4):
                units.load(view(units.slot(), 4, D), wo_r[0].rearrange("(c p) n -> p c n", p=P)[:, 4 * n:4 * n + 4, :])

        def ret_pe(pe, units):
            norm_done(pe, 2)
            for n in range(4):
                units.wait()
                w = view(units.slot(), DC, BANK)
                if n >= 2:
                    pe.wait_ge(E("rt_ro"), 2 * (n - 1))
                for m in range(4):
                    dst = bank(4 + 2 * (n % 2) + m // 2)[:, (m % 2) * S:(m % 2 + 1) * S]
                    last = rows_of(dst, lambda c: w[:, c, m * P:(m + 1) * P], lambda c: xnT[:, c, :], DC)
                    if m % 2:
                        last.then_inc(E("rt_qk_ps"), 1)
                units.n += 1
            for h in range(RET_HEADS):
                units.wait()
                w = view(units.slot(), DC, BANK)
                if h >= 2:
                    pe.wait_ge(E("rt_v"), NT * (h - 1))
                for t in range(NT):
                    last = rows_of(bank(2 * (h % 2) + t), tile_of(xnT, t), lambda c: w[:, c, :], DC)
                    last.then_inc(E("rt_v_ps"), 1)
                units.n += 1
            pe.wait_ge(E("rt_ro"), 8)
            pe.wait_ge(E("rt_v"), 8)

            def turn_back(h):
                pe.wait_ge(E("rt_y"), NT * (h + 1))
                for t in range(NT):
                    for c in range(4):
                        last = nc.tensor.transpose(bank(6 + c // 2)[:, (c % 2) * S + t * P:(c % 2) * S + (t + 1) * P],
                                                   r_y[:, t, c * P:(c + 1) * P], ident)
                last.then_inc(E("rt_yT_ps"), 1)

            for h in range(RET_HEADS):
                if h >= 1:
                    pe.wait_ge(E("rt_dec"), h)
                for cc in range(2):
                    nc.tensor.matmul(bank(2)[:, 0:S], rkT[:, 2 * h + cc, 0:P], rqT[:, 2 * h + cc, :],
                                     start=(cc == 0), stop=(cc == 1))
                for cc in range(2):
                    last = nc.tensor.matmul(bank(2)[:, S:SC], rkT[:, 2 * h + cc, P:S], rqT[:, 2 * h + cc, P:S],
                                            start=(cc == 0), stop=(cc == 1))
                last.then_inc(E("rt_s_ps"), 1)
                units.wait()
                w = view(units.slot(), DC, BANK)
                if h >= 1:
                    pe.wait_ge(E("rt_sg"), NT * h)
                for t in range(NT):
                    last = rows_of(bank(t), tile_of(xnT, t), lambda c: w[:, c, :], DC)
                    last.then_inc(E("rt_g_ps"), 1)
                units.n += 1
                if h >= 1:
                    if h >= 2:
                        pe.wait_ge(E("rt_yT"), 2 * h - 2)
                    turn_back(h - 1)
                    pe.wait_ge(E("rt_on"), NT * h)
                pe.wait_ge(E("rt_dec"), h + 1)
                v = [rv[:, t, h * RET_V:(h + 1) * RET_V] for t in range(NT)]
                nc.tensor.matmul(bank(4), r_sT[:, 0:P], v[0], start=True, stop=True).then_inc(E("rt_o_ps"), 1)
                nc.tensor.matmul(bank(5), r_sT[:, P:S], v[0], start=True, stop=False)
                nc.tensor.matmul(bank(5), r_sT[:, S:SC], v[1], start=False, stop=True).then_inc(E("rt_o_ps"), 1)
            pe.wait_ge(E("rt_sg"), NT * RET_HEADS)
            for n in range(4):
                if n == RET_HEADS - 1:
                    pe.wait_ge(E("rt_yT"), 2 * n)
                    turn_back(n)
                units.wait()
                pe.wait_ge(E("rt_yT"), 2 * (n + 1))
                w = view(units.slot(), 4, D)
                for m in range(2):
                    for t in range(NT):
                        for c in range(4):
                            last = nc.tensor.matmul(bank(m * NT + t), ryT[:, 4 * n + c, t * P:(t + 1) * P],
                                                    w[:, c, m * BANK:(m + 1) * BANK], start=(n == 0 and c == 0),
                                                    stop=(n == 3 and c == 3), skip_group_check=True)
                        if n == 3:
                            last.then_inc(E("ret_ps"), 1)
                units.n += 1
                if n < 3:
                    last.then_inc(E("rt_wo"), 1)
                    pe.wait_ge(E("rt_wo"), n + 1)
                    pe.sem_inc(used, 1)

        def ret_act(act, link):
            for n in range(4):
                act.wait_ge(E("rt_qk_ps"), 2 * (n + 1))
                act.sem_inc(used, 1)
            for h in range(RET_HEADS):
                for t in range(NT):
                    act.wait_ge(E("rt_v_ps"), NT * h + t + 1)
                    if t == NT - 1:
                        act.sem_inc(used, 1)
                    nc.scalar.activation(rv[:, t, h * RET_V:(h + 1) * RET_V], bank(2 * (h % 2) + t),
                                         ACT.Copy).then_inc(E("rt_v"), 1)
            act.wait_ge(E("rt_ro"), 8)
            for h in range(RET_HEADS):
                for t in range(NT):
                    act.wait_ge(E("rt_g_ps"), NT * h + t + 1)
                    if t == NT - 1:
                        act.sem_inc(used, 1)
                    if h >= 1:
                        act.wait_ge(E("rt_y"), NT * (h - 1) + t + 1)
                    nc.scalar.activation(r_sg[:, t, :], bank(t), ACT.Silu).then_inc(E("rt_sg"), 1)

        def ret_pool(pool):
            for h in range(RET_HEADS):
                pool.wait_ge(E("rt_var"), h + 1)
                nc.gpsimd.tensor_tensor(grstd, gvar, C("minus_half")[:, 0:NT], ALU.pow).then_inc(E("rt_rstd"), 1)

        def ret_dve(dve, units, link):
            for i in range(8):
                dve.wait_ge(E("rt_qk_ps"), i + 1)
                dst = (rqT if i < 4 else rkT)[:, 2 * (i % 4):2 * (i % 4) + 2, :]
                src = bank(4 + i % 4, 2, S)
                cos = C("r_cos").unsqueeze(1).to_broadcast([P, 2, S])
                sin = C("r_sin").unsqueeze(1).to_broadcast([P, 2, S])
                link(nc.vector.tensor_tensor(rope_c, src, cos, ALU.mult))
                link(nc.vector.tensor_tensor(rope_s, src, sin, ALU.mult))
                link(nc.vector.tensor_tensor(dst[:, 0, :], rope_c[:, 0, :], rope_s[:, 1, :], ALU.subtract))
                nc.vector.tensor_tensor(dst[:, 1, :], rope_s[:, 0, :], rope_c[:, 1, :], ALU.add).then_inc(E("rt_ro"), 1)
                dve.wait_ge(E("rt_ro"), i + 1)

            def turned_back(h):
                dve.wait_ge(E("rt_yT_ps"), h + 1)
                for b in range(2):
                    c = 4 * h + 2 * b
                    nc.vector.tensor_tensor(ryT[:, c:c + 2, :], bank(6 + b, 2, S),
                                            spread(G("gn")[:, c:c + 2], 2, S), ALU.mult).then_inc(E("rt_yT"), 1)

            dve.wait_ge(E("decay_in"), 16)
            for h in range(RET_HEADS):
                dve.wait_ge(E("rt_s_ps"), h + 1)
                if h >= 1:
                    dve.wait_ge(E("rt_o_ps"), NT * h)
                nc.vector.tensor_tensor(r_sT, bank(2)[:, 0:SC], decay[:, h, :], ALU.mult).then_inc(E("rt_dec"), 1)
                if h >= 1:
                    turned_back(h - 1)
                for t in range(NT):
                    dve.wait_ge(E("rt_o_ps"), NT * h + t + 1)
                    link(nc.vector.bn_stats(stats[:, t, :], bank(4 + t)))
                    link(nc.vector.bn_aggr(mv[:, t, :], stats[:, t, :]))
                nc.vector.tensor_scalar(gvar, mv[:, :, 1], EPS, None, ALU.add).then_inc(E("rt_var"), 1)
                dve.wait_ge(E("rt_rstd"), h + 1)
                if h >= 1:
                    dve.wait_ge(E("rt_yT_ps"), h)
                for t in range(NT):
                    nc.vector.tensor_scalar(r_y[:, t, :], bank(4 + t), mv[:, t, 0:1], grstd[:, t:t + 1], ALU.subtract,
                                            ALU.mult).then_inc(E("rt_on"), 1)
                for t in range(NT):
                    dve.wait_ge(E("rt_on"), NT * h + t + 1)
                    dve.wait_ge(E("rt_sg"), NT * h + t + 1)
                    nc.vector.tensor_tensor(r_y[:, t, :], r_y[:, t, :], r_sg[:, t, :], ALU.mult).then_inc(E("rt_y"), 1)
            turned_back(RET_HEADS - 1)
            ffn_first_dve(dve, units, 1, GATE)
            residual_dve(dve, "ret", units=1)

        def pool_load(units):
            units.load(view(units.slot()[:, 0:2 * D], 8, 256), pool_w[0].rearrange("g (c p) n -> p (g c) n", p=P))

        def pool_dve(dve, link):
            dve.wait_ge(E("rows_in"), 16)
            link(nc.vector.tensor_tensor(pl_bs, R("pool_b"), R("pool_scale"), ALU.mult))
            for t in range(NT):
                link(nc.vector.tensor_tensor(x[:, t, :], x[:, t, :], pl_bs, ALU.add))
            for t in range(NT):
                dve.wait_ge(E("pl_ps"), t + 1)
                if t == NT - 1:
                    dve.sem_inc(used, 1)
                y = pl_y[:, t, :]
                link(nc.vector.tensor_tensor(view(y, 2, BANK), PS[:, 4 + 2 * t:6 + 2 * t, :], view(R("pool_scale"), 2, BANK),
                                             ALU.mult))
                nc.vector.tensor_tensor(x[:, t, :], x[:, t, :], y, ALU.add).then_inc(E("pool_add"), 1)

        def pool_pe(pe, units):
            norm_done(pe, 4)
            units.wait()
            w = view(units.slot()[:, 0:2 * D], 8, 256)
            for t in range(NT):
                for g in range(4):
                    dst = bank(4 + 2 * t + g // 2)[:, (g % 2) * 256:(g % 2 + 1) * 256]
                    for c in range(2):
                        last = nc.tensor.matmul(dst, xnT[:, 2 * g + c, t * P:(t + 1) * P], w[:, 2 * g + c, :],
                                                start=(c == 0), stop=(c == 1))
                last.then_inc(E("pl_ps"), 1)
            units.n += 1

        def mla_load(units):
            units.load(view(units.slot()[:, 0:DC * 320], DC, 320), w_dkv.rearrange("(p c) n -> p c n", c=DC))
            units.load(view(units.slot()[:, 0:DC * Q_RANK], DC, Q_RANK), wq_down[0].rearrange("(p c) n -> p c n", c=DC))
            units.load(view(units.slot()[:, 0:2 * D], 2, D), w_uk.rearrange("(c p) n -> p c n", p=P))
            units.load(view(units.slot()[:, 0:2 * D], 2, D), w_uv.rearrange("(c p) n -> p c n", p=P))
            for n in range(2):
                units.load(view(units.slot()[:, 0:3 * 768], 3, 768),
                           wq_up[0].rearrange("(c p) n -> p c n", p=P)[:, :, n * 768:(n + 1) * 768])
            for n in range(2):
                units.load(view(units.slot(), DC, BANK),
                           wo_m[0].rearrange("(c p) n -> p c n", p=P)[:, :, n * BANK:(n + 1) * BANK])

        def mla_pe(pe, units):
            norm_done(pe, 6)
            units.wait()
            w = view(units.slot()[:, 0:DC * 320], DC, 320)
            for t in range(NT):
                last = rows_of(bank(4 + t)[:, 0:320], tile_of(xkvT, t), lambda c: w[:, c, :], DC)
                last.then_inc(E("ml_kv_ps"), 1)
            units.n += 1
            units.wait()
            w = view(units.slot()[:, 0:DC * Q_RANK], DC, Q_RANK)
            for t in range(NT):
                last = rows_of(bank(6 + t)[:, 0:Q_RANK], tile_of(xnT, t), lambda c: w[:, c, :], DC)
                last.then_inc(E("ml_q_ps"), 1)
            units.n += 1
            pe.wait_ge(E("ml_lat"), 2 * NT)
            pe.wait_ge(E("ml_kr"), 1)
            for t in range(NT):
                for c in range(2):
                    nc.tensor.transpose(bank(0)[:, c * S + t * P:c * S + (t + 1) * P], ckv[:, t, c * P:(c + 1) * P], ident)
                for c in range(2):
                    nc.tensor.transpose(bank(1)[:, c * S + t * P:c * S + (t + 1) * P], cq[:, t, c * P:(c + 1) * P], ident)
                nc.tensor.transpose(bank(2)[:, t * P:(t + 1) * P], cq[:, t, 2 * P:3 * P], ident)
                last = nc.tensor.transpose(bank(2)[:, S + t * P:S + (t + 1) * P], kr2[:, t, :], ident)
            last.then_inc(E("ml_t_ps"), 1)
            pe.wait_ge(E("ml_t"), 4)
            units.wait()
            w = view(units.slot()[:, 0:2 * D], 2, D)
            for h in range(M_HEADS):
                if h >= 2 and h % 2 == 0:
                    pe.wait_ge(E("ml_kn"), h // 2 - 1) if h >= 4 else None
                last = rows_of(bank((h // 2) % 2)[:, (h % 2) * S:(h % 2 + 1) * S],
                               lambda c: w[:, c, h * P:(h + 1) * P], lambda c: ckvT[:, c, :], 2)
                if h % 2:
                    last.then_inc(E("ml_kn_ps"), 1)
            units.n += 1
            units.wait()
            w = view(units.slot()[:, 0:2 * D], 2, D)
            for t in range(NT):
                for n in range(2):
                    last = rows_of(bank(4 + 2 * t + n), tile_of(ckvT, t), lambda c: w[:, c, n * BANK:(n + 1) * BANK], 2)
                    last.then_inc(E("ml_v_ps"), 1)
            units.n += 1
            pe.wait_ge(E("ml_v"), 2)
            for n in range(2):
                units.wait()
                w = view(units.slot()[:, 0:3 * 768], 3, 768)
                wh = w.rearrange("p c (h d) -> p c h d", h=4)
                for t in range(NT):
                    last = rows_of(view(bank(4 + t)[:, n * S:(n + 1) * S], 4, M_ROPE), tile_of(cqT, t),
                                   lambda c: wh[:, c, :, M_NOPE:], 3)
                    if n == 1:
                        last.then_inc(E("ml_qr_ps"), 1)
                for j in range(4):
                    h = 4 * n + j
                    if j % 2 == 0:
                        if h >= 4:
                            pe.wait_ge(E("ml_qn"), h // 2 - 1)
                        else:
                            pe.wait_ge(E("ml_kn"), 3 + h // 2)
                    last = rows_of(bank((h // 2) % 2)[:, (h % 2) * S:(h % 2 + 1) * S],
                                   lambda c: wh[:, c, j, 0:M_NOPE], lambda c: cqT[:, c, :], 3)
                    if j % 2:
                        last.then_inc(E("ml_qn_ps"), 1)
                units.n += 1
            pe.wait_ge(E("ml_qr"), NT)
            for j in range(4):
                for t in range(NT):
                    last = nc.tensor.transpose(bank(2 + j // 2)[:, (j % 2) * S + t * P:(j % 2) * S + (t + 1) * P],
                                               qr[:, t, j * P:(j + 1) * P], ident)
            last.then_inc(E("ml_qrT_ps"), 1)
            pe.wait_ge(E("ml_qrT"), 2)
            pe.wait_ge(E("ml_qn"), 4)
            pe.wait_ge(E("ml_v"), 4)

            def score(h, dst):
                a = M_ROPE * (h % 2)
                q2, k2 = qrT[a:a + M_ROPE, h // 2, :], krT[a:a + M_ROPE, :]
                nc.tensor.matmul(dst[:, 0:P], qnT[:, h, 0:P], knT[:, h, 0:P], start=True, stop=False)
                nc.tensor.matmul(dst[:, 0:P], q2[:, 0:P], k2[:, 0:P], start=False, stop=True)
                nc.tensor.matmul(dst[:, P:SC], qnT[:, h, P:S], knT[:, h, :], start=True, stop=False)
                return nc.tensor.matmul(dst[:, P:SC], q2[:, P:S], k2, start=False, stop=True)

            heads_pe(pe, "ml", score, lambda h, t: m_v[:, t, h * M_V:(h + 1) * M_V], lambda h: bank(4 + h % 2)[:, 0:S], 1)
            pe.wait_ge(E("at_o"), 4 + 8)
            for n in range(2):
                units.wait()
                w = view(units.slot(), DC, BANK)
                for t in range(NT):
                    last = rows_of(bank(n * NT + t), tile_of(m_aT, t), lambda c: w[:, c, :], DC)
                    last.then_inc(E("mla_ps"), 1)
                units.n += 1

        def mla_act(act, link):
            for t in range(NT):
                act.wait_ge(E("ml_kv_ps"), t + 1)
                if t == NT - 1:
                    act.sem_inc(used, 1)
                nc.scalar.activation(ckv[:, t, :], bank(4 + t)[:, 0:320], ACT.Copy).then_inc(E("ml_c"), 1)
            for t in range(NT):
                act.wait_ge(E("ml_q_ps"), t + 1)
                if t == NT - 1:
                    act.sem_inc(used, 1)
                nc.scalar.activation(cq[:, t, :], bank(6 + t)[:, 0:Q_RANK], ACT.Copy).then_inc(E("ml_c"), 1)
            act.wait_ge(E("ml_t_ps"), 1)
            for c in range(2):
                last = nc.scalar.activation(ckvT[:, c, :], bank(0)[:, c * S:(c + 1) * S], ACT.Copy, scale=G("kv_norm")[:, c:c + 1])
            last.then_inc(E("ml_t"), 1)
            for c in range(3):
                last = nc.scalar.activation(cqT[:, c, :], bank(1 + c // 2)[:, (c % 2) * S:(c % 2 + 1) * S], ACT.Copy,
                                            scale=G("q_norm")[:, c:c + 1])
            last.then_inc(E("ml_t"), 2)
            nc.scalar.activation(krT, bank(2)[:, S:2 * S], ACT.Copy).then_inc(E("ml_t"), 1)
            for j in range(4):
                act.wait_ge(E("ml_kn_ps"), j + 1)
                if j == 3:
                    act.sem_inc(used, 1)
                nc.scalar.activation(knT[:, 2 * j:2 * j + 2, :], bank(j % 2, 2, S), ACT.Copy).then_inc(E("ml_kn"), 1)
            act.wait_ge(E("ml_v_ps"), 4)
            act.sem_inc(used, 1)
            for j in range(4):
                act.wait_ge(E("ml_qn_ps"), j + 1)
                if j % 2:
                    act.sem_inc(used, 1)
                nc.scalar.activation(qnT[:, 2 * j:2 * j + 2, :], bank(j % 2, 2, S), ACT.Copy).then_inc(E("ml_qn"), 1)
            heads_act(act, link, "ml", lambda h: m_aT[:, h, :], lambda h: bank(4 + h % 2)[:, 0:S], 1)

        def mla_pool(pool):
            pool.wait_ge(E("ml_ms"), 1)
            nc.gpsimd.tensor_tensor(hrstd[:, :, 0:2], hms[:, :, 0:2],
                                    view(C("minus_half")[:, 0:4], NT, 2), ALU.pow).then_inc(E("ml_rstd"), 1)

        def turn_rows(link, dst, src, t, n):
            half = M_ROPE // 2
            cos = view(C("m_cos"), NT, half)[:, t, :].unsqueeze(1).to_broadcast([P, n, half])
            sin = view(C("m_sin"), NT, half)[:, t, :].unsqueeze(1).to_broadcast([P, n, half])
            a, b = src[:, :, 0:half], src[:, :, half:]
            u = view(m_scor.rearrange("p a b -> p (a b)")[:, 0:n * half], n, half)
            link(nc.vector.tensor_tensor(dst[:, :, 0:half], a, cos, ALU.mult))
            link(nc.vector.tensor_tensor(u, b, sin, ALU.mult))
            link(nc.vector.tensor_tensor(dst[:, :, 0:half], dst[:, :, 0:half], u, ALU.subtract))
            link(nc.vector.tensor_tensor(dst[:, :, half:], b, cos, ALU.mult))
            link(nc.vector.tensor_tensor(u, a, sin, ALU.mult))
            return nc.vector.tensor_tensor(dst[:, :, half:], dst[:, :, half:], u, ALU.add)

        def mla_dve(dve, link):
            dve.wait_ge(E("ml_c"), 2 * NT)
            for t in range(NT):
                link(nc.vector.tensor_tensor(m_sq[:, 0:KV_RANK], ckv[:, t, 0:KV_RANK], ckv[:, t, 0:KV_RANK], ALU.mult))
                link(nc.vector.tensor_reduce(hss[:, t, 0:1], m_sq[:, 0:KV_RANK], AX_X, ALU.add))
                link(nc.vector.tensor_tensor(m_sq, cq[:, t, :], cq[:, t, :], ALU.mult))
                link(nc.vector.tensor_reduce(hss[:, t, 1:2], m_sq, AX_X, ALU.add))
            link(nc.vector.tensor_scalar(hms[:, :, 0:1], hss[:, :, 0:1], 1.0 / KV_RANK, EPS, ALU.mult, ALU.add))
            nc.vector.tensor_scalar(hms[:, :, 1:2], hss[:, :, 1:2], 1.0 / Q_RANK, EPS, ALU.mult, ALU.add).then_inc(E("ml_ms"), 1)
            for t in range(NT):
                link(turn_rows(link, view(kr2[:, t, 0:M_ROPE], 1, M_ROPE), view(ckv[:, t, KV_RANK:], 1, M_ROPE), t, 1))
                last = nc.vector.tensor_copy(kr2[:, t, M_ROPE:], kr2[:, t, 0:M_ROPE])
                if t == 0:
                    link(last)
            last.then_inc(E("ml_kr"), 1)
            dve.wait_ge(E("ml_rstd"), 1)
            for t in range(NT):
                nc.vector.tensor_scalar(ckv[:, t, 0:KV_RANK], ckv[:, t, 0:KV_RANK], hrstd[:, t, 0:1], None,
                                        ALU.mult).then_inc(E("ml_lat"), 1)
                nc.vector.tensor_scalar(cq[:, t, :], cq[:, t, :], hrstd[:, t, 1:2], None, ALU.mult).then_inc(E("ml_lat"), 1)
            for t in range(NT):
                for n in range(2):
                    dve.wait_ge(E("ml_v_ps"), 2 * t + n + 1)
                    nc.vector.tensor_copy(m_v[:, t, n * BANK:(n + 1) * BANK], bank(4 + 2 * t + n)).then_inc(E("ml_v"), 1)
            for t in range(NT):
                dve.wait_ge(E("ml_qr_ps"), t + 1)
                turn_rows(link, view(qr[:, t, :], M_HEADS, M_ROPE), bank(4 + t, M_HEADS, M_ROPE), t,
                          M_HEADS).then_inc(E("ml_qr"), 1)
                dve.wait_ge(E("ml_qr"), t + 1)
            dve.wait_ge(E("ml_qrT_ps"), 1)
            for b in range(2):
                nc.vector.tensor_copy(qrT[:, 2 * b:2 * b + 2, :], bank(2 + b, 2, S)).then_inc(E("ml_qrT"), 1)
            heads_dve(dve, link, "ml", C("mla_mask"), M_SCALE)
            residual_dve(dve, "mla", units=2)

        def route_pe(pe, l):
            norm_done(pe, 5 + 2 * l)
            w = view(G(f"route{l}"), DC, N_ROUTE)
            for t in range(NT):
                last = rows_of(bank(4)[:, t * N_ROUTE:(t + 1) * N_ROUTE], tile_of(xnT, t), lambda c: w[:, c, :], DC)
            last.then_inc(E("ro_ps"), 1)
            pe.wait_ge(E("ro_oh"), l + 1)
            r = bank(5)
            nc.tensor.matmul(r[:, 0:N_EXP], C("before"), ohs[:, 0, :], start=True, stop=True)
            nc.tensor.matmul(r[:, N_EXP:2 * N_EXP], C("ones"), ohs[:, 0, :], start=True, stop=False)
            nc.tensor.matmul(r[:, N_EXP:2 * N_EXP], C("before"), ohs[:, 1, :], start=False, stop=True)
            nc.tensor.matmul(r[:, 2 * N_EXP:3 * N_EXP], C("ones"), ohs[:, 0, :], start=True, stop=False)
            nc.tensor.matmul(r[:, 2 * N_EXP:3 * N_EXP], C("ones"), ohs[:, 1, :], start=False,
                             stop=True).then_inc(E("ro_rank_ps"), 1)

        def route_act(act, link, l):
            act.wait_ge(E("ro_gsh"), l + 1)
            nc.scalar.activation(gcand, gsh, ACT.Exp).then_inc(E("ro_gexp"), 1)
            act.wait_ge(E("ro_m2"), l + 1)
            nc.scalar.activation(r2, m2, ACT.Exp).then_inc(E("ro_r2"), 1)

        def route_dve(dve, link, l):
            v = nc.vector

            def first(dst, values, top, order, n, cand):
                link(v.tensor_tensor(dst, values, spread(top, NT, n), ALU.is_equal))
                link(v.tensor_tensor(cand, dst, order.unsqueeze(1).to_broadcast([P, NT, n]), ALU.mult))
                link(v.tensor_reduce(cmax, cand, AX_X, ALU.max))
                link(v.tensor_tensor(dst, cand, spread(cmax, NT, n), ALU.is_equal))

            dve.wait_ge(E("ro_ps"), l + 1)
            link(v.tensor_tensor(lg, bank(4, NT, N_ROUTE), G(f"route_b{l}").unsqueeze(1).to_broadcast([P, NT, N_ROUTE]), ALU.add))
            lg_g, lg_e = lg[:, :, 0:N_GROUPS], lg[:, :, N_GROUPS:]
            link(v.tensor_reduce(gmax, lg_g, AX_X, ALU.max))
            v.tensor_tensor(gsh, lg_g, spread(gmax, NT, N_GROUPS), ALU.subtract).then_inc(E("ro_gsh"), 1)
            dve.wait_ge(E("ro_gexp"), l + 1)
            link(v.tensor_reduce(gprob, gcand, AX_X, ALU.add))
            link(v.reciprocal(gprob, gprob))
            first(goh, lg_g, gmax, C("first4"), N_GROUPS, gcand)
            link(v.tensor_scalar(pen, goh, -NEG, NEG, ALU.mult, ALU.add))
            for t in range(NT):
                link(v.tensor_tensor(view(em[:, t, :], N_GROUPS, GROUP), view(lg_e[:, t, :], N_GROUPS, GROUP),
                                     spread(pen[:, t, :], N_GROUPS, GROUP), ALU.add))
            link(v.tensor_reduce(m1, em, AX_X, ALU.max))
            first(oh1, em, m1, C("first32"), N_EXP, er)
            link(v.scalar_tensor_tensor(em, oh1, FAR, em, ALU.mult, ALU.add))
            link(v.tensor_reduce(m2, em, AX_X, ALU.max))
            first(oh2, em, m2, C("first32"), N_EXP, er)
            v.tensor_tensor(ohs, oh1, oh2, ALU.add).then_inc(E("ro_oh"), 1)
            v.tensor_tensor(m2, m2, m1, ALU.subtract).then_inc(E("ro_m2"), 1)
            dve.wait_ge(E("ro_r2"), l + 1)
            link(v.tensor_scalar(rd2, r2, 1.0, None, ALU.add))
            link(v.reciprocal(rd2, rd2))
            link(v.tensor_tensor(gate[:, :, 0], gprob, rd2, ALU.mult))
            link(v.tensor_tensor(gate[:, :, 1], gate[:, :, 0], r2, ALU.mult))
            dve.wait_ge(E("ro_rank_ps"), l + 1)
            ranks = bank(5)[:, 0:NT * N_EXP].rearrange("p (t e) -> p t e", t=NT)
            link(v.tensor_reduce(count_max, bank(5)[:, 2 * N_EXP:3 * N_EXP], AX_X, ALU.max))
            v.tensor_copy(flag[:, l:l + 1], count_max).then_inc(E("ro_flag"), 1)
            link(v.tensor_tensor(ea, ranks, C("row_of").unsqueeze(1).to_broadcast([P, NT, N_EXP]), ALU.add))
            for k, oh in enumerate((oh1, oh2)):
                link(v.tensor_tensor(er, oh, ranks, ALU.mult))
                link(v.tensor_reduce(rank1, er, AX_X, ALU.add))
                link(v.tensor_tensor(er, oh, ea, ALU.mult))
                link(v.tensor_reduce(pos[:, :, k], er, AX_X, ALU.add))
                for r in range(1, ROUNDS):
                    link(v.tensor_scalar(over, rank1, float(r * CAP), float(CAP * (N_EXP - 1)), ALU.is_ge, ALU.mult))
                    link(v.tensor_tensor(pos[:, :, k], pos[:, :, k], over, ALU.add))

        PER_STEP = {"xg_ps": 2, "xg": 2, "wT_ps": 1, "wT": 1, "sel": 1, "gu_ps": 2, "sg": 1, "h": 1, "hT_ps": 1, "hT": 1,
                    "y_ps": 2, "y": 2, "c_ps": 4, "add": 4}
        AHEAD = ("xg_ps", "xg", "wT_ps", "wT", "sel")
        PRIMED = ("xg", "h", "c_ps", "add", "y_ps")

        class Pairs:

            def __init__(self, name, ahead, runs=0):
                self.name, self.ahead, self.runs = name, ahead, runs

            def __getitem__(self, what):
                return E(self.name + "_" + what)

            def wait(self, eng, what, value):
                before = self.runs * (PER_STEP[what] * (N_PAIRS + (what in AHEAD)) + (what in PRIMED))
                eng.wait_ge(self[what], before + (what in PRIMED) + value)

        def select(dve, link, q, b):
            v, col = nc.vector, C("column")
            for t in range(NT):
                link(v.tensor_scalar(wtmp, col, pos[:, t, 0:1], gate[:, t, 0:1], ALU.is_equal, ALU.mult))
                link(v.tensor_scalar(wsel[:, b, t, :], col, pos[:, t, 1:2], gate[:, t, 1:2], ALU.is_equal, ALU.mult))
                link(v.tensor_tensor(wsel[:, b, t, :], wsel[:, b, t, :], wtmp, ALU.add))
                link(v.tensor_scalar(wtmp, col, pos[:, t, 0:1], None, ALU.is_equal))
                link(v.scalar_tensor_tensor(sel[:, b, t, :], col, pos[:, t, 1:2], wtmp, ALU.is_equal, ALU.add))
            link(v.tensor_scalar(pos, pos, float(P), None, ALU.subtract))

        LINKS = 5 * NT + 1

        def gather_dve(dve, q, b, l, n, half):
            q.wait(dve, "xg_ps", 2 * n + half + 1)
            g = G(f"g_moe{l}")[:, 4 * half:4 * half + 4]
            nc.vector.tensor_tensor(view(xg[:, b, half * 4 * P:(half + 1) * 4 * P], 4, P), bank(4 + half, 4, P),
                                    spread(g, 4, P), ALU.mult).then_inc(q["xg"], 1)

        def gather_pe(b, q, half):
            for c in range(4 * half, 4 * half + 4):
                for t in range(NT):
                    last = nc.tensor.matmul(bank(4 + half)[:, (c % 4) * P:(c % 4 + 1) * P], hs[:, t, c:D:DC],
                                            sel[:, b, t, :], start=(t == 0), stop=(t == NT - 1))
            last.then_inc(q["xg_ps"], 1)

        def weights_pe(b, q):
            for t in range(NT):
                last = nc.tensor.transpose(bank(7)[:, t * P:(t + 1) * P], wsel[:, b, t, :], ident)
            last.then_inc(q["wT_ps"], 1)

        def pair_pe(pe, q, s, b, six):
            q.wait(pe, "xg", 2 * s + 2 * q.ahead)
            q.wait(pe, "add", 4 * s)
            for what in range(2):
                w = [view(six(2 * what + e), DC, BANK) for e in range(2)]
                for c in range(DC):
                    for e in range(2):
                        last = nc.tensor.matmul(PS[CAP * e:CAP * (e + 1), what, :],
                                                xg[:, b, c * P + CAP * e:c * P + CAP * (e + 1)], w[e][:, c, :],
                                                start=(c == 0), stop=(c == DC - 1))
                last.then_inc(q["gu_ps"], 1)
            q.wait(pe, "sel", s + 1 + q.ahead)
            gather_pe(1 - b, q, 0)
            q.wait(pe, "h", s + 1)
            for c in range(4):
                last = nc.tensor.transpose(bank(6)[:, c * P:(c + 1) * P], e_h[:, c:D_EXP:4], ident)
            last.then_inc(q["hT_ps"], 1)
            weights_pe(1 - b, q)
            gather_pe(1 - b, q, 1)
            w = [view(six(4 + e), 4, D) for e in range(2)]
            q.wait(pe, "hT", s + 1)
            for n in range(2):
                for c in range(4):
                    for e in range(2):
                        last = nc.tensor.matmul(PS[CAP * e:CAP * (e + 1), 2 + n, :], e_hT[:, c, CAP * e:CAP * (e + 1)],
                                                w[e][:, c, n * BANK:(n + 1) * BANK], start=(c == 0), stop=(c == 3))
                last.then_inc(q["y_ps"], 1)
            q.wait(pe, "wT", s + 1 + q.ahead)
            q.wait(pe, "xg", 2 * s + 2 * q.ahead + 1)
            for n in range(2):
                q.wait(pe, "y", 2 * s + n + 1)
                for t in range(NT):
                    nc.tensor.matmul(bank(COMBINE[n][t]), wT[:, b, t * P:(t + 1) * P], e_y[:, n * BANK:(n + 1) * BANK],
                                     start=True, stop=True).then_inc(q["c_ps"], 1)

        COMBINE = ((2, 7), (3, 4))

        def pair_act(act, q, s, b):
            q.wait(act, "gu_ps", 2 * s + 1)
            if q.ahead:
                act.sem_inc(used, 2)
            q.wait(act, "h", s)
            nc.scalar.activation(sg, bank(0), ACT.Silu).then_inc(q["sg"], 1)
            q.wait(act, "wT_ps", s + q.ahead + 1)
            q.wait(act, "c_ps", 4 * s)
            nc.scalar.activation(wT[:, 1 - b, :], bank(7)[:, 0:S], ACT.Copy).then_inc(q["wT"], 1)
            for n in range(2):
                q.wait(act, "y_ps", 2 * s + n + 1)
                if q.ahead and n == 1:
                    act.sem_inc(used, 2)
                nc.scalar.activation(e_y[:, n * BANK:(n + 1) * BANK], bank(2 + n), ACT.Copy).then_inc(q["y"], 1)

        def pair_dve(dve, link, q, s, b, l):
            select(dve, link, q, 1 - b)
            dve.sem_inc(q["sel"], 1)
            q.wait(dve, "gu_ps", 2 * s + 2)
            q.wait(dve, "sg", s + 1)
            if q.ahead:
                dve.sem_inc(used, 2)
            nc.vector.tensor_tensor(e_h, sg, bank(1), ALU.mult).then_inc(q["h"], 1)
            gather_dve(dve, q, 1 - b, l, s + q.ahead, 0)
            q.wait(dve, "hT_ps", s + 1)
            nc.vector.tensor_copy(e_hT, bank(6, 4, P)).then_inc(q["hT"], 1)
            gather_dve(dve, q, 1 - b, l, s + q.ahead, 1)
            for n in range(2):
                for t in range(NT):
                    q.wait(dve, "c_ps", 4 * s + 2 * n + t + 1)
                    v = x[:, t, n * BANK:(n + 1) * BANK]
                    nc.vector.tensor_tensor(v, v, bank(COMBINE[n][t]), ALU.add).then_inc(q["add"], 1)

        def expert_source(l, e, k):
            src = (e_gate, e_up, e_down)[k // 2]
            rows = src[l].rearrange("e (p c) n -> e p (c n)", p=P)
            return rows[bass.ds(e + k % 2, 1)].rearrange("e p n -> p (e n)")

        TURNS = N_PAIRS // 2

        def moe_load(sp, units, l):
            with sp.Fori(0, TURNS) as turn:
                units.loop(turn, 2 * SLOTS)
                for j in range(2):
                    for k in range(6):
                        units.load(units.slot(), expert_source(l, turn * 4 + 2 * j, k))
                units.done(TURNS)
            more = Pairs(f"more{l}", 0)
            sp.wait_ge(E("ro_flag"), l + 1)
            count = sp.value_load(flag[0:1, l:l + 1])
            with sp.If(count > CAP):
                sp.wait_ge(used, units.n)
                with sp.Fori(0, ROUNDS - 1) as r:
                    with sp.Fori(0, N_PAIRS) as e:
                        sp.wait_ge(more["y_ps"], (r * N_PAIRS + e) * 2 + 1)
                        for k in range(6):
                            sp.dma_start(ring[:, k, :], expert_source(l, e * 2, k)).then_inc(more["loaded"], 16)
                sp.wait_ge(more["loaded"], 96 * (ROUNDS - 1) * N_PAIRS)
                sp.wait_ge(more["y_ps"], (ROUNDS - 1) * N_PAIRS * 2 + 1)

        def moe_pe(pe, units, l):
            q = Pairs("moe", 1, l)
            for what in ("c_ps", "y_ps"):
                pe.sem_inc(q[what], 1)
            route_pe(pe, l)
            q.wait(pe, "sel", 1)
            gather_pe(0, q, 0)
            weights_pe(0, q)
            gather_pe(0, q, 1)
            q.wait(pe, "wT", 1)
            with pe.Fori(0, TURNS) as turn:
                units.loop(turn, 2 * SLOTS)
                for j in range(2):
                    def six(k):
                        units.wait()
                        got = units.slot()
                        units.n += 1
                        return got

                    pair_pe(pe, q, turn * 2 + j, j, six)
                units.done(TURNS)
            more = Pairs(f"more{l}", 0)
            pe.wait_ge(E("ro_flag"), l + 1)
            count = pe.value_load(flag[0:1, l:l + 1])
            with pe.If(count > CAP):
                q.wait(pe, "xg", 2 * N_PAIRS + 2)
                q.wait(pe, "wT", N_PAIRS + 1)
                q.wait(pe, "add", 4 * N_PAIRS)
                for what in ("c_ps", "y_ps"):
                    pe.sem_inc(more[what], 1)
                with pe.Fori(0, (ROUNDS - 1) * N_PAIRS // 2) as turn:
                    for j in range(2):
                        s = turn * 2 + j
                        pe.wait_ge(more["loaded"], 96 * s + 96)
                        pair_pe(pe, more, s, j, lambda k: ring[:, k, :])

        def moe_act(act, link, l):
            q = Pairs("moe", 1, l)
            route_act(act, link, l)
            q.wait(act, "wT_ps", 1)
            nc.scalar.activation(wT[:, 0, :], bank(7)[:, 0:S], ACT.Copy).then_inc(q["wT"], 1)
            with act.Fori(0, TURNS) as turn:
                for j in range(2):
                    pair_act(act, q, turn * 2 + j, j)
            more = Pairs(f"more{l}", 0)
            act.wait_ge(E("ro_flag"), l + 1)
            count = act.value_load(flag[0:1, l:l + 1])
            with act.If(count > CAP):
                q.wait(act, "c_ps", 4 * N_PAIRS)
                q.wait(act, "h", N_PAIRS)
                with act.Fori(0, (ROUNDS - 1) * N_PAIRS // 2) as turn:
                    for j in range(2):
                        pair_act(act, more, turn * 2 + j, j)
                more.wait(act, "add", 4 * (ROUNDS - 1) * N_PAIRS)

        def moe_dve(dve, link, l, links):
            q = Pairs("moe", 1, l)
            for what in ("xg", "h", "add"):
                dve.sem_inc(q[what], 1)
            route_dve(dve, link, l)
            select(dve, link, q, 0)
            dve.sem_inc(q["sel"], 1)
            gather_dve(dve, q, 0, l, 0, 0)
            gather_dve(dve, q, 0, l, 0, 1)
            with dve.Fori(0, TURNS) as turn:
                link.loop(turn, 2 * LINKS)
                for j in range(2):
                    pair_dve(dve, link, q, turn * 2 + j, j, l)
                link.done(TURNS)
            more = Pairs(f"more{l}", 0)
            dve.wait_ge(E("ro_flag"), l + 1)
            count = dve.value_load(flag[0:1, l:l + 1])
            with dve.If(count > CAP):
                link2 = Chain(dve, more["links"])
                for what in ("xg", "h", "add"):
                    dve.sem_inc(more[what], 1)
                with dve.Fori(0, (ROUNDS - 1) * N_PAIRS // 2) as turn:
                    link2.loop(turn, 2 * LINKS)
                    for j in range(2):
                        pair_dve(dve, link2, more, turn * 2 + j, j, l)
                    link2.done((ROUNDS - 1) * N_PAIRS // 2)

        N_FIRST = const_at["minus_half"][1]
        EVEN_UNITS, RET_UNITS = 8, 16

        block = ctx.enter_context(nc.Block())

        @block.sync
        def _(sp):
            units = Units(sp)
            sp.dma_start(x[:, 0, :], x_in[0, 0:P, :]).then_inc(E("x_in"), 16)
            sp.dma_start(x[:, 1, :], x_in[0, P:S, :]).then_inc(E("x_in"), 16)
            even_load(units)
            ffn_load(sp, units, 0)
            ret_load(units)
            ffn_load(sp, units, 1)
            pool_load(units)
            moe_load(sp, units, 0)
            mla_load(units)
            moe_load(sp, units, 1)
            for t in range(NT):
                sp.wait_ge(E("out_rdy"), t + 1)
                sp.dma_start(out[0, t * P:(t + 1) * P, :], hs[:, t, :]).then_inc(E("out_sent"), 16)
            sp.wait_ge(E("out_sent"), 16 * NT)

        @block.tensor
        def _(pe):
            units = Units(pe)
            pe.wait_ge(E("first_in"), 16)
            norm_pe(pe, 0)
            even_pe(pe, units)
            norm_pe(pe, 1)
            ffn_pe(pe, units, 0)
            norm_pe(pe, 2)
            ret_pe(pe, units)
            norm_pe(pe, 3)
            ffn_pe(pe, units, 1)
            norm_pe(pe, 4)
            pool_pe(pe, units)
            norm_pe(pe, 5)
            moe_pe(pe, units, 0)
            norm_pe(pe, 6)
            mla_pe(pe, units)
            norm_pe(pe, 7)
            moe_pe(pe, units, 1)

        @block.scalar
        def _(act):
            act.dma_start(cst[:, 0:N_FIRST], const[:, 0:N_FIRST]).then_inc(E("first_in"), 16)
            act.dma_start(par[:, :], params).then_inc(E("param_in"), 16)
            act.dma_start(cst[:, N_FIRST:], const[:, N_FIRST:]).then_inc(E("const_in"), 16)
            link = Chain(act, E("act_link"))
            units = Units(act)
            units.n = EVEN_UNITS
            act.wait_ge(E("param_in"), 16)
            norm_act(act, link, 0)
            even_act(act, link)
            ffn_first_act(act, units, 0, GATE)
            norm_act(act, link, 1)
            ffn_first_act(act, units, 0, VALUE)
            ffn_act(act, units, 0)
            act.wait_ge(E("ffn_ps"), 2 * NT)
            act.dma_start(late[:, 0:RET_HEADS * SC], decay_in).then_inc(E("decay_in"), 16)
            norm_act(act, link, 2)
            ret_act(act, link)
            units.n += RET_UNITS
            ffn_first_act(act, units, 1, GATE)
            norm_act(act, link, 3)
            ffn_first_act(act, units, 1, VALUE)
            ffn_act(act, units, 1)
            act.wait_ge(E("ffn_ps"), 4 * NT)
            act.dma_start(work[:, 0:4 * SC], band_in).then_inc(E("band_in"), 16)
            act.dma_start(late[:, :], rows).then_inc(E("rows_in"), 16)
            norm_act(act, link, 4)
            norm_act(act, link, 5)
            moe_act(act, link, 0)
            norm_act(act, link, 6)
            mla_act(act, link)
            norm_act(act, link, 7)
            moe_act(act, link, 1)
            norm_act(act, link, 8)

        @block.gpsimd
        def _(pool):
            pool.wait_ge(E("first_in"), 16)
            norm_pool(pool, 0)
            even_pool(pool)
            norm_pool(pool, 1)
            norm_pool(pool, 2)
            ret_pool(pool)
            for k in range(3, 7):
                norm_pool(pool, k)
            mla_pool(pool)
            norm_pool(pool, 7)
            norm_pool(pool, 8)

        @block.vector
        def _(dve):
            link = Chain(dve, E("dve_link"))
            units = Units(dve)
            units.n = EVEN_UNITS
            dve.wait_ge(E("param_in"), 16)
            norm_dve(dve, link, 0)
            dve.wait_ge(E("const_in"), 16)
            even_dve(dve, units, link)
            norm_dve(dve, link, 1)
            ffn_first_dve(dve, units, 0, VALUE)
            ffn_dve(dve, units, link, 0)
            norm_dve(dve, link, 2)
            units.n += RET_UNITS
            ret_dve(dve, units, link)
            norm_dve(dve, link, 3)
            ffn_first_dve(dve, units, 1, VALUE)
            ffn_dve(dve, units, link, 1)
            norm_dve(dve, link, 4)
            pool_dve(dve, link)
            norm_dve(dve, link, 5)
            moe_dve(dve, link, 0, None)
            norm_dve(dve, link, 6)
            mla_dve(dve, link)
            norm_dve(dve, link, 7)
            moe_dve(dve, link, 1, None)
            dve.wait_ge(E("n_rstd"), 9 * NT)
            dve.wait_ge(E("rows_in"), 16)
            for t in range(NT):
                nc.vector.scalar_tensor_tensor(hs[:, t, :], x[:, t, :], rstd[:, t:t + 1], R("final"), ALU.mult,
                                               ALU.mult).then_inc(E("out_rdy"), 1)


def kernel(**inputs):
    import concourse.bacc as bacc
    from concourse.bass_utils import run_bass_kernel_spmd

    a = {k: np.ascontiguousarray(v) for k, v in inputs.items()}
    table, _, decay, band = shape_constants()

    def striped(v):
        return v.reshape(P, -1)

    def stacked(v):
        return v.reshape(-1, P).T

    def router(l):
        w = np.concatenate([a["router_group_w_2"][l], a["router_expert_w_2"][l]], axis=1)
        return w.reshape(P, DC * N_ROUTE)

    def router_bias(l):
        b = np.concatenate([a["router_group_b_2"][l], a["router_expert_b_2"][l]])
        return np.broadcast_to(b[None, :], (P, N_ROUTE))

    def ffn_taps(l):
        w = a["ffn_conv_w"][l].reshape(3, 2, N_SLABS, 2, P)
        return w.transpose(4, 2, 1, 3, 0).reshape(P, -1)

    by_name = {
        "g_even": striped(a["even_norm"][0]), "g_ffn0": striped(a["ffn_norm"][0]), "g_odd": striped(a["odd_norm"][0]),
        "g_ffn1": striped(a["ffn_norm"][1]), "g_pool": stacked(a["pool_norm_2"][0]), "g_moe0": striped(a["ffn_norm_2"][0]),
        "g_kvin": striped(a["kv_in_norm_2"]), "g_attn": striped(a["attn_norm_2"][0]), "g_moe1": striped(a["ffn_norm_2"][1]),
        "q_gain": np.concatenate([a["even_q_gain"][0]] * 2)[:, None],
        "k_gain": np.concatenate([a["even_k_gain"][0]] * 2)[:, None],
        "sconv": a["even_sconv_w"][0].reshape(3, 4, P).transpose(2, 1, 0).reshape(P, -1),
        "gn": stacked(a["ret_gn_gain"][0].reshape(-1)), "conv0": ffn_taps(0), "conv1": ffn_taps(1),
        "kv_norm": stacked(a["kv_norm_2"]), "q_norm": stacked(a["q_norm_2"][0]),
        "route0": router(0), "route1": router(1), "route_b0": router_bias(0), "route_b1": router_bias(1),
    }
    params = np.ascontiguousarray(np.concatenate([by_name[n] for n, _ in PARAMS], axis=1))
    row_values = {"pool_b": a["pool_b_2"][0].reshape(-1), "pool_scale": a["pool_scale_2"][0], "final": a["final_norm_2"]}
    rows = np.ascontiguousarray(np.broadcast_to(np.concatenate([row_values[n] for n, _ in ROWS])[None, :], (P, 3 * D)))
    arrays = {"const": np.ascontiguousarray(table), "decay": decay, "band": band, "params": params, "rows": rows}
    for name in ("x", "even_w_in", "even_w_out", "ret_wq", "ret_wk", "ret_wv", "ret_wg", "ret_wo", "ffn_w_up", "ffn_w_down",
                 "pool_w_2", "w_dkv_2", "w_uk_2", "w_uv_2", "wq_down_2", "wq_up_2", "wo_2", "w_gate_2", "w_up_2", "w_down_2"):
        arrays[name] = a[name]
    nc = bacc.Bacc("TRN2", target_bir_lowering=False, num_devices=1)
    args = [nc.dram_tensor(k, v.shape, F32, kind="ExternalInput").ap() for k, v in arrays.items()]
    args.append(nc.dram_tensor("out", (1, S, D), F32, kind="ExternalOutput").ap())
    build(nc, *args)
    r = run_bass_kernel_spmd(nc, [arrays], core_ids=[0])
    return r.results[0]["out"]
```

```python
from contextlib import ExitStack

import numpy as np

import concourse.bass as bass
from concourse import mybir

F32 = mybir.dt.float32
F32R = mybir.dt.float32r
I32 = mybir.dt.int32
ALU = mybir.AluOpType
ACT = mybir.ActivationFunctionType
AX_X = mybir.AxisListType.X

P = 128
S = 256
NT = S // P
D = 1024
DC = D // P
BANK = 512
EPS = 1e-6
NEG = -1.0e30
FAR = -2.0e30

A_HEADS, A_DIM = 8, 64
DILATED = ((128, 1), (512, 4), (2048, 16))
RET_HEADS, RET_K, RET_V = 4, 256, 512
ROPE_BASE = 10000.0
D_FF = 2816
SLAB = 256
N_SLABS = D_FF // SLAB
POOL_WINDOWS = (2, 4, 8, 16)
M_HEADS, M_NOPE, M_ROPE, M_V = 8, 128, 64, 128
Q_RANK, KV_RANK = 384, 256
M_CHUNK = 64
M_SCALE = 1.0 / float(np.sqrt(M_NOPE + M_ROPE))
N_GROUPS, GROUP = 4, 8
N_EXP = N_GROUPS * GROUP
N_ROUTE = N_GROUPS + N_EXP
D_EXP = 512
CAP = 64
N_PAIRS = N_EXP // 2
ROUNDS = S // CAP
SLOTS = 6
UNIT = 4096
SC = P + S


def shape_constants():
    f = np.float32
    q = np.arange(S)[:, None]
    k = np.arange(S)[None, :]
    diff = q - k
    times = np.zeros((S, S))
    for window, dil in DILATED:
        times += (diff >= 0) & (diff % dil == 0) & (diff // dil <= window // dil)
    dil_mask = np.where(times > 0, np.log(np.maximum(times, 1)), NEG)
    mla_mask = np.where(k // M_CHUNK <= q // M_CHUNK, 0.0, NEG)

    def by_tile(m):
        return np.concatenate([m[0:P, 0:P], m[P:S, 0:S]], axis=1)

    log_g = np.log1p(-(2.0 ** (-5.0 - np.arange(RET_HEADS))))
    decay = []
    for h in range(RET_HEADS):
        m = np.where(diff >= 0, np.exp(log_g[h] * np.maximum(diff, 0)), 0.0).T * RET_K ** -0.5
        decay.append(np.concatenate([m[0:P, 0:S], m[P:S, P:S]], axis=1))
    half = RET_K // 2
    inv = f(ROPE_BASE) ** (-np.arange(half, dtype=f) / f(half))
    ang = (np.arange(S, dtype=f)[:, None] * inv[None, :]).astype(f).T
    half = M_ROPE // 2
    inv = f(ROPE_BASE) ** (-np.arange(half, dtype=f) / f(half))
    ang2 = (np.arange(S, dtype=f)[:, None] * inv[None, :]).astype(f).reshape(NT, P, half).transpose(1, 0, 2)
    band = []
    for window in POOL_WINDOWS:
        m = ((diff >= 0) & (diff < window)) / np.minimum(q + 1, window) - np.eye(S)
        band.append(np.concatenate([m.T[0:P, 0:S], m.T[P:S, P:S]], axis=1))
    row = np.arange(P)
    parts = {
        "ident": np.eye(P),
        "minus_half": np.full((P, NT * 2 * A_HEADS), -0.5),
        "dil_mask": by_tile(dil_mask),
        "mla_mask": by_tile(mla_mask),
        "r_cos": np.cos(ang), "r_sin": np.sin(ang),
        "m_cos": np.cos(ang2).reshape(P, -1), "m_sin": np.sin(ang2).reshape(P, -1),
        "before": (row[:, None] < row[None, :]) * 1.0,
        "ones": np.ones((P, P)),
        "column": np.tile(row[None, :], (P, 1)),
        "first4": np.tile(N_GROUPS - np.arange(N_GROUPS)[None, :], (P, 1)),
        "first32": np.tile(N_EXP - np.arange(N_EXP)[None, :], (P, 1)),
        "row_of": np.tile(CAP * np.arange(N_EXP)[None, :], (P, 1)),
    }
    where, at = {}, 0
    for name, a in parts.items():
        where[name] = (at, at + a.shape[1])
        at += a.shape[1]
    table = np.concatenate([a.astype(f) for a in parts.values()], axis=1)
    return table, where, np.concatenate(decay, axis=1).astype(f), np.concatenate(band, axis=1).astype(f)


PARAMS = [
    ("g_even", DC), ("g_ffn0", DC), ("g_odd", DC), ("g_ffn1", DC), ("g_pool", DC),
    ("g_moe0", DC), ("g_kvin", DC), ("g_attn", DC), ("g_moe1", DC),
    ("q_gain", 1), ("k_gain", 1), ("sconv", 12), ("gn", 16), ("conv0", 132), ("conv1", 132),
    ("kv_norm", 2), ("q_norm", 3), ("route0", DC * N_ROUTE), ("route1", DC * N_ROUTE),
    ("route_b0", N_ROUTE), ("route_b1", N_ROUTE),
]
ROWS = [("pool_b", D), ("pool_scale", D), ("final", D)]


def places(table):
    where, at = {}, 0
    for name, n in table:
        where[name] = (at, at + n)
        at += n
    return where, at


class Chain:

    def __init__(self, eng, sem):
        self.eng, self.sem, self.n, self.turn, self.per, self.base = eng, sem, 0, None, 0, 0

    def __call__(self, ins):
        self.n += 1
        ins.then_inc(self.sem, 1)
        self.eng.wait_ge(self.sem, self.n if self.turn is None else self.turn * self.per + self.n)

    def loop(self, turn, per):
        self.turn, self.per, self.base = turn, per, self.n

    def done(self, turns):
        assert self.n - self.base == self.per, (self.n - self.base, self.per)
        self.turn, self.n = None, self.base + self.per * turns


def build(nc, const, decay_in, band_in, params, rows, x_in, w_in, w_out, wq, wk, wv, wg, wo_r, w_up, w_down, pool_w, w_dkv, w_uk, w_uv,
          wq_down, wq_up, wo_m, e_gate, e_up, e_down, out):
    const_at = shape_constants()[1]
    param_at, n_params = places(PARAMS)
    row_at, n_rows = places(ROWS)
    n_const = const.shape[1]
    ctx = ExitStack()
    with ctx:
        def sb(name, shape, dt=F32):
            return ctx.enter_context(nc.sbuf_tensor(name, shape, dt))

        def sem(name):
            return ctx.enter_context(nc.semaphore(name))

        ring = sb("ring", [P, SLOTS, UNIT])
        cst = sb("cst", [P, n_const])
        par = sb("par", [P, n_params])
        x = sb("x_res", [P, NT, D])
        hs_at = -(-nc.sbuf_base // 32) * 32
        hs = sb("hs", [P, NT, D])
        small = sb("small", [P, 512])
        flag = sb("flag", [P, 2], I32)
        WORK = 14720
        late_at = -(-nc.sbuf_base // 32) * 32
        xnT_at = late_at + 4 * n_rows
        work_at = xnT_at + 4 * DC * S

        def placed(name, shape, at, dt=F32):
            return nc.alloc_sbuf_tensor_at(name, shape, dt, offset=at)

        late = placed("late", [P, n_rows], late_at)
        xnT = placed("xnT", [P, DC, S], xnT_at)[:, :, :]
        work = placed("work", [P, WORK], work_at)
        PS = ctx.enter_context(nc.psum_tensor("PS", [P, 8, BANK], F32))

        def C(name):
            a, b = const_at[name]
            return cst[:, a:b]

        def G(name):
            a, b = param_at[name]
            return par[:, a:b]

        def R(name):
            a, b = row_at[name]
            return late[:, a:b]

        def view(v, *shape):
            if len(shape) == 2:
                return v.rearrange("p (a b) -> p a b", b=shape[1])
            if len(shape) == 3:
                return v.rearrange("p (a b c) -> p a b c", b=shape[1], c=shape[2])
            return v

        def area(at, *shape):
            n = int(np.prod(shape))
            assert at + n <= WORK
            return view(work[:, at:at + n], *shape)

        def scratch(at, *shape):
            return view(small[:, at:at + int(np.prod(shape))], *shape)

        def bank(b, *shape):
            return view(PS[:, b, 0:int(np.prod(shape))], *shape) if shape else PS[:, b, :]

        def spread(col, *shape):
            return col.unsqueeze(len(col.shape)).to_broadcast([P, *shape])

        ident = C("ident")
        decay = view(late[:, 0:RET_HEADS * SC], RET_HEADS, SC)

        ss, ms, rstd, ms_part = scratch(0, NT, 2), scratch(4, NT), scratch(6, NT), scratch(288, NT)
        hss, hms, hrstd = scratch(8, NT, 16), scratch(40, NT, 16), scratch(72, NT, 16)
        nmx, den, rden = scratch(104, 2, 2), scratch(108, 2, 2), scratch(112, 2, 2)
        gqk = scratch(116, 1)
        stats, mv, gvar, grstd = scratch(120, NT, 6), scratch(132, NT, 2), scratch(136, NT), scratch(138, NT)
        gmax, gprob, cmax, m1, m2 = (scratch(144 + 2 * i, NT) for i in range(5))
        r2, rd2, count_max = scratch(154, NT), scratch(156, NT), scratch(158, 1)
        pos, gate = scratch(160, NT, 2), scratch(164, NT, 2)
        rank, over, row = scratch(168, 2 * NT), scratch(172, 2 * NT), scratch(284, 2 * NT)
        gsh, goh, gcand, pen = (scratch(176 + 8 * i, NT, N_GROUPS) for i in range(4))
        lg = scratch(208, NT, N_ROUTE)

        qk_t = area(0, NT, 2 * BANK)
        v_t = area(2048, NT, BANK)
        qT, kT = area(3072, 4, S), area(4096, 4, S)
        gbT, gcT, zT = area(5120, 4, S), area(6144, 4, S), area(7168, 4, S)
        mix_hi = placed("mix_hi", [P, 8, S], work_at + 4 * 8192, F32R)
        mix_lo = [placed("mix_lo_heads", [P, 4, S], work_at, F32R),
                  placed("mix_lo_conv", [P, 4, S], work_at + 4 * 6144, F32R)]
        scor, prob, probT = area(10240, 2, SC), area(11008, 2, SC), area(11776, 2, SC)
        convt = area(13568, 4, S)
        sq = [area(13568, D), area(10240, D)]
        QUARTER = UNIT // 4
        e_w_at = [late_at, late_at + 4 * QUARTER, late_at + 8 * QUARTER, work_at + 4 * 12544]
        e_w = [[placed(f"e_w{i}_{part}", [P, QUARTER], e_w_at[2 * i + j], F32R) for j, part in enumerate(("hi", "lo"))]
               for i in range(2)]
        assert 3 * QUARTER <= n_rows and 12544 + QUARTER <= 13568
        f_u = area(0, 4, S)
        f_cw = area(1024, 12)
        f_at = work_at + 4 * 1040
        HALF = UNIT // 2
        f_w = [[placed(f"f_w_{kind}_{part}", [P, HALF], f_at + 4 * HALF * (2 * i + j), F32R)
                for j, part in enumerate(("hi", "lo"))] for i, kind in enumerate(("gate", "value", "down"))]
        f_h = [placed(f"f_h_{part}", [P, 2, S], f_at + 4 * (6 * HALF + j * 2 * S), F32R) for j, part in enumerate(("hi", "lo"))]
        f_x = [placed("f_x_hi", [P, DC, S], xnT_at, F32R), placed("f_x_lo", [P, DC, S], late_at, F32R)]
        assert 1040 + 6 * HALF + 4 * S <= WORK and DC * S <= n_rows
        R_AT, R_HEAD = 32, 2048
        r_q = [area(R_AT + R_HEAD * h, 2, S) for h in range(RET_HEADS)]
        r_k = [area(R_AT + R_HEAD * h + 512, 2, S) for h in range(RET_HEADS)]
        r_v = [area(R_AT + R_HEAD * h + 1024, NT, RET_V) for h in range(RET_HEADS)]
        r_yT = [[placed(f"r_y{h}_{part}", [P, 4, S], work_at + 4 * (R_AT + R_HEAD * h + 1024 * j), F32R)
                 for j, part in enumerate(("hi", "lo"))] for h in range(RET_HEADS)]
        rope_at = R_AT + RET_HEADS * (R_HEAD + 1024)
        rope_c, rope_s = area(rope_at, 2, S), area(rope_at + 512, 2, S)
        r_y = area(rope_at, NT, RET_V)
        r_sT = late[:, RET_HEADS * SC:(RET_HEADS + 1) * SC]
        r_w_at = [work_at + 4 * (R_AT + RET_HEADS * R_HEAD + QUARTER * i) for i in range(4)] + [
            work_at + 4 * (rope_at + 1024), late_at + 4 * (RET_HEADS + 1) * SC]
        r_w = [[placed(f"r_w{i}_{part}", [P, QUARTER], r_w_at[2 * i + j], F32R) for j, part in enumerate(("hi", "lo"))]
               for i in range(3)]
        assert rope_at + 1024 + QUARTER <= WORK and (RET_HEADS + 1) * SC + QUARTER <= n_rows
        assert 1040 + 2 * HALF <= R_AT + 3 * R_HEAD
        r_x = [f_x[0], placed("r_x_lo", [P, DC, S], hs_at, F32R)]
        pl_band = area(1040 + 4 * HALF, 4, SC)
        pl_y = area(1536, NT, D)
        pl_bs = area(3584, D)
        xkvT = area(0, DC, S)
        qnT = area(0, M_HEADS, S)
        ckv, cq, kr2 = area(2048, NT, 320), area(2688, NT, Q_RANK), area(3456, NT, P)
        m_w_at = [late_at, late_at + 4 * QUARTER, late_at + 8 * QUARTER, xnT_at]
        m_w = [[placed(f"m_w{i}_{part}", [P, QUARTER], m_w_at[2 * i + j], F32R) for j, part in enumerate(("hi", "lo"))]
               for i in range(2)]
        m_aT = [placed(f"m_aT_{part}", [P, 2, S], xnT_at + 4 * (QUARTER + 2 * S * j), F32R)
                for j, part in enumerate(("hi", "lo"))]
        assert 3 * QUARTER <= n_rows and QUARTER + 4 * S <= DC * S
        ckvT, cqT = area(4096, 2, S), area(4608, 3, S)
        knT = area(5376, M_HEADS, S)
        m_v = area(7424, NT, M_HEADS * M_V)
        qr, qrT = area(9472, NT, BANK), area(10496, 4, S)
        m_scor, m_prob, m_probT = area(11520, 2, SC), area(12288, 2, SC), area(13056, 2, SC)
        m_sq, krT = area(13824, Q_RANK), area(14208, S)
        sel, wsel = area(0, 2, NT, P), area(512, 2, NT, P)
        wT, xg = area(1152, 2, S), area(1664, 2, DC * P)
        sg, e_h, e_hT, e_y = area(3712, BANK), area(4224, BANK), area(4736, 4, P), area(5248, D)
        oh1, oh2, ohs, em, er = (area(6400 + 64 * i, NT, N_EXP) for i in range(5))
        ohk, erk = area(6400, 2 * NT, N_EXP), area(6656, 2 * NT, N_EXP)
        lgT = area(6784, S)
        extra_at = 7552
        extra = [(area(extra_at, UNIT),),
                 (area(extra_at + UNIT, UNIT // 2), xnT.rearrange("p c s -> p (c s)")),
                 (late[:, 0:n_rows], area(extra_at + UNIT + UNIT // 2, UNIT - n_rows))]
        wtmp, wtmp2 = area(7040, NT, P), area(7040 + NT * P, NT, P)

        named = {}

        def E(name):
            if name not in named:
                named[name] = sem(name)
            return named[name]

        loaded = [sem(f"loaded{i}") for i in range(SLOTS)]
        used = sem("used")

        class Units:

            def __init__(self, eng):
                self.eng, self.n, self.turn, self.per, self.base = eng, 0, None, 0, 0

            def slot(self, k=0):
                return ring[:, (self.n + k) % SLOTS, :]

            def wait(self, k=0):
                u = self.n + k
                there = 16 * (u // SLOTS + 1)
                if self.turn is not None:
                    there = self.turn * (16 * self.per // SLOTS) + there
                self.eng.wait_ge(loaded[u % SLOTS], there)

            def load(self, dst, src):
                u = self.n
                if u >= SLOTS:
                    done = u - SLOTS + 1
                    self.eng.wait_ge(used, done if self.turn is None else self.turn * self.per + done)
                self.eng.dma_start(dst, src).then_inc(loaded[u % SLOTS], 16)
                self.n += 1

            def loop(self, turn, per):
                self.turn, self.per, self.base = turn, per, self.n

            def done(self, turns):
                assert self.n - self.base == self.per
                self.turn, self.n = None, self.base + self.per * turns

        NORMS = ["g_even", "g_ffn0", "g_odd", "g_ffn1", "g_pool", "g_moe0", "g_attn", "g_moe1"]
        BY_TILE = ((0, 0), (0, 1), (1, 0), (1, 1))

        def in_order(name, before, order=BY_TILE):
            return name, {piece: before + i + 1 for i, piece in enumerate(order)}

        BY_HALF = ((0, 0), (1, 0), (0, 1), (1, 1))
        X_DONE = [("x_in", dict.fromkeys(BY_TILE, 16 * NT)), in_order("even_add", 0), in_order("ffn_add", 0),
                  in_order("ret_add", 0), in_order("ffn_add", 4), ("pool_add", {(t, n): t + 1 for t, n in BY_TILE}),
                  in_order("moe_add", 4 * N_PAIRS - 3, BY_HALF), in_order("mla_add", 0),
                  in_order("moe_add", 8 * N_PAIRS - 2, BY_HALF)]
        SPLIT = {0: r_x, 1: f_x, 2: r_x, 3: f_x}
        A_BANKS = [sum(4 if i in SPLIT or i == 6 else 2 for i in range(k)) for k in range(9)]
        D_BANKS = A_BANKS

        def chunk(t, k, c):
            if NORMS[k] == "g_pool":
                return t[:, c * P:(c + 1) * P]
            return t[:, c:D:DC]

        def norm_act(act, link, k, meanwhile=None):
            name, values = X_DONE[k]
            for t, n in sorted(values, key=values.get):
                act.wait_ge(E(name), values[t, n])
                half = slice(n * BANK, (n + 1) * BANK)
                link(nc.scalar.activation(hs[:, t, half], x[:, t, half], ACT.Square, accum_out=ss[:, t, n:n + 1]))
                if n == 0:
                    link(nc.scalar.activation(ms_part[:, t:t + 1], ss[:, t, 0:1], ACT.Copy, bias=EPS, scale=1.0 / D))
                else:
                    nc.scalar.activation(ms[:, t:t + 1], ss[:, t, 1:2], ACT.Identity, bias=ms_part[:, t:t + 1],
                                         scale=1.0 / D).then_inc(E("n_ms"), 1)
            if k == 8:
                return
            if meanwhile:
                meanwhile()
            g = G(NORMS[k])
            for b in (range(4) if k == 6 or k in SPLIT else [1, 3]):
                act.wait_ge(E("n_tr"), 4 * k + b + 1)
                if k == 6:
                    act.wait_ge(E("n_xd"), D_BANKS[k] + b + 1)
                for j in range(2):
                    c = 2 * b + j
                    last = nc.scalar.activation((SPLIT[k][0] if k in SPLIT else xnT)[:, c, :], bank(b)[:, j * S:(j + 1) * S], ACT.Copy,
                                                scale=g[:, c:c + 1])
                last.then_inc(E("n_xa"), 1)

        def norm_pool(pool, k):
            for t in range(NT):
                pool.wait_ge(E("n_ms"), NT * k + t + 1)
                nc.gpsimd.tensor_tensor(rstd[:, t:t + 1], ms[:, t:t + 1], C("minus_half")[:, 0:1],
                                        ALU.pow).then_inc(E("n_rstd"), 1)

        def norm_dve(dve, link, k, meanwhile=None):
            for t in range(NT):
                dve.wait_ge(E("n_rstd"), NT * k + t + 1)
                nc.vector.tensor_scalar(hs[:, t, :], x[:, t, :], rstd[:, t:t + 1], None,
                                        ALU.mult).then_inc(E("n_hs"), 1)
            if meanwhile:
                meanwhile()
            g = G("g_kvin" if k == 6 else NORMS[k])
            if k in SPLIT:
                for b in range(4):
                    dve.wait_ge(E("n_xa"), A_BANKS[k] + b + 1)
                    if SPLIT[k] is r_x and b == 0:
                        dve.wait_ge(E("n_tr"), 4 * k + 4)
                    for c in (2 * b, 2 * b + 1):
                        last = nc.vector.scalar_tensor_tensor(
                            SPLIT[k][1][:, c, :], bank(b)[:, (c % 2) * S:(c % 2 + 1) * S], g[:, c:c + 1],
                            SPLIT[k][0][:, c, :].bitcast(F32), ALU.mult, ALU.subtract)
                    last.then_inc(E("n_xd"), 1)
                return
            dst = xkvT if k == 6 else xnT
            for b in ([0, 2] if k != 6 else range(4)):
                dve.wait_ge(E("n_tr"), 4 * k + b + 1)
                nc.vector.tensor_tensor(dst[:, 2 * b:2 * b + 2, :], bank(b, 2, S),
                                        spread(g[:, 2 * b:2 * b + 2], 2, S), ALU.mult).then_inc(E("n_xd"), 1)

        def norm_pe(pe, k):
            if NORMS[k] == "g_pool":
                pe.wait_ge(E("n_hs"), NT * (k + 1))
                pe.wait_ge(E("band_in"), 16)
                for c in range(DC):
                    dst = bank(c // 2)[:, (c % 2) * S:(c % 2 + 1) * S]
                    nc.tensor.matmul(dst, chunk(hs[:, 0, :], k, c), pl_band[:, c // 2, 0:S], start=True, stop=False)
                    last = nc.tensor.matmul(dst[:, P:S], chunk(hs[:, 1, :], k, c), pl_band[:, c // 2, S:SC],
                                            start=False, stop=True)
                    if c % 2:
                        last.then_inc(E("n_tr"), 1)
                return
            for t in range(NT):
                pe.wait_ge(E("n_hs"), NT * k + t + 1)
                for c in range(DC):
                    last = nc.tensor.transpose(bank(c // 2)[:, (c % 2) * S + t * P:(c % 2) * S + (t + 1) * P],
                                               chunk(hs[:, t, :], k, c), ident)
                    if t == NT - 1 and c % 2:
                        last.then_inc(E("n_tr"), 1)

        def norm_done(eng, k):
            eng.wait_ge(E("n_xa"), A_BANKS[k + 1])
            eng.wait_ge(E("n_xd"), D_BANKS[k + 1])

        def norm_bank(eng, k, b):
            eng.wait_ge(E("n_xd"), D_BANKS[k] + b + 1)

        def rows_of(dst, lhs, w, n):
            for c in range(n):
                last = nc.tensor.matmul(dst, lhs(c), w(c), start=(c == 0), stop=(c == n - 1))
            return last

        def tile_of(src, t):
            return lambda c: src[:, c, t * P:(t + 1) * P]

        def first_head(kind):
            return 8 if kind == "ml" else 0

        HEAD_BANKS = {"ev": (4, (6, 7), 2), "ml": (0, (2,), 1)}

        def heads_pe(pe, kind, score, value, out_of, per_evac, between=None):
            s_bank, t_banks, o_banks = HEAD_BANKS[kind]
            for i in range(8 + 2):
                if i < 8:
                    h = i
                    if h >= 2:
                        pe.wait_ge(E("at_sc"), first_head(kind) + h - 1)
                    last = score(h, bank(s_bank + h % 2))
                    last.then_inc(E("at_s_ps"), 1)
                if between:
                    between(i)
                if 1 <= i <= 8:
                    h = i - 1
                    pe.wait_ge(E("at_p"), first_head(kind) + h + 1)
                    if h >= len(t_banks):
                        pe.wait_ge(E("at_pT"), first_head(kind) + h + 1 - len(t_banks))
                    p = (prob if kind == "ev" else m_prob)[:, h % 2, :]
                    for j in range(3):
                        last = nc.tensor.transpose(bank(t_banks[h % len(t_banks)])[:, j * P:(j + 1) * P], p[:, j * P:(j + 1) * P], ident)
                    last.then_inc(E("at_t_ps"), 1)
                if i >= 2:
                    h = i - 2
                    pe.wait_ge(E("at_pT"), first_head(kind) + h + 1)
                    n = h // per_evac
                    if h % per_evac == 0 and n >= o_banks:
                        pe.wait_ge(E(kind + "_lo"), n + 1 - o_banks)
                    pT = (probT if kind == "ev" else m_probT)[:, h % 2, :]
                    dst = out_of(h)
                    nc.tensor.matmul(dst, value(h, 0), pT[:, 0:S], start=True, stop=False)
                    nc.tensor.matmul(dst[:, P:S], value(h, 1), pT[:, S:SC], start=False,
                                     stop=True).then_inc(E("at_o_ps"), 1)

        def heads_dve(dve, link, kind, mask, scale, between=None, before=None):
            s_bank = HEAD_BANKS[kind][0]
            sc, pr = (scor, prob) if kind == "ev" else (m_scor, m_prob)
            for i in range(8 + 1):
                if before:
                    before(i)
                if i < 8:
                    h = i
                    dve.wait_ge(E("at_s_ps"), first_head(kind) + h + 1)
                    if h >= 2:
                        dve.wait_ge(E("at_e"), first_head(kind) + h - 1)
                    nc.vector.scalar_tensor_tensor(sc[:, h % 2, :], bank(s_bank + h % 2)[:, 0:SC], scale, mask, ALU.mult,
                                                   ALU.add).then_inc(E("at_sc"), 1)
                    dve.wait_ge(E("at_sc"), first_head(kind) + h + 1)
                    nc.vector.tensor_reduce(nmx[:, h % 2, 0:1], sc[:, h % 2, 0:P], AX_X, ALU.max, negate=True)
                    nc.vector.tensor_reduce(nmx[:, h % 2, 1:2], sc[:, h % 2, P:SC], AX_X, ALU.max,
                                            negate=True).then_inc(E("at_m"), 1)
                if i >= 1:
                    h = i - 1
                    dve.wait_ge(E("at_e"), first_head(kind) + h + 1)
                    link(nc.vector.reciprocal(rden[:, h % 2, :], den[:, h % 2, :]))
                    p = pr[:, h % 2, :]
                    nc.vector.tensor_scalar(p[:, 0:P], p[:, 0:P], rden[:, h % 2, 0:1], None, ALU.mult)
                    nc.vector.tensor_scalar(p[:, P:SC], p[:, P:SC], rden[:, h % 2, 1:2], None,
                                            ALU.mult).then_inc(E("at_p"), 1)
                if between:
                    between(i)

        def heads_act(act, link, kind, dst_of, src_of, per_evac, between=None, before=None):
            t_banks = HEAD_BANKS[kind][1]
            sc, pr, prT = (scor, prob, probT) if kind == "ev" else (m_scor, m_prob, m_probT)
            for i in range(8 + 2):
                if before:
                    before(i)
                if i < 8:
                    h = i
                    act.wait_ge(E("at_m"), first_head(kind) + h + 1)
                    if h >= 2:
                        act.wait_ge(E("at_t_ps"), first_head(kind) + h - 1)
                    nc.scalar.activation(pr[:, h % 2, 0:P], sc[:, h % 2, 0:P], ACT.Exp, bias=nmx[:, h % 2, 0:1],
                                         accum_out=den[:, h % 2, 0:1])
                    nc.scalar.activation(pr[:, h % 2, P:SC], sc[:, h % 2, P:SC], ACT.Exp, bias=nmx[:, h % 2, 1:2],
                                         accum_out=den[:, h % 2, 1:2]).then_inc(E("at_e"), 1)
                if 1 <= i <= 8:
                    h = i - 1
                    act.wait_ge(E("at_t_ps"), first_head(kind) + h + 1)
                    if h >= 2:
                        act.wait_ge(E("at_o_ps"), first_head(kind) + h - 1)
                    nc.scalar.activation(prT[:, h % 2, :], bank(t_banks[h % len(t_banks)])[:, 0:SC],
                                         ACT.Copy).then_inc(E("at_pT"), 1)
                if i >= 2 and (i - 2) % per_evac == per_evac - 1:
                    h = i - 2
                    act.wait_ge(E("at_o_ps"), first_head(kind) + h + 1)
                    nc.scalar.activation(dst_of(h // per_evac), src_of(h // per_evac),
                                         ACT.Copy).then_inc(E("at_o"), 1)
                if between:
                    between(i)

        def residual_dve(dve, name, before=0, first_bank=0):
            for t in range(NT):
                for n in range(2):
                    dve.wait_ge(E(name + "_ps"), before + 2 * t + n + 1)
                    v = x[:, t, n * BANK:(n + 1) * BANK]
                    nc.vector.tensor_tensor(v, v, bank(first_bank + n * NT + t), ALU.add).then_inc(E(name + "_add"), 1)

        W_IN_ORDER = (0, 1, 2, 4, 5, 3)
        CONV_FIRST, CONV_PAIRS = 2, 6

        def even_load(units):
            for n in W_IN_ORDER:
                units.load(view(units.slot(), DC, BANK),
                           w_in[0].rearrange("(p c) n -> p c n", c=DC)[:, :, n * BANK:(n + 1) * BANK])
            for n in range(2):
                units.load(view(units.slot(), 4, D), w_out[0].rearrange("(c p) n -> p c n", p=P)[:, 4 * n:4 * n + 4, :])

        Q_CONV, Q_OUT, Q_EVEN = 12, 24, 32

        def three_products(dst, lhs, rhs, start, stop):
            nc.tensor.matmul(dst, lhs[0], rhs[0], start=start, stop=False, skip_group_check=True)
            nc.tensor.matmul(dst, lhs[0], rhs[1], start=False, stop=False, skip_group_check=True)
            return nc.tensor.matmul(dst, lhs[1], rhs[0], start=False, stop=stop, skip_group_check=True)

        USED_EVEN = Q_EVEN - 1

        def rows_quarter(w, k, first):
            for t in range(NT):
                for c in range(2):
                    last = three_products(bank(first + t), [v[:, 2 * k + c, t * P:(t + 1) * P] for v in r_x],
                                          [v[:, c, :] for v in w], k == c == 0, k == 3 and c == 1)
            last.then_inc(E("q_used"), 1)

        def even_raw(units, q):
            if Q_CONV <= q < Q_OUT:
                return view(units.slot(), DC, BANK)[:, :, q % 4 * P:(q % 4 + 1) * P]
            return view(units.slot()[:, q % 4 * QUARTER:(q % 4 + 1) * QUARTER], DC, P)

        def even_rounds(act, units, first, end):
            for q in range(first, end):
                if q % 4 == 0:
                    units.wait()
                if q >= 2:
                    act.wait_ge(E("q_used"), q - 1)
                nc.scalar.activation(view(e_w[q % 2][0][:, :], DC, P), even_raw(units, q), ACT.Copy).then_inc(E("q_round"), 1)
                if q % 4 == 3:
                    units.n += 1

        def even_rests(dve, units, first, end):
            for q in range(first, end):
                dve.wait_ge(E("q_round"), q + 1)
                nc.vector.tensor_tensor(view(e_w[q % 2][1][:, :], DC, P), even_raw(units, q),
                                        view(e_w[q % 2][0][:, :], DC, P).bitcast(F32), ALU.subtract).then_inc(E("q_split"), 1)
                if q % 4 == 3:
                    dve.wait_ge(E("q_split"), q + 1)
                    dve.sem_inc(used, 1)
                    units.n += 1

        def even_pe(pe, units):
            def quarter(q, *shape):
                pe.wait_ge(E("q_split"), q + 1)
                return [view(v[:, :], *shape) for v in e_w[q % 2]]

            for q in range(Q_CONV):
                n, k = q // 4, q % 4
                if n == 0:
                    norm_bank(pe, 0, k)
                if n == 2 and k == 0:
                    pe.wait_ge(E("ev_qkv"), NT)
                rows_quarter(quarter(q, 2, BANK), k, 4 + 2 * (n % 2))

            def conv_chunk(i):
                pair = i // 2
                w = quarter(Q_CONV + i, DC, P)
                if i % 2 == 0 and pair >= 2:
                    pe.wait_ge(*((E("ev_gc"), pair - 1) if pair < 4 else (E("ev_z"), pair - 3)))
                for c in range(DC):
                    last = three_products(bank(pair % 2)[:, (i % 2) * S:(i % 2 + 1) * S], [v[:, c, :] for v in w],
                                          [v[:, c, :] for v in r_x], c == 0, c == DC - 1)
                last.then_inc(E("q_used"), 1)

            for i in range(2 * CONV_FIRST):
                conv_chunk(i)
            pe.wait_ge(E("ev_qkv"), 6)
            pe.wait_ge(E("ev_qkn"), NT)
            for half in range(2):
                for j in range(4):
                    for t in range(NT):
                        last = nc.tensor.transpose(
                            bank(4 + 2 * half + j // 2)[:, (j % 2) * S + t * P:(j % 2) * S + (t + 1) * P],
                            qk_t[:, t, half * BANK + j * P:half * BANK + (j + 1) * P], ident)
                last.then_inc(E("ev_qkT_ps"), 1)
            conv_chunk(2 * CONV_FIRST)
            pe.wait_ge(E("ev_qT"), 2)
            pe.wait_ge(E("ev_kT"), 2)

            def score(h, dst):
                a = A_DIM * (h % 2)
                q, k = qT[a:a + A_DIM, h // 2, :], kT[a:a + A_DIM, h // 2, :]
                nc.tensor.matmul(dst[:, 0:P], q[:, 0:P], k[:, 0:P], start=True, stop=True)
                return nc.tensor.matmul(dst[:, P:SC], q[:, P:S], k, start=True, stop=True)

            def between(i):
                if 2 * CONV_FIRST + 1 + i < 2 * CONV_PAIRS:
                    conv_chunk(2 * CONV_FIRST + 1 + i)

            heads_pe(pe, "ev", score, lambda h, t: v_t[:, t, h * A_DIM:(h + 1) * A_DIM],
                     lambda h: PS[A_DIM * (h % 2):A_DIM * (h % 2) + A_DIM, 2 + (h // 2) % 2, 0:S], 2, between)
            for q in range(Q_OUT, Q_EVEN):
                c = q - Q_OUT
                w = quarter(q, QUARTER)
                if c < 4:
                    pe.wait_ge(E("ev_lo"), c + 1)
                elif c == 4:
                    pe.wait_ge(E("ev_conv"), 1)
                mix = [mix_hi[:, c, :], mix_lo[c // 4][:, c % 4, :]]
                for t in range(NT):
                    for n in range(2):
                        last = three_products(bank(4 + n * NT + t), [v[:, t * P:(t + 1) * P] for v in mix],
                                              [v[:, n * BANK:(n + 1) * BANK] for v in w], c == 0, q == Q_EVEN - 1)
                        if q == Q_EVEN - 1:
                            last.then_inc(E("even_ps"), 1)
                if q < Q_EVEN - 1:
                    last.then_inc(E("q_used"), 1)
            units.n += EVEN_UNITS

        def even_act(act, units, link):
            done = 0

            def rounds(end):
                nonlocal done
                even_rounds(act, units, done, end)
                done = max(done, end)

            norm_act(act, link, 0, lambda: rounds(2))
            for n in range(3):
                rounds(4 * n + 6)
                act.wait_ge(E("q_used"), 4 * n + 4)
                for t in range(NT):
                    dst = v_t[:, t, :] if n == 2 else qk_t[:, t, n * BANK:(n + 1) * BANK]
                    if n < 2:
                        nc.scalar.activation(sq[t][:, n * BANK:(n + 1) * BANK], bank(4 + 2 * n + t), ACT.Square)
                    nc.scalar.activation(dst, bank(4 + 2 * (n % 2) + t), ACT.Copy).then_inc(E("ev_qkv"), 1)
            for b in range(2):
                rounds(Q_CONV + 2 * b + 4)
                act.wait_ge(E("q_used"), Q_CONV + 2 * b + 2)
                nc.scalar.activation(gcT[:, 2 * b:2 * b + 2, :], bank(b, 2, S), ACT.Copy).then_inc(E("ev_gc"), 1)
            act.wait_ge(E("ev_gqk"), 1)
            act.wait_ge(E("ev_qkT_ps"), 1)
            for b in range(2):
                nc.scalar.activation(qT[:, 2 * b:2 * b + 2, :], bank(4 + b, 2, S), ACT.Copy,
                                     scale=gqk).then_inc(E("ev_qT"), 1)

            def between(i):
                if i in (6, 8):
                    b = (i - 6) // 2
                    act.wait_ge(E("q_used"), Q_CONV + 8 + 2 * (b + 1))
                    nc.scalar.activation(gbT[:, 2 * b:2 * b + 2, :], bank(b, 2, S), ACT.Copy).then_inc(E("ev_gb"), 1)

            heads_act(act, link, "ev", lambda j: mix_hi[:, j, :], lambda j: bank(2 + j % 2)[:, 0:S], 2, between,
                      lambda i: rounds(min(Q_OUT + 2, Q_CONV + 2 * CONV_FIRST + 3 + i)))
            rounds(Q_EVEN)

        def even_pool(pool):
            pool.wait_ge(E("ev_hms"), 1)
            nc.gpsimd.tensor_tensor(hrstd, hms, view(C("minus_half"), NT, 2 * A_HEADS), ALU.pow).then_inc(E("ev_hr"), 1)

        def conv3(link, dst, src, taps, chunks):
            for j in chunks:
                link(nc.vector.tensor_scalar(dst[:, j, :], src[:, j, :], taps[:, 3 * j + 2:3 * j + 3], None, ALU.mult))
                for back in (1, 2):
                    link(nc.vector.scalar_tensor_tensor(dst[:, j, back:S], src[:, j, 0:S - back],
                                                        taps[:, 3 * j + 2 - back:3 * j + 3 - back],
                                                        dst[:, j, back:S], ALU.mult, ALU.add))

        def even_dve(dve, units, link):
            done = 0

            def rests(end):
                nonlocal done
                even_rests(dve, units, done, end)
                done = max(done, end)

            nc.vector.tensor_tensor(gqk, G("q_gain"), G("k_gain"), ALU.mult).then_inc(E("ev_gqk"), 1)
            norm_dve(dve, link, 0, lambda: rests(2))
            dve.wait_ge(E("const_in"), 16)
            rests(10)
            dve.wait_ge(E("ev_qkv"), 4)
            for t in range(NT):
                link(nc.vector.tensor_reduce(hss[:, t, :], view(sq[t], 16, A_DIM), AX_X, ALU.add))
                rests(11 + t)
            nc.vector.tensor_scalar(hms, hss, 1.0 / A_DIM, EPS, ALU.mult, ALU.add).then_inc(E("ev_hms"), 1)
            rests(13)
            dve.wait_ge(E("ev_hr"), 1)
            for t in range(NT):
                v = view(qk_t[:, t, :], 16, A_DIM)
                nc.vector.tensor_tensor(v, v, spread(hrstd[:, t, :], 16, A_DIM), ALU.mult).then_inc(E("ev_qkn"), 1)
                rests(14 + t)
            rests(18)
            dve.wait_ge(E("ev_qkT_ps"), 2)
            for b in range(2):
                nc.vector.tensor_copy(kT[:, 2 * b:2 * b + 2, :], bank(6 + b, 2, S)).then_inc(E("ev_kT"), 1)

            def split_heads(j):
                dve.wait_ge(E("at_o"), j + 1)
                nc.vector.tensor_tensor(mix_lo[0][:, j, :], bank(2 + j % 2)[:, 0:S], mix_hi[:, j, :].bitcast(F32),
                                        ALU.subtract).then_inc(E("ev_lo"), 1)

            def between(i):
                if i in (4, 6, 8):
                    split_heads(i // 2 - 2)
                if i in (2, 4):
                    b = (i - 2) // 2
                    dve.wait_ge(E("ev_gc"), b + 1)
                    dve.wait_ge(E("q_used"), Q_CONV + 4 + 2 * (b + 1))
                    nc.vector.tensor_tensor(zT[:, 2 * b:2 * b + 2, :], gcT[:, 2 * b:2 * b + 2, :], bank(b, 2, S),
                                            ALU.mult).then_inc(E("ev_z"), 1)
                    dve.wait_ge(E("ev_z"), b + 1)
                if 2 <= i < 6:
                    conv3(link, convt, zT, G("sconv"), [i - 2])

            heads_dve(dve, link, "ev", C("dil_mask"), A_DIM ** -0.5, between,
                      lambda i: rests(min(Q_OUT + 2, Q_CONV + 2 * CONV_FIRST + 3 + i)))
            split_heads(3)
            rests(Q_OUT + 3)
            dve.wait_ge(E("ev_gb"), 2)
            link(nc.vector.tensor_tensor(convt, convt, gbT, ALU.mult))
            rests(Q_OUT + 4)
            link(nc.vector.tensor_copy(mix_hi[:, 4:8, :], convt))
            nc.vector.tensor_tensor(mix_lo[1][:, :, :], convt, mix_hi[:, 4:8, :].bitcast(F32), ALU.subtract).then_inc(E("ev_conv"), 1)
            dve.wait_ge(E("ev_conv"), 1)
            rests(Q_EVEN)
            ffn_first_dve(dve, units, 0, GATE)
            residual_dve(dve, "even", first_bank=4)

        IN_LOOP = 3
        LOOP_TURNS = (N_SLABS - 2) // IN_LOOP
        assert 2 + IN_LOOP * LOOP_TURNS == N_SLABS
        GATE, VALUE, DOWN = range(3)

        def ffn_load(sp, units, l):
            up = w_up[l].rearrange("(p c) (g n) -> p c g n", c=DC, g=2)
            down = w_down[l].rearrange("(c p) n -> p c n", p=P)

            def load_up(at):
                units.load(view(units.slot(), DC, 2, SLAB), up[:, :, :, bass.ds(at, SLAB)])

            def load_down(at):
                units.load(view(units.slot()[:, 0:2 * D], 2, D), down[:, bass.ds(at, 2), :])

            load_up(0)
            load_up(SLAB)
            load_down(0)
            with sp.Fori(0, LOOP_TURNS) as turn:
                units.loop(turn, SLOTS)
                for j in range(IN_LOOP):
                    load_up(turn * (IN_LOOP * SLAB) + (2 + j) * SLAB)
                    load_down(turn * (IN_LOOP * 2) + (1 + j) * 2)
                units.done(LOOP_TURNS)
            load_down(2 * (N_SLABS - 1))

        SPLITS = 3 * N_SLABS

        def split_count(l, kind, s):
            if isinstance(s, int) and s == 0 and kind != DOWN:
                return l * SPLITS + 1 + kind
            if kind == DOWN:
                last = isinstance(s, int) and s == N_SLABS - 1
                return l * SPLITS + (SPLITS if last else 3 * s + 5)
            return l * SPLITS + 3 * s + kind

        def ffn_pe(pe, units, l):
            s0 = l * N_SLABS

            def up(s):
                for kind in (GATE, VALUE):
                    pe.wait_ge(E("ffn_split"), split_count(l, kind, s))
                    w = [view(f_w[kind][i][:, :], DC, SLAB) for i in range(2)]
                    for j in range(2):
                        m = 2 * kind + j
                        if l > 0 or not isinstance(s, int) or s > 0:
                            pe.wait_ge(E("ffn_u"), 4 * (s0 + s))
                        for c in range(DC):
                            if m == 0 and c % 2 == 0 and isinstance(s, int) and s == 0:
                                norm_bank(pe, 1 + 2 * l, c // 2)
                            last = three_products(bank(4 + m)[:, 0:S], [v[:, c, j * P:(j + 1) * P] for v in w],
                                                  [v[:, c, :] for v in f_x], c == 0, c == DC - 1)
                        last.then_inc(E("ffn_u_ps"), 1)

            def down(s, start=False, stop=False):
                pe.wait_ge(E("ffn_split"), split_count(l, DOWN, s))
                pe.wait_ge(E("ffn_h"), 1 + s0 + s + 1)
                w = [view(f_w[GATE if stop else DOWN][i][:, :], 2, D) for i in range(2)]
                for t in range(NT):
                    for n in range(2):
                        for c in range(2):
                            last = three_products(bank(n * NT + t), [v[:, c, t * P:(t + 1) * P] for v in f_h],
                                                  [v[:, c, n * BANK:(n + 1) * BANK] for v in w],
                                                  start and c == 0, stop and c == 1)
                        if stop:
                            last.then_inc(E("ffn_ps"), 1)
                if not stop:
                    last.then_inc(E("ffn_d"), 1)

            if l == 0:
                pe.sem_inc(E("ffn_d"), 1)
            up(0)
            up(1)
            down(0, start=True)
            with pe.Fori(2, N_SLABS) as s:
                up(s)
                down(s - 1)
            down(N_SLABS - 1, stop=True)
            units.n += 2 * N_SLABS

        def raw_half(kind, slot):
            if kind == DOWN:
                return view(slot[:, 0:HALF], DC, SLAB)
            return view(slot, DC, 2, SLAB)[:, :, kind, :]

        def ffn_slabs(eng, units, slab, link=None, links=0):
            slab(0)
            with eng.Fori(0, LOOP_TURNS) as turn:
                units.loop(turn, SLOTS)
                if link:
                    link.loop(turn, IN_LOOP * links)
                for j in range(IN_LOOP):
                    slab(turn * IN_LOOP + (1 + j))
                units.done(LOOP_TURNS)
                if link:
                    link.done(LOOP_TURNS)
            slab(N_SLABS - 1)

        def round_half(kind, slot, into=None):
            nc.scalar.activation(view(f_w[kind if into is None else into][0][:, :], DC, SLAB), raw_half(kind, slot),
                                 ACT.Copy).then_inc(E("ffn_round"), 1)

        def ffn_first_act(act, units, l, kind):
            if kind == GATE:
                act.wait_ge(*((E("at_o_ps"), 8) if l == 0 else (E("q_used"), USED_EVEN + 4 * RET_UNITS - 4)))
                units.wait()
            else:
                act.wait_ge(E("even_ps" if l == 0 else "ret_ps"), 2 * NT)
            round_half(kind, units.slot())
            if kind == VALUE:
                units.n += 1

        def ffn_act(act, units, l):
            s0 = l * N_SLABS

            def newest(s, m):
                act.wait_ge(E("ffn_cw"), s0 + s + 1)
                act.wait_ge(E("ffn_u_ps"), 4 * (s0 + s) + m + 1)
                act.wait_ge(E("ffn_h"), 1 + s0 + s)
                nc.scalar.activation(f_u[:, m, :], bank(4 + m)[:, 0:S], ACT.Copy,
                                     scale=f_cw[:, 3 * m + 2:3 * m + 3]).then_inc(E("ffn_t"), 1)


            def slab(s):
                last = isinstance(s, int) and s == N_SLABS - 1
                for kind in (GATE, VALUE):
                    for j in range(2):
                        newest(s, 2 * kind + j)
                    if kind == GATE:
                        units.wait()
                    if not last:
                        round_half(kind, units.slot())
                    elif kind == GATE:
                        round_half(DOWN, units.slot(), into=GATE)
                        units.n += 1
                act.wait_ge(E("ffn_u"), 4 * (s0 + s) + 2)
                nc.scalar.activation(f_u[:, 0:2, :], f_u[:, 0:2, :], ACT.Silu).then_inc(E("ffn_g"), 1)
                if not last:
                    units.n += 1
                    units.wait()
                    act.wait_ge(E("ffn_d"), 1 + s0 - l + s)
                    round_half(DOWN, units.slot())
                    units.n += 1

            ffn_slabs(act, units, slab)

        def rest_half(dve, l, kind, s, slot, into=None):
            hi, lo = f_w[kind if into is None else into]
            dve.wait_ge(E("ffn_round"), split_count(l, kind, s))
            nc.vector.tensor_tensor(view(lo[:, :], DC, SLAB), raw_half(kind, slot), view(hi[:, :], DC, SLAB).bitcast(F32),
                                    ALU.subtract).then_inc(E("ffn_split"), 1)

        def give_back(dve, units, l, kind, s):
            dve.wait_ge(E("ffn_split"), split_count(l, kind, s))
            dve.sem_inc(used, 1)
            units.n += 1

        def ffn_first_dve(dve, units, l, kind):
            rest_half(dve, l, kind, 0, units.slot())
            if kind == VALUE:
                give_back(dve, units, l, VALUE, 0)

        FFN_LINKS = 7

        def ffn_dve(dve, units, link, l):
            s0 = l * N_SLABS
            taps = G(f"conv{l}")

            def conv(s, m):
                dve.wait_ge(E("ffn_t"), 4 * (s0 + s) + m + 1)
                u = bank(4 + m)
                link(nc.vector.scalar_tensor_tensor(f_u[:, m, 1:S], u[:, 0:S - 1], f_cw[:, 3 * m + 1:3 * m + 2],
                                                    f_u[:, m, 1:S], ALU.mult, ALU.add))
                nc.vector.scalar_tensor_tensor(f_u[:, m, 2:S], u[:, 0:S - 2], f_cw[:, 3 * m:3 * m + 1],
                                               f_u[:, m, 2:S], ALU.mult, ALU.add).then_inc(E("ffn_u"), 1)

            def slab(s):
                last = isinstance(s, int) and s == N_SLABS - 1
                link(nc.vector.tensor_copy(f_cw, taps[:, bass.ds(s * 12, 12)]))
                dve.sem_inc(E("ffn_cw"), 1)
                for kind in (GATE, VALUE):
                    for j in range(2):
                        conv(s, 2 * kind + j)
                    if not last:
                        rest_half(dve, l, kind, s + 1, units.slot())
                    elif kind == GATE:
                        rest_half(dve, l, DOWN, s, units.slot(), into=GATE)
                        give_back(dve, units, l, DOWN, s)
                if not last:
                    give_back(dve, units, l, VALUE, s + 1)
                dve.wait_ge(E("ffn_u"), 4 * (s0 + s) + 4)
                dve.wait_ge(E("ffn_g"), s0 + s + 1)
                link(nc.vector.tensor_tensor(f_u[:, 0:2, :], f_u[:, 0:2, :], f_u[:, 2:4, :], ALU.mult))
                dve.wait_ge(E("ffn_d"), 1 + s0 - l + s)
                link(nc.vector.tensor_copy(f_h[0][:, :, :], f_u[:, 0:2, :]))
                nc.vector.tensor_tensor(f_h[1][:, :, :], f_u[:, 0:2, :], f_h[0][:, :, :].bitcast(F32),
                                        ALU.subtract).then_inc(E("ffn_h"), 1)
                if not last:
                    rest_half(dve, l, DOWN, s, units.slot())
                    give_back(dve, units, l, DOWN, s)

            if l == 0:
                dve.sem_inc(E("ffn_h"), 1)
            ffn_slabs(dve, units, slab, link, FFN_LINKS)
            if l == 0:
                rest_quarters(dve, units, 0, EARLY)
            residual_dve(dve, "ffn", 4 * l)

        RET_UNITS = 16
        EARLY = 2
        Q_V, Q_G, Q_O, Q_END = 16, 32, 48, 64

        def ret_load(units):
            for w, n_slabs in ((wq, 2), (wk, 2), (wv, 4), (wg, 4)):
                for n in range(n_slabs):
                    units.load(view(units.slot(), DC, BANK),
                               w[0].rearrange("(p c) n -> p c n", c=DC)[:, :, n * BANK:(n + 1) * BANK])
            for n in range(4):
                units.load(view(units.slot(), 4, D), wo_r[0].rearrange("(c p) n -> p c n", p=P)[:, 4 * n:4 * n + 4, :])

        def raw_quarter(units, q):
            return units.slot()[:, q % 4 * QUARTER:(q % 4 + 1) * QUARTER]

        def round_quarters(act, units, first, end):
            for q in range(first, end):
                if q % 4 == 0:
                    units.wait()
                if q >= 3:
                    act.wait_ge(E("q_used"), USED_EVEN + q - 2)
                nc.scalar.activation(r_w[q % 3][0][:, :], raw_quarter(units, q), ACT.Copy).then_inc(E("q_round"), 1)
                if q % 4 == 3:
                    units.n += 1

        def rest_quarters(dve, units, first, end):
            for q in range(first, end):
                dve.wait_ge(E("q_round"), Q_EVEN + q + 1)
                nc.vector.tensor_tensor(r_w[q % 3][1][:, :], raw_quarter(units, q), r_w[q % 3][0][:, :].bitcast(F32),
                                        ALU.subtract).then_inc(E("q_split"), 1)
                if q % 4 == 3:
                    dve.wait_ge(E("q_split"), Q_EVEN + q + 1)
                    dve.sem_inc(used, 1)
                    units.n += 1

        def ret_pe(pe, units):
            def quarter(q, *shape):
                pe.wait_ge(E("q_split"), Q_EVEN + q + 1)
                return [view(v[:, :], *shape) for v in r_w[q % 3]]

            for q in range(Q_V):
                n, k = q // 4, q % 4
                w = quarter(q, 2, BANK)
                if n == 0:
                    norm_bank(pe, 2, k)
                if n >= 2 and k == 0:
                    pe.wait_ge(E("rt_ro"), 2 * (n - 1))
                for c in range(2):
                    for m in range(4):
                        dst = bank(4 - 4 * (n % 2) + m)[:, 0:S]
                        last = three_products(dst, [v[:, c, m * P:(m + 1) * P] for v in w], [v[:, 2 * k + c, :] for v in r_x],
                                              k == c == 0, k == 3 and c == 1)
                last.then_inc(E("q_used"), 1)

            for h in range(RET_HEADS):
                if h >= 2:
                    pe.wait_ge(E("rt_v"), NT * (h - 1))
                else:
                    pe.wait_ge(E("rt_ro"), 5 + h)
                for k in range(4):
                    rows_quarter(quarter(Q_V + 4 * h + k, 2, BANK), k, 4 + 2 * (h % 2))
            pe.wait_ge(E("rt_ro"), 8)
            pe.wait_ge(E("rt_v"), 8)

            def turn_back(h):
                pe.wait_ge(E("rt_y"), NT * (h + 1))
                for t in range(NT):
                    for c in range(4):
                        last = nc.tensor.transpose(bank(6 + c // 2)[:, (c % 2) * S + t * P:(c % 2) * S + (t + 1) * P],
                                                   r_y[:, t, c * P:(c + 1) * P], ident)
                last.then_inc(E("rt_yT_ps"), 1)

            for h in range(RET_HEADS):
                if h >= 1:
                    pe.wait_ge(E("rt_dec"), h)
                for cc in range(2):
                    nc.tensor.matmul(bank(2)[:, 0:S], r_k[h][:, cc, 0:P], r_q[h][:, cc, :], start=(cc == 0), stop=(cc == 1))
                for cc in range(2):
                    last = nc.tensor.matmul(bank(2)[:, S:SC], r_k[h][:, cc, P:S], r_q[h][:, cc, P:S],
                                            start=(cc == 0), stop=(cc == 1))
                last.then_inc(E("rt_s_ps"), 1)
                if h >= 1:
                    pe.wait_ge(E("rt_sg"), NT * h)
                for k in range(4):
                    rows_quarter(quarter(Q_G + 4 * h + k, 2, BANK), k, 0)
                if h >= 1:
                    if h >= 2:
                        pe.wait_ge(E("rt_yT"), 2 * h - 2)
                    turn_back(h - 1)
                    pe.wait_ge(E("rt_on"), NT * h)
                pe.wait_ge(E("rt_dec"), h + 1)
                v = [r_v[h][:, t, :] for t in range(NT)]
                nc.tensor.matmul(bank(4), r_sT[:, 0:P], v[0], start=True, stop=True).then_inc(E("rt_o_ps"), 1)
                nc.tensor.matmul(bank(5), r_sT[:, P:S], v[0], start=True, stop=False)
                nc.tensor.matmul(bank(5), r_sT[:, S:SC], v[1], start=False, stop=True).then_inc(E("rt_o_ps"), 1)
            pe.wait_ge(E("rt_sg"), NT * RET_HEADS)
            for q in range(Q_O, Q_END):
                n, c = (q - Q_O) // 4, q % 4
                if q == Q_END - 4:
                    pe.wait_ge(E("rt_yT"), 2 * n)
                    turn_back(n)
                if c == 0:
                    pe.wait_ge(E("rt_yT"), 2 * (n + 1))
                w = quarter(q, QUARTER)
                for t in range(NT):
                    for m in range(2):
                        last = three_products(bank(m * NT + t), [v[:, c, t * P:(t + 1) * P] for v in r_yT[n]],
                                              [v[:, m * BANK:(m + 1) * BANK] for v in w], q == Q_O, q == Q_END - 1)
                        if q == Q_END - 1:
                            last.then_inc(E("ret_ps"), 1)
                if q < Q_END - 1:
                    last.then_inc(E("q_used"), 1)
            units.n += RET_UNITS

        def ret_first_act(act, units):
            act.wait_ge(E("ffn_d"), 1 + (N_SLABS - 1))
            round_quarters(act, units, 0, EARLY)

        def ret_act(act, units):
            done = EARLY

            def rounds(end):
                nonlocal done
                round_quarters(act, units, done, end)
                done = end

            def turned_back(h):
                act.wait_ge(E("rt_yT_ps"), h + 1)
                for b in range(2):
                    for c in (2 * b, 2 * b + 1):
                        last = nc.scalar.activation(r_yT[h][0][:, c, :], bank(6 + b)[:, (c % 2) * S:(c % 2 + 1) * S], ACT.Copy,
                                                    scale=G("gn")[:, 4 * h + c:4 * h + c + 1])
                    last.then_inc(E("rt_yh"), 1)

            for h in range(RET_HEADS):
                rounds(Q_V + 4 * h + 7)
                act.wait_ge(E("q_used"), USED_EVEN + Q_V + 4 * h + 4)
                for t in range(NT):
                    nc.scalar.activation(r_v[h][:, t, :], bank(4 + 2 * (h % 2) + t), ACT.Copy).then_inc(E("rt_v"), 1)
            act.wait_ge(E("rt_ro"), 8)
            for h in range(RET_HEADS):
                rounds(Q_G + 4 * h + 7)
                act.wait_ge(E("q_used"), USED_EVEN + Q_G + 4 * h + 4)
                if h >= 1:
                    act.wait_ge(E("rt_yT_ps"), h)
                for t in range(NT):
                    nc.scalar.activation(r_y[:, t, :], bank(t), ACT.Silu).then_inc(E("rt_sg"), 1)
                if h >= 1:
                    turned_back(h - 1)
            rounds(Q_END - 2)
            turned_back(RET_HEADS - 1)
            rounds(Q_END)

        def ret_pool(pool):
            for h in range(RET_HEADS):
                pool.wait_ge(E("rt_var"), h + 1)
                nc.gpsimd.tensor_tensor(grstd, gvar, C("minus_half")[:, 0:NT], ALU.pow).then_inc(E("rt_rstd"), 1)

        def ret_dve(dve, units, link):
            done = EARLY

            def rests(end):
                nonlocal done
                rest_quarters(dve, units, done, end)
                done = end

            for i in range(8):
                if i % 2 == 0:
                    rests(2 * i + 7)
                    dve.wait_ge(E("q_used"), USED_EVEN + 2 * i + 4)
                dst = (r_q if i < 4 else r_k)[i % 4]
                b = 4 - 4 * (i // 2 % 2) + 2 * (i % 2)
                src = PS[:, b:b + 2, 0:S]
                cos = C("r_cos").unsqueeze(1).to_broadcast([P, 2, S])
                sin = C("r_sin").unsqueeze(1).to_broadcast([P, 2, S])
                link(nc.vector.tensor_tensor(rope_c, src, cos, ALU.mult))
                link(nc.vector.tensor_tensor(rope_s, src, sin, ALU.mult))
                link(nc.vector.tensor_tensor(dst[:, 0, :], rope_c[:, 0, :], rope_s[:, 1, :], ALU.subtract))
                nc.vector.tensor_tensor(dst[:, 1, :], rope_s[:, 0, :], rope_c[:, 1, :], ALU.add).then_inc(E("rt_ro"), 1)
                dve.wait_ge(E("rt_ro"), i + 1)

            def turned_back(h):
                for b in range(2):
                    dve.wait_ge(E("rt_yh"), 2 * h + b + 1)
                    for c in (2 * b, 2 * b + 1):
                        last = nc.vector.scalar_tensor_tensor(
                            r_yT[h][1][:, c, :], bank(6 + b)[:, (c % 2) * S:(c % 2 + 1) * S], G("gn")[:, 4 * h + c:4 * h + c + 1],
                            r_yT[h][0][:, c, :].bitcast(F32), ALU.mult, ALU.subtract)
                    last.then_inc(E("rt_yT"), 1)

            rests(Q_G + 3)
            dve.wait_ge(E("decay_in"), 16)
            for h in range(RET_HEADS):
                dve.wait_ge(E("rt_s_ps"), h + 1)
                if h >= 1:
                    dve.wait_ge(E("rt_o_ps"), NT * h)
                nc.vector.tensor_tensor(r_sT, bank(2)[:, 0:SC], decay[:, h, :], ALU.mult).then_inc(E("rt_dec"), 1)
                rests(Q_G + 4 * h + 6)
                if h >= 1:
                    turned_back(h - 1)
                rests(Q_G + 4 * h + 7)
                for t in range(NT):
                    dve.wait_ge(E("rt_o_ps"), NT * h + t + 1)
                    link(nc.vector.bn_stats(stats[:, t, :], bank(4 + t)))
                    link(nc.vector.bn_aggr(mv[:, t, :], stats[:, t, :]))
                nc.vector.tensor_scalar(gvar, mv[:, :, 1], EPS, None, ALU.add).then_inc(E("rt_var"), 1)
                for t in range(NT):
                    dve.wait_ge(E("rt_sg"), NT * h + t + 1)
                    nc.vector.scalar_tensor_tensor(r_y[:, t, :], bank(4 + t), mv[:, t, 0:1], r_y[:, t, :], ALU.subtract,
                                                   ALU.mult).then_inc(E("rt_on"), 1)
                dve.wait_ge(E("rt_rstd"), h + 1)
                for t in range(NT):
                    dve.wait_ge(E("rt_on"), NT * h + t + 1)
                    nc.vector.tensor_scalar(r_y[:, t, :], r_y[:, t, :], grstd[:, t:t + 1], None, ALU.mult).then_inc(E("rt_y"), 1)
            rests(Q_END - 2)
            turned_back(RET_HEADS - 1)
            rests(Q_END)
            ffn_first_dve(dve, units, 1, GATE)
            residual_dve(dve, "ret")

        def pool_load(units):
            units.load(view(units.slot()[:, 0:2 * D], 8, 256), pool_w[0].rearrange("g (c p) n -> p (g c) n", p=P))

        def pool_dve(dve, link):
            dve.wait_ge(E("rows_in"), 16)
            link(nc.vector.tensor_tensor(pl_bs, R("pool_b"), R("pool_scale"), ALU.mult))
            for t in range(NT):
                link(nc.vector.tensor_tensor(x[:, t, :], x[:, t, :], pl_bs, ALU.add))
            for t in range(NT):
                dve.wait_ge(E("pl_ps"), t + 1)
                if t == NT - 1:
                    dve.sem_inc(used, 1)
                y = pl_y[:, t, :]
                link(nc.vector.tensor_tensor(view(y, 2, BANK), PS[:, 4 + 2 * t:6 + 2 * t, :], view(R("pool_scale"), 2, BANK),
                                             ALU.mult))
                nc.vector.tensor_tensor(x[:, t, :], x[:, t, :], y, ALU.add).then_inc(E("pool_add"), 1)

        def pool_pe(pe, units):
            norm_done(pe, 4)
            units.wait()
            w = view(units.slot()[:, 0:2 * D], 8, 256)
            for t in range(NT):
                for g in range(4):
                    dst = bank(4 + 2 * t + g // 2)[:, (g % 2) * 256:(g % 2 + 1) * 256]
                    for c in range(2):
                        last = nc.tensor.matmul(dst, xnT[:, 2 * g + c, t * P:(t + 1) * P], w[:, 2 * g + c, :],
                                                start=(c == 0), stop=(c == 1))
                last.then_inc(E("pl_ps"), 1)
            units.n += 1

        def mla_load(units):
            units.load(view(units.slot()[:, 0:DC * 320], DC, 320), w_dkv.rearrange("(p c) n -> p c n", c=DC))
            units.load(view(units.slot()[:, 0:DC * Q_RANK], DC, Q_RANK), wq_down[0].rearrange("(p c) n -> p c n", c=DC))
            units.load(view(units.slot()[:, 0:2 * D], 2, D), w_uk.rearrange("(c p) n -> p c n", p=P))
            units.load(view(units.slot()[:, 0:2 * D], 2, D), w_uv.rearrange("(c p) n -> p c n", p=P))
            for n in range(2):
                units.load(view(units.slot()[:, 0:3 * 768], 3, 768),
                           wq_up[0].rearrange("(c p) n -> p c n", p=P)[:, :, n * 768:(n + 1) * 768])
            for n in range(2):
                units.load(view(units.slot(), 4, D), wo_m[0].rearrange("(c p) n -> p c n", p=P)[:, 4 * n:4 * n + 4, :])

        def mla_pe(pe, units):
            units.wait()
            w = view(units.slot()[:, 0:DC * 320], DC, 320)
            for t in range(NT):
                for c in range(DC):
                    if t == 0 and c % 2 == 0:
                        norm_bank(pe, 6, c // 2)
                    last = nc.tensor.matmul(bank(4 + t)[:, 0:320], xkvT[:, c, t * P:(t + 1) * P], w[:, c, :],
                                            start=(c == 0), stop=(c == DC - 1))
                last.then_inc(E("ml_kv_ps"), 1)
            units.n += 1
            norm_done(pe, 6)
            units.wait()
            w = view(units.slot()[:, 0:DC * Q_RANK], DC, Q_RANK)
            for t in range(NT):
                last = rows_of(bank(6 + t)[:, 0:Q_RANK], tile_of(xnT, t), lambda c: w[:, c, :], DC)
                last.then_inc(E("ml_q_ps"), 1)
            units.n += 1
            pe.wait_ge(E("ml_lat"), NT)
            pe.wait_ge(E("ml_kr"), NT)
            for t in range(NT):
                for c in range(2):
                    nc.tensor.transpose(bank(0)[:, c * S + t * P:c * S + (t + 1) * P], ckv[:, t, c * P:(c + 1) * P], ident)
                last = nc.tensor.transpose(bank(1)[:, t * P:(t + 1) * P], kr2[:, t, :], ident)
            last.then_inc(E("ml_t_ps"), 1)
            pe.wait_ge(E("ml_t"), 2)
            units.wait()
            w = view(units.slot()[:, 0:2 * D], 2, D)
            for h in range(M_HEADS):
                if h >= 4 and h % 2 == 0:
                    pe.wait_ge(E("ml_kn"), h // 2 - 1)
                last = rows_of(bank((h // 2) % 2)[:, (h % 2) * S:(h % 2 + 1) * S],
                               lambda c: w[:, c, h * P:(h + 1) * P], lambda c: ckvT[:, c, :], 2)
                if h % 2:
                    last.then_inc(E("ml_kn_ps"), 1)
            units.n += 1
            pe.wait_ge(E("ml_lat"), 2 * NT)
            for t in range(NT):
                for c in range(3):
                    last = nc.tensor.transpose(bank(2 + c // 2)[:, (c % 2) * S + t * P:(c % 2) * S + (t + 1) * P],
                                               cq[:, t, c * P:(c + 1) * P], ident)
            last.then_inc(E("ml_t_ps"), 1)
            units.wait()
            w = view(units.slot()[:, 0:2 * D], 2, D)
            for t in range(NT):
                for n in range(2):
                    last = rows_of(bank(4 + 2 * t + n), tile_of(ckvT, t), lambda c: w[:, c, n * BANK:(n + 1) * BANK], 2)
                    last.then_inc(E("ml_v_ps"), 1)
            units.n += 1
            pe.wait_ge(E("ml_v"), 2)
            pe.wait_ge(E("ml_t"), 3)
            for n in range(2):
                units.wait()
                w = view(units.slot()[:, 0:3 * 768], 3, 768)
                wh = w.rearrange("p c (h d) -> p c h d", h=4)
                for t in range(NT):
                    last = rows_of(view(bank(4 + t)[:, n * S:(n + 1) * S], 4, M_ROPE), tile_of(cqT, t),
                                   lambda c: wh[:, c, :, M_NOPE:], 3)
                    if n == 1:
                        last.then_inc(E("ml_qr_ps"), 1)
                for j in range(4):
                    h = 4 * n + j
                    if j % 2 == 0:
                        if h >= 4:
                            pe.wait_ge(E("ml_qn"), h // 2 - 1)
                        else:
                            pe.wait_ge(E("ml_kn"), 3 + h // 2)
                    last = rows_of(bank((h // 2) % 2)[:, (h % 2) * S:(h % 2 + 1) * S],
                                   lambda c: wh[:, c, j, 0:M_NOPE], lambda c: cqT[:, c, :], 3)
                    if j % 2:
                        last.then_inc(E("ml_qn_ps"), 1)
                units.n += 1
            pe.wait_ge(E("ml_qr"), NT)
            for j in range(4):
                for t in range(NT):
                    last = nc.tensor.transpose(bank(2 + j // 2)[:, (j % 2) * S + t * P:(j % 2) * S + (t + 1) * P],
                                               qr[:, t, j * P:(j + 1) * P], ident)
            last.then_inc(E("ml_qrT_ps"), 1)
            pe.wait_ge(E("ml_qrT"), 2)
            pe.wait_ge(E("ml_qn"), 4)
            pe.wait_ge(E("ml_v"), 4)

            def score(h, dst):
                a = M_ROPE * (h % 2)
                q2, k2 = qrT[a:a + M_ROPE, h // 2, :], krT[a:a + M_ROPE, :]
                nc.tensor.matmul(dst[:, 0:P], qnT[:, h, 0:P], knT[:, h, 0:P], start=True, stop=False)
                nc.tensor.matmul(dst[:, 0:P], q2[:, 0:P], k2[:, 0:P], start=False, stop=True)
                nc.tensor.matmul(dst[:, P:SC], qnT[:, h, P:S], knT[:, h, :], start=True, stop=False)
                return nc.tensor.matmul(dst[:, P:SC], q2[:, P:S], k2, start=False, stop=True)

            def project(h):
                pe.wait_ge(E("ml_lo"), h + 1)
                pe.wait_ge(E("q_split"), Q_MLA + h + 1)
                for t in range(NT):
                    for n in range(2):
                        last = three_products(bank(4 + n * NT + t), [v[:, h % 2, t * P:(t + 1) * P] for v in m_aT],
                                              [v[:, n * BANK:(n + 1) * BANK] for v in m_w[h % 2]], h == 0, h == M_HEADS - 1)
                        if h == M_HEADS - 1:
                            last.then_inc(E("mla_ps"), 1)
                if h < M_HEADS - 1:
                    last.then_inc(E("q_used"), 1)

            heads_pe(pe, "ml", score, lambda h, t: m_v[:, t, h * M_V:(h + 1) * M_V], lambda h: bank(3)[:, 0:S], 1,
                     lambda i: project(i - 3) if i >= 3 else None)
            project(M_HEADS - 1)
            units.n += 2

        Q_MLA = Q_EVEN + Q_END
        MLA_BEFORE = 1 + 6 * N_PAIRS - len(extra) + 6
        USED_MLA = Q_MLA - 2

        def raw_head(units, h):
            return units.slot(h // 4)[:, h % 4 * QUARTER:(h % 4 + 1) * QUARTER]

        def mla_act(act, units, link):
            units.n += MLA_BEFORE

            def project(i):
                h = i - 2
                if h >= 0:
                    if h % 4 == 0:
                        units.wait(h // 4)
                    if h >= 2:
                        act.wait_ge(E("q_used"), USED_MLA + h - 1)
                    nc.scalar.activation(m_w[h % 2][0][:, :], raw_head(units, h), ACT.Copy).then_inc(E("q_round"), 1)

            for j, (ps, first, n) in enumerate((("ml_kv_ps", 4, KV_RANK), ("ml_q_ps", 6, Q_RANK))):
                for t in range(NT):
                    act.wait_ge(E(ps), t + 1)
                    if t == NT - 1:
                        act.sem_inc(used, 1)
                    link(nc.scalar.activation(m_sq[:, 0:n], bank(first + t)[:, 0:n], ACT.Square, accum_out=hss[:, t, j:j + 1]))
                    nc.scalar.activation(hms[:, t, j:j + 1], hss[:, t, j:j + 1], ACT.Copy, bias=EPS,
                                         scale=1.0 / n).then_inc(E("ml_ms"), 1)
            act.wait_ge(E("ml_t_ps"), 1)
            for c in range(2):
                last = nc.scalar.activation(ckvT[:, c, :], bank(0)[:, c * S:(c + 1) * S], ACT.Copy, scale=G("kv_norm")[:, c:c + 1])
            last.then_inc(E("ml_t"), 1)
            nc.scalar.activation(krT, bank(1)[:, 0:S], ACT.Copy).then_inc(E("ml_t"), 1)
            for j in range(4):
                act.wait_ge(E("ml_kn_ps"), j + 1)
                if j == 3:
                    act.sem_inc(used, 1)
                nc.scalar.activation(knT[:, 2 * j:2 * j + 2, :], bank(j % 2, 2, S), ACT.Copy).then_inc(E("ml_kn"), 1)
            act.wait_ge(E("ml_t_ps"), 2)
            for c in range(3):
                last = nc.scalar.activation(cqT[:, c, :], bank(2 + c // 2)[:, (c % 2) * S:(c % 2 + 1) * S], ACT.Copy,
                                            scale=G("q_norm")[:, c:c + 1])
            last.then_inc(E("ml_t"), 1)
            act.wait_ge(E("ml_v_ps"), 4)
            act.sem_inc(used, 1)
            for j in range(4):
                act.wait_ge(E("ml_qn_ps"), j + 1)
                if j % 2:
                    act.sem_inc(used, 1)
                nc.scalar.activation(qnT[:, 2 * j:2 * j + 2, :], bank(j % 2, 2, S), ACT.Copy).then_inc(E("ml_qn"), 1)
            heads_act(act, link, "ml", lambda h: m_aT[0][:, h % 2, :], lambda h: bank(3)[:, 0:S], 1, None, project)

        def mla_pool(pool):
            for j in range(2):
                for t in range(NT):
                    pool.wait_ge(E("ml_ms"), NT * j + t + 1)
                    nc.gpsimd.tensor_tensor(hrstd[:, t, j:j + 1], hms[:, t, j:j + 1], C("minus_half")[:, 0:1],
                                            ALU.pow).then_inc(E("ml_rstd"), 1)

        def turn_rows(link, dst, src, t, n):
            half = M_ROPE // 2
            cos = view(C("m_cos"), NT, half)[:, t, :].unsqueeze(1).to_broadcast([P, n, half])
            sin = view(C("m_sin"), NT, half)[:, t, :].unsqueeze(1).to_broadcast([P, n, half])
            a, b = src[:, :, 0:half], src[:, :, half:]
            u = view(m_scor.rearrange("p a b -> p (a b)")[:, 0:n * half], n, half)
            link(nc.vector.tensor_tensor(dst[:, :, 0:half], a, cos, ALU.mult))
            link(nc.vector.tensor_tensor(u, b, sin, ALU.mult))
            link(nc.vector.tensor_tensor(dst[:, :, 0:half], dst[:, :, 0:half], u, ALU.subtract))
            link(nc.vector.tensor_tensor(dst[:, :, half:], b, cos, ALU.mult))
            link(nc.vector.tensor_tensor(u, a, sin, ALU.mult))
            return nc.vector.tensor_tensor(dst[:, :, half:], dst[:, :, half:], u, ALU.add)

        def mla_dve(dve, units, link):
            units.n += MLA_BEFORE
            for t in range(NT):
                dve.wait_ge(E("ml_rstd"), t + 1)
                nc.vector.tensor_scalar(ckv[:, t, 0:KV_RANK], bank(4 + t)[:, 0:KV_RANK], hrstd[:, t, 0:1], None,
                                        ALU.mult).then_inc(E("ml_lat"), 1)
                link(turn_rows(link, view(kr2[:, t, 0:M_ROPE], 1, M_ROPE), view(bank(4 + t)[:, KV_RANK:KV_RANK + M_ROPE], 1, M_ROPE),
                               t, 1))
                nc.vector.tensor_copy(kr2[:, t, M_ROPE:], kr2[:, t, 0:M_ROPE]).then_inc(E("ml_kr"), 1)
            for t in range(NT):
                dve.wait_ge(E("ml_rstd"), NT + t + 1)
                nc.vector.tensor_scalar(cq[:, t, :], bank(6 + t)[:, 0:Q_RANK], hrstd[:, t, 1:2], None,
                                        ALU.mult).then_inc(E("ml_lat"), 1)
            for t in range(NT):
                for n in range(2):
                    dve.wait_ge(E("ml_v_ps"), 2 * t + n + 1)
                    nc.vector.tensor_copy(m_v[:, t, n * BANK:(n + 1) * BANK], bank(4 + 2 * t + n)).then_inc(E("ml_v"), 1)
            for t in range(NT):
                dve.wait_ge(E("ml_qr_ps"), t + 1)
                turn_rows(link, view(qr[:, t, :], M_HEADS, M_ROPE), bank(4 + t, M_HEADS, M_ROPE), t,
                          M_HEADS).then_inc(E("ml_qr"), 1)
                dve.wait_ge(E("ml_qr"), t + 1)
            dve.wait_ge(E("ml_qrT_ps"), 1)
            for b in range(2):
                nc.vector.tensor_copy(qrT[:, 2 * b:2 * b + 2, :], bank(2 + b, 2, S)).then_inc(E("ml_qrT"), 1)

            def weights(i):
                h = i - 2
                if h >= 0:
                    dve.wait_ge(E("q_round"), Q_MLA + h + 1)
                    nc.vector.tensor_tensor(m_w[h % 2][1][:, :], raw_head(units, h), m_w[h % 2][0][:, :].bitcast(F32),
                                            ALU.subtract).then_inc(E("q_split"), 1)
                    if h % 4 == 3:
                        dve.wait_ge(E("q_split"), Q_MLA + h + 1)
                        dve.sem_inc(used, 1)

            def output(i):
                h = i - 2
                if h >= 0:
                    dve.wait_ge(E("at_o"), 4 + h + 1)
                    nc.vector.tensor_tensor(m_aT[1][:, h % 2, :], bank(3)[:, 0:S], m_aT[0][:, h % 2, :].bitcast(F32),
                                            ALU.subtract).then_inc(E("ml_lo"), 1)

            heads_dve(dve, link, "ml", C("mla_mask"), M_SCALE, output, weights)
            weights(M_HEADS + 1)
            output(M_HEADS + 1)
            residual_dve(dve, "mla", first_bank=4)

        def route_pe(pe, l):
            norm_done(pe, 5 + 2 * l)
            w = view(G(f"route{l}"), DC, N_ROUTE)
            rows_of(bank(6)[0:N_ROUTE, 0:S], lambda c: w[:, c, :], lambda c: xnT[:, c, :], DC).then_inc(E("ro_ps"), 1)
            pe.wait_ge(E("ro_lT"), l + 1)
            for t in range(NT):
                last = nc.tensor.transpose(bank(4)[:, t * N_ROUTE:(t + 1) * N_ROUTE], lgT[0:N_ROUTE, t * P:(t + 1) * P],
                                           ident[0:N_ROUTE, 0:N_ROUTE])
            last.then_inc(E("ro_ps"), 1)
            pe.wait_ge(E("ro_oh"), l + 1)
            r = bank(5)
            nc.tensor.matmul(r[:, 0:N_EXP], C("before"), ohs[:, 0, :], start=True, stop=True)
            nc.tensor.matmul(r[:, N_EXP:2 * N_EXP], C("ones"), ohs[:, 0, :], start=True, stop=False)
            nc.tensor.matmul(r[:, N_EXP:2 * N_EXP], C("before"), ohs[:, 1, :], start=False, stop=True)
            nc.tensor.matmul(r[:, 2 * N_EXP:3 * N_EXP], C("ones"), ohs[:, 0, :], start=True, stop=False)
            nc.tensor.matmul(r[:, 2 * N_EXP:3 * N_EXP], C("ones"), ohs[:, 1, :], start=False,
                             stop=True).then_inc(E("ro_ps"), 1)

        def route_act(act, link, l):
            act.wait_ge(E("ro_ps"), 3 * l + 1)
            nc.scalar.activation(lgT[0:N_ROUTE, :], bank(6)[0:N_ROUTE, 0:S], ACT.Copy).then_inc(E("ro_lT"), 1)
            act.wait_ge(E("ro_shift"), 2 * l + 1)
            nc.scalar.activation(gcand, gsh, ACT.Exp).then_inc(E("ro_exp"), 1)
            act.wait_ge(E("ro_shift"), 2 * l + 2)
            nc.scalar.activation(r2, m2, ACT.Exp).then_inc(E("ro_exp"), 1)

        def route_dve(dve, link, l):
            v = nc.vector

            def first(dst, values, top, order, n, cand):
                link(v.tensor_tensor(dst, values, spread(top, NT, n), ALU.is_equal))
                link(v.tensor_tensor(cand, dst, order.unsqueeze(1).to_broadcast([P, NT, n]), ALU.mult))
                link(v.tensor_reduce(cmax, cand, AX_X, ALU.max))
                link(v.tensor_tensor(dst, cand, spread(cmax, NT, n), ALU.is_equal))

            dve.wait_ge(E("ro_ps"), 3 * l + 2)
            link(v.tensor_tensor(lg, bank(4, NT, N_ROUTE), G(f"route_b{l}").unsqueeze(1).to_broadcast([P, NT, N_ROUTE]), ALU.add))
            lg_g, lg_e = lg[:, :, 0:N_GROUPS], lg[:, :, N_GROUPS:]
            link(v.tensor_reduce(gmax, lg_g, AX_X, ALU.max))
            v.tensor_tensor(gsh, lg_g, spread(gmax, NT, N_GROUPS), ALU.subtract).then_inc(E("ro_shift"), 1)
            dve.wait_ge(E("ro_exp"), 2 * l + 1)
            link(v.tensor_reduce(gprob, gcand, AX_X, ALU.add))
            link(v.reciprocal(gprob, gprob))
            first(goh, lg_g, gmax, C("first4"), N_GROUPS, gcand)
            link(v.tensor_scalar(pen, goh, -NEG, NEG, ALU.mult, ALU.add))
            for t in range(NT):
                link(v.tensor_tensor(view(em[:, t, :], N_GROUPS, GROUP), view(lg_e[:, t, :], N_GROUPS, GROUP),
                                     spread(pen[:, t, :], N_GROUPS, GROUP), ALU.add))
            link(v.tensor_reduce(m1, em, AX_X, ALU.max))
            first(oh1, em, m1, C("first32"), N_EXP, er)
            link(v.scalar_tensor_tensor(em, oh1, FAR, em, ALU.mult, ALU.add))
            link(v.tensor_reduce(m2, em, AX_X, ALU.max))
            first(oh2, em, m2, C("first32"), N_EXP, er)
            v.tensor_tensor(ohs, oh1, oh2, ALU.add).then_inc(E("ro_oh"), 1)
            v.tensor_tensor(m2, m2, m1, ALU.subtract).then_inc(E("ro_shift"), 1)
            dve.wait_ge(E("ro_exp"), 2 * l + 2)
            link(v.tensor_scalar(rd2, r2, 1.0, None, ALU.add))
            link(v.reciprocal(rd2, rd2))
            link(v.tensor_tensor(gate[:, :, 0], gprob, rd2, ALU.mult))
            link(v.tensor_tensor(gate[:, :, 1], gate[:, :, 0], r2, ALU.mult))
            link(v.tensor_tensor(erk, ohk, C("row_of").unsqueeze(1).to_broadcast([P, 2 * NT, N_EXP]), ALU.mult))
            link(v.tensor_reduce(row, erk, AX_X, ALU.add))
            dve.wait_ge(E("ro_ps"), 3 * l + 3)
            ranks = bank(5)[:, 0:NT * N_EXP].rearrange("p (t e) -> p t e", t=NT)
            for k, oh in enumerate((oh1, oh2)):
                last = v.tensor_tensor(erk[:, NT * k:NT * (k + 1), :], oh, ranks, ALU.mult)
            link(last)
            link(v.tensor_reduce(rank, erk, AX_X, ALU.add))
            v.tensor_reduce(count_max, bank(5)[:, 2 * N_EXP:3 * N_EXP], AX_X, ALU.max)
            link(v.tensor_scalar(over, rank, float(CAP), None, ALU.is_ge))
            for r in range(2, ROUNDS):
                link(v.scalar_tensor_tensor(over, rank, float(r * CAP), over, ALU.is_ge, ALU.add))
            link(v.scalar_tensor_tensor(row, over, float(CAP * (N_EXP - 1)), row, ALU.mult, ALU.add))
            link(v.tensor_tensor(pos.rearrange("p t k -> p k t"), view(row, 2, NT), view(rank, 2, NT), ALU.add))
            v.tensor_copy(flag[:, l:l + 1], count_max).then_inc(E("ro_flag"), 1)

        PER_STEP = {"xg_ps": 2, "xg": 2, "wT_ps": 1, "wT": 1, "sel": 2, "gu_ps": 2, "sg": 1, "h": 1, "hT_ps": 1, "hT": 1,
                    "y_ps": 2, "y": 2, "c_ps": 4, "add": 4}
        AHEAD = ("xg_ps", "xg", "wT_ps", "wT", "sel")
        PRIMED = ("xg", "h", "c_ps", "add", "y_ps")

        class Pairs:

            def __init__(self, name, ahead, runs=0):
                self.name, self.ahead, self.runs = name, ahead, runs

            def __getitem__(self, what):
                return E(self.name + "_" + what)

            def wait(self, eng, what, value):
                before = self.runs * (PER_STEP[what] * (N_PAIRS + (what in AHEAD)) + (what in PRIMED))
                eng.wait_ge(self[what], before + (what in PRIMED) + value)

        def select(dve, link, q, b):
            v, col, tiles = nc.vector, C("column"), range(NT)
            for t in tiles:
                last = v.tensor_scalar(wtmp[:, t, :], col, pos[:, t, 0:1], None, ALU.is_equal)
            link(last)
            for t in tiles:
                last = v.scalar_tensor_tensor(sel[:, b, t, :], col, pos[:, t, 1:2], wtmp[:, t, :], ALU.is_equal, ALU.add)
            last.then_inc(q["sel"], 1)
            for t in tiles:
                v.tensor_scalar(wsel[:, b, t, :], col, pos[:, t, 1:2], gate[:, t, 1:2], ALU.is_equal, ALU.mult)
                last = v.tensor_scalar(wtmp2[:, t, :], col, pos[:, t, 0:1], gate[:, t, 0:1], ALU.is_equal, ALU.mult)
            link(last)
            link(v.tensor_scalar(pos, pos, float(P), None, ALU.subtract))
            for t in tiles:
                last = v.tensor_tensor(wsel[:, b, t, :], wsel[:, b, t, :], wtmp2[:, t, :], ALU.add)
            last.then_inc(q["sel"], 1)

        LINKS = 3

        def gather_dve(dve, q, b, l, n, half):
            q.wait(dve, "xg_ps", 2 * n + half + 1)
            g = G(f"g_moe{l}")[:, 4 * half:4 * half + 4]
            nc.vector.tensor_tensor(view(xg[:, b, half * 4 * P:(half + 1) * 4 * P], 4, P), bank(4 + half, 4, P),
                                    spread(g, 4, P), ALU.mult).then_inc(q["xg"], 1)

        def gather_pe(b, q, half):
            for c in range(4 * half, 4 * half + 4):
                for t in range(NT):
                    last = nc.tensor.matmul(bank(4 + half)[:, (c % 4) * P:(c % 4 + 1) * P], hs[:, t, c:D:DC],
                                            sel[:, b, t, :], start=(t == 0), stop=(t == NT - 1))
            last.then_inc(q["xg_ps"], 1)

        def weights_pe(b, q):
            for t in range(NT):
                last = nc.tensor.transpose(bank(7)[:, t * P:(t + 1) * P], wsel[:, b, t, :], ident)
            last.then_inc(q["wT_ps"], 1)

        def chunk_of(w, c):
            for piece in w if isinstance(w, tuple) else (w,):
                n = piece.shape[-1] // BANK
                if c < n:
                    return piece[:, c * BANK:(c + 1) * BANK]
                c -= n

        def pair_pe(pe, q, s, b, six):
            q.wait(pe, "add", 4 * s)
            for what in range(2):
                w = [six(2 * what + e) for e in range(2)]
                for c in range(DC):
                    if what == 0 and c % (DC // 2) == 0:
                        q.wait(pe, "xg", 2 * s + 2 * q.ahead - (c == 0))
                    for e in range(2):
                        last = nc.tensor.matmul(PS[CAP * e:CAP * (e + 1), what, :],
                                                xg[:, b, c * P + CAP * e:c * P + CAP * (e + 1)], chunk_of(w[e], c),
                                                start=(c == 0), stop=(c == DC - 1))
                last.then_inc(q["gu_ps"], 1)
            q.wait(pe, "sel", 2 * s + 1 + 2 * q.ahead)
            gather_pe(1 - b, q, 0)
            q.wait(pe, "h", s + 1)
            for c in range(4):
                last = nc.tensor.transpose(bank(6)[:, c * P:(c + 1) * P], e_h[:, c:D_EXP:4], ident)
            last.then_inc(q["hT_ps"], 1)
            q.wait(pe, "sel", 2 * s + 2 + 2 * q.ahead)
            weights_pe(1 - b, q)
            gather_pe(1 - b, q, 1)
            w = [view(six(4 + e), 4, D) for e in range(2)]
            q.wait(pe, "hT", s + 1)
            for n in range(2):
                for c in range(4):
                    for e in range(2):
                        last = nc.tensor.matmul(PS[CAP * e:CAP * (e + 1), 2 + n, :], e_hT[:, c, CAP * e:CAP * (e + 1)],
                                                w[e][:, c, n * BANK:(n + 1) * BANK], start=(c == 0), stop=(c == 3))
                last.then_inc(q["y_ps"], 1)
            q.wait(pe, "wT", s + 1 + q.ahead)
            q.wait(pe, "xg", 2 * s + 2 * q.ahead + 1)
            for n in range(2):
                q.wait(pe, "y", 2 * s + n + 1)
                for t in range(NT):
                    nc.tensor.matmul(bank(COMBINE[n][t]), wT[:, b, t * P:(t + 1) * P], e_y[:, n * BANK:(n + 1) * BANK],
                                     start=True, stop=True).then_inc(q["c_ps"], 1)

        COMBINE = ((2, 7), (3, 4))

        def apart(q, s):
            return q.ahead and isinstance(s, int) and s == 1

        def pair_act(act, q, s, b):
            q.wait(act, "gu_ps", 2 * s + 1)
            if q.ahead and not apart(q, s):
                act.sem_inc(used, 2)
            q.wait(act, "h", s)
            nc.scalar.activation(sg, bank(0), ACT.Silu).then_inc(q["sg"], 1)
            q.wait(act, "wT_ps", s + q.ahead + 1)
            q.wait(act, "c_ps", 4 * s)
            nc.scalar.activation(wT[:, 1 - b, :], bank(7)[:, 0:S], ACT.Copy).then_inc(q["wT"], 1)
            for n in range(2):
                q.wait(act, "y_ps", 2 * s + n + 1)
                if q.ahead and n == 1:
                    act.sem_inc(used, 2)
                nc.scalar.activation(e_y[:, n * BANK:(n + 1) * BANK], bank(2 + n), ACT.Copy).then_inc(q["y"], 1)

        def pair_dve(dve, link, q, s, b, l):
            select(dve, link, q, 1 - b)
            q.wait(dve, "gu_ps", 2 * s + 2)
            q.wait(dve, "sg", s + 1)
            if q.ahead:
                dve.sem_inc(used, 1 if apart(q, s) else 2)
            nc.vector.tensor_tensor(e_h, sg, bank(1), ALU.mult).then_inc(q["h"], 1)
            gather_dve(dve, q, 1 - b, l, s + q.ahead, 0)
            q.wait(dve, "hT_ps", s + 1)
            nc.vector.tensor_copy(e_hT, bank(6, 4, P)).then_inc(q["hT"], 1)
            gather_dve(dve, q, 1 - b, l, s + q.ahead, 1)
            for n in range(2):
                for t in range(NT):
                    q.wait(dve, "c_ps", 4 * s + 2 * n + t + 1)
                    v = x[:, t, n * BANK:(n + 1) * BANK]
                    nc.vector.tensor_tensor(v, v, bank(COMBINE[n][t]), ALU.add).then_inc(q["add"], 1)

        def expert_source(l, e, k):
            src = (e_gate, e_up, e_down)[k // 2]
            rows = src[l].rearrange("e (p c) n -> e p (c n)", p=P)
            return rows[bass.ds(e + k % 2, 1)].rearrange("e p n -> p (e n)")

        TURNS = N_PAIRS // 2 - 1

        def moe_load(sp, units, l):
            for k in range(6):
                units.load(units.slot(), expert_source(l, 0, k))
            if l == 0:
                sp.wait_ge(E("n_tr"), 4 * 4 + 4)
            else:
                sp.wait_ge(E("at_o_ps"), 16)
            for k, i in ((0, 0), (1, 0), (2, 0), (2, 1), (1, 1)):
                if (k, i) == (2, 0):
                    sp.wait_ge(E("mla_ps" if l else "pool_add"), 2 * NT if l else NT)
                if (k, i) == (1, 1):
                    sp.wait_ge(E("ro_ps"), 3 * l + 1)
                at = sum(piece.shape[-1] for piece in extra[k][:i])
                sp.dma_start(extra[k][i], expert_source(l, 2, k)[:, at:at + extra[k][i].shape[-1]]).then_inc(E(f"extra_in{k}"), 16)
            for k in range(3, 6):
                units.load(units.slot(), expert_source(l, 2, k))
            with sp.Fori(0, TURNS) as turn:
                units.loop(turn, 2 * SLOTS)
                for j in range(2):
                    for k in range(6):
                        units.load(units.slot(), expert_source(l, turn * 4 + 4 + 2 * j, k))
                units.done(TURNS)
            more = Pairs(f"more{l}", 0)
            sp.wait_ge(E("ro_flag"), l + 1)
            count = sp.value_load(flag[0:1, l:l + 1])
            with sp.If(count > CAP):
                sp.wait_ge(used, units.n)
                with sp.Fori(0, ROUNDS - 1) as r:
                    with sp.Fori(0, N_PAIRS) as e:
                        sp.wait_ge(more["y_ps"], (r * N_PAIRS + e) * 2 + 1)
                        for k in range(6):
                            sp.dma_start(ring[:, k, :], expert_source(l, e * 2, k)).then_inc(more["loaded"], 16)
                sp.wait_ge(more["loaded"], 96 * (ROUNDS - 1) * N_PAIRS)
                sp.wait_ge(more["y_ps"], (ROUNDS - 1) * N_PAIRS * 2 + 1)

        def moe_pe(pe, units, l):
            q = Pairs("moe", 1, l)
            for what in ("c_ps", "y_ps"):
                pe.sem_inc(q[what], 1)
            route_pe(pe, l)
            q.wait(pe, "sel", 1)
            gather_pe(0, q, 0)
            q.wait(pe, "sel", 2)
            weights_pe(0, q)
            gather_pe(0, q, 1)
            q.wait(pe, "wT", 1)

            def six(k):
                units.wait()
                got = units.slot()
                units.n += 1
                return got

            def second_six(k):
                if k >= len(extra):
                    return six(k)
                pe.wait_ge(E(f"extra_in{k}"), 16 * len(extra[k]) * (l + 1))
                return extra[k]

            pair_pe(pe, q, 0, 0, six)
            pair_pe(pe, q, 1, 1, second_six)
            with pe.Fori(0, TURNS) as turn:
                units.loop(turn, 2 * SLOTS)
                for j in range(2):
                    pair_pe(pe, q, turn * 2 + (2 + j), j, six)
                units.done(TURNS)
            more = Pairs(f"more{l}", 0)
            pe.wait_ge(E("ro_flag"), l + 1)
            count = pe.value_load(flag[0:1, l:l + 1])
            with pe.If(count > CAP):
                q.wait(pe, "xg", 2 * N_PAIRS + 2)
                q.wait(pe, "wT", N_PAIRS + 1)
                q.wait(pe, "add", 4 * N_PAIRS)
                for what in ("c_ps", "y_ps"):
                    pe.sem_inc(more[what], 1)
                with pe.Fori(0, (ROUNDS - 1) * N_PAIRS // 2) as turn:
                    for j in range(2):
                        s = turn * 2 + j
                        pe.wait_ge(more["loaded"], 96 * s + 96)
                        pair_pe(pe, more, s, j, lambda k: ring[:, k, :])

        def moe_act(act, link, l):
            q = Pairs("moe", 1, l)
            route_act(act, link, l)
            q.wait(act, "wT_ps", 1)
            nc.scalar.activation(wT[:, 0, :], bank(7)[:, 0:S], ACT.Copy).then_inc(q["wT"], 1)
            for s in range(2):
                pair_act(act, q, s, s)
            with act.Fori(0, TURNS) as turn:
                for j in range(2):
                    pair_act(act, q, turn * 2 + (2 + j), j)
            more = Pairs(f"more{l}", 0)
            act.wait_ge(E("ro_flag"), l + 1)
            count = act.value_load(flag[0:1, l:l + 1])
            with act.If(count > CAP):
                q.wait(act, "c_ps", 4 * N_PAIRS)
                q.wait(act, "h", N_PAIRS)
                with act.Fori(0, (ROUNDS - 1) * N_PAIRS // 2) as turn:
                    for j in range(2):
                        pair_act(act, more, turn * 2 + j, j)
                more.wait(act, "add", 4 * (ROUNDS - 1) * N_PAIRS)

        def moe_dve(dve, link, l):
            q = Pairs("moe", 1, l)
            for what in ("xg", "h", "add"):
                dve.sem_inc(q[what], 1)
            route_dve(dve, link, l)
            select(dve, link, q, 0)
            gather_dve(dve, q, 0, l, 0, 0)
            gather_dve(dve, q, 0, l, 0, 1)
            for s in range(2):
                pair_dve(dve, link, q, s, s, l)
            with dve.Fori(0, TURNS) as turn:
                link.loop(turn, 2 * LINKS)
                for j in range(2):
                    pair_dve(dve, link, q, turn * 2 + (2 + j), j, l)
                link.done(TURNS)
            more = Pairs(f"more{l}", 0)
            dve.wait_ge(E("ro_flag"), l + 1)
            count = dve.value_load(flag[0:1, l:l + 1])
            with dve.If(count > CAP):
                link2 = Chain(dve, more["links"])
                for what in ("xg", "h", "add"):
                    dve.sem_inc(more[what], 1)
                with dve.Fori(0, (ROUNDS - 1) * N_PAIRS // 2) as turn:
                    link2.loop(turn, 2 * LINKS)
                    for j in range(2):
                        pair_dve(dve, link2, more, turn * 2 + j, j, l)
                    link2.done((ROUNDS - 1) * N_PAIRS // 2)

        N_FIRST = const_at["minus_half"][1]
        EVEN_UNITS = 8

        block = ctx.enter_context(nc.Block())

        @block.sync
        def _(sp):
            units = Units(sp)
            sp.dma_start(x[:, 0, :], x_in[0, 0:P, :]).then_inc(E("x_in"), 16)
            sp.dma_start(x[:, 1, :], x_in[0, P:S, :]).then_inc(E("x_in"), 16)
            even_load(units)
            ffn_load(sp, units, 0)
            ret_load(units)
            ffn_load(sp, units, 1)
            pool_load(units)
            sp.wait_ge(E("ffn_d"), 1 + 2 * (N_SLABS - 1))
            sp.dma_start(pl_band.rearrange("p a b -> p (a b)"), band_in).then_inc(E("band_in"), 16)
            sp.wait_ge(E("ffn_ps"), 4 * NT)
            sp.dma_start(late[:, 0:2 * D], rows[:, 0:2 * D]).then_inc(E("rows_in"), 16)
            moe_load(sp, units, 0)
            mla_load(units)
            moe_load(sp, units, 1)
            sp.dma_start(R("final"), rows[:, 2 * D:3 * D]).then_inc(E("final_in"), 16)
            for t in range(NT):
                sp.wait_ge(E("out_rdy"), t + 1)
                sp.dma_start(out[0, t * P:(t + 1) * P, :], hs[:, t, :]).then_inc(E("out_sent"), 16)
            sp.wait_ge(E("out_sent"), 16 * NT)

        @block.tensor
        def _(pe):
            units = Units(pe)
            pe.wait_ge(E("first_in"), 16)
            norm_pe(pe, 0)
            even_pe(pe, units)
            norm_pe(pe, 1)
            ffn_pe(pe, units, 0)
            norm_pe(pe, 2)
            ret_pe(pe, units)
            norm_pe(pe, 3)
            ffn_pe(pe, units, 1)
            norm_pe(pe, 4)
            pool_pe(pe, units)
            norm_pe(pe, 5)
            moe_pe(pe, units, 0)
            norm_pe(pe, 6)
            mla_pe(pe, units)
            norm_pe(pe, 7)
            moe_pe(pe, units, 1)

        @block.scalar
        def _(act):
            act.dma_start(cst[:, 0:N_FIRST], const[:, 0:N_FIRST]).then_inc(E("first_in"), 16)
            act.dma_start(par[:, :], params).then_inc(E("param_in"), 16)
            act.dma_start(cst[:, N_FIRST:], const[:, N_FIRST:]).then_inc(E("const_in"), 16)
            link = Chain(act, E("act_link"))
            units = Units(act)
            act.wait_ge(E("param_in"), 16)
            even_act(act, units, link)
            ffn_first_act(act, units, 0, GATE)
            norm_act(act, link, 1)
            ffn_first_act(act, units, 0, VALUE)
            ffn_act(act, units, 0)
            ret_first_act(act, units)
            norm_act(act, link, 2)
            act.wait_ge(E("ffn_ps"), 2 * NT)
            act.dma_start(late[:, 0:RET_HEADS * SC], decay_in).then_inc(E("decay_in"), 16)
            ret_act(act, units)
            ffn_first_act(act, units, 1, GATE)
            norm_act(act, link, 3)
            ffn_first_act(act, units, 1, VALUE)
            ffn_act(act, units, 1)
            norm_act(act, link, 4)
            norm_act(act, link, 5)
            moe_act(act, link, 0)
            norm_act(act, link, 6)
            mla_act(act, units, link)
            norm_act(act, link, 7)
            moe_act(act, link, 1)
            norm_act(act, link, 8)

        @block.gpsimd
        def _(pool):
            pool.wait_ge(E("first_in"), 16)
            norm_pool(pool, 0)
            even_pool(pool)
            norm_pool(pool, 1)
            norm_pool(pool, 2)
            ret_pool(pool)
            for k in range(3, 7):
                norm_pool(pool, k)
            mla_pool(pool)
            norm_pool(pool, 7)
            norm_pool(pool, 8)

        @block.vector
        def _(dve):
            link = Chain(dve, E("dve_link"))
            units = Units(dve)
            dve.wait_ge(E("param_in"), 16)
            even_dve(dve, units, link)
            norm_dve(dve, link, 1)
            ffn_first_dve(dve, units, 0, VALUE)
            ffn_dve(dve, units, link, 0)
            norm_dve(dve, link, 2)
            ret_dve(dve, units, link)
            norm_dve(dve, link, 3)
            ffn_first_dve(dve, units, 1, VALUE)
            ffn_dve(dve, units, link, 1)
            norm_dve(dve, link, 4)
            pool_dve(dve, link)
            norm_dve(dve, link, 5)
            moe_dve(dve, link, 0)
            norm_dve(dve, link, 6)
            mla_dve(dve, units, link)
            norm_dve(dve, link, 7)
            moe_dve(dve, link, 1)
            dve.wait_ge(E("n_rstd"), 9 * NT)
            dve.wait_ge(E("final_in"), 16)
            for t in range(NT):
                nc.vector.scalar_tensor_tensor(hs[:, t, :], x[:, t, :], rstd[:, t:t + 1], R("final"), ALU.mult,
                                               ALU.mult).then_inc(E("out_rdy"), 1)


def kernel(**inputs):
    import concourse.bacc as bacc
    from concourse.bass_utils import run_bass_kernel_spmd

    a = {k: np.ascontiguousarray(v) for k, v in inputs.items()}
    table, _, decay, band = shape_constants()

    def striped(v):
        return v.reshape(P, -1)

    def stacked(v):
        return v.reshape(-1, P).T

    def router(l):
        w = np.concatenate([a["router_group_w_2"][l], a["router_expert_w_2"][l]], axis=1)
        return w.reshape(P, DC * N_ROUTE)

    def router_bias(l):
        b = np.concatenate([a["router_group_b_2"][l], a["router_expert_b_2"][l]])
        return np.broadcast_to(b[None, :], (P, N_ROUTE))

    def ffn_taps(l):
        w = a["ffn_conv_w"][l].reshape(3, 2, N_SLABS, 2, P)
        return w.transpose(4, 2, 1, 3, 0).reshape(P, -1)

    by_name = {
        "g_even": striped(a["even_norm"][0]), "g_ffn0": striped(a["ffn_norm"][0]), "g_odd": striped(a["odd_norm"][0]),
        "g_ffn1": striped(a["ffn_norm"][1]), "g_pool": stacked(a["pool_norm_2"][0]), "g_moe0": striped(a["ffn_norm_2"][0]),
        "g_kvin": striped(a["kv_in_norm_2"]), "g_attn": striped(a["attn_norm_2"][0]), "g_moe1": striped(a["ffn_norm_2"][1]),
        "q_gain": np.concatenate([a["even_q_gain"][0]] * 2)[:, None],
        "k_gain": np.concatenate([a["even_k_gain"][0]] * 2)[:, None],
        "sconv": a["even_sconv_w"][0].reshape(3, 4, P).transpose(2, 1, 0).reshape(P, -1),
        "gn": stacked(a["ret_gn_gain"][0].reshape(-1)), "conv0": ffn_taps(0), "conv1": ffn_taps(1),
        "kv_norm": stacked(a["kv_norm_2"]), "q_norm": stacked(a["q_norm_2"][0]),
        "route0": router(0), "route1": router(1), "route_b0": router_bias(0), "route_b1": router_bias(1),
    }
    params = np.ascontiguousarray(np.concatenate([by_name[n] for n, _ in PARAMS], axis=1))
    row_values = {"pool_b": a["pool_b_2"][0].reshape(-1), "pool_scale": a["pool_scale_2"][0], "final": a["final_norm_2"]}
    rows = np.ascontiguousarray(np.broadcast_to(np.concatenate([row_values[n] for n, _ in ROWS])[None, :], (P, 3 * D)))
    arrays = {"const": np.ascontiguousarray(table), "decay": decay, "band": band, "params": params, "rows": rows}
    for name in ("x", "even_w_in", "even_w_out", "ret_wq", "ret_wk", "ret_wv", "ret_wg", "ret_wo", "ffn_w_up", "ffn_w_down",
                 "pool_w_2", "w_dkv_2", "w_uk_2", "w_uv_2", "wq_down_2", "wq_up_2", "wo_2", "w_gate_2", "w_up_2", "w_down_2"):
        arrays[name] = a[name]
    nc = bacc.Bacc("TRN2", target_bir_lowering=False, num_devices=1)
    args = [nc.dram_tensor(k, v.shape, F32, kind="ExternalInput").ap() for k, v in arrays.items()]
    args.append(nc.dram_tensor("out", (1, S, D), F32, kind="ExternalOutput").ap())
    build(nc, *args)
    r = run_bass_kernel_spmd(nc, [arrays], core_ids=[0])
    return r.results[0]["out"]
```
